# Optimizing a Trainium2 kernel written in Bass

```python
import math
import jax, jax.numpy as jnp
from jax import lax
import numpy as np

D_MODEL = 1024
BATCH = 1
SEQ = 1024
DEPTH = 1

PLE_DIM = 256
SSM_WIDTH = D_MODEL // 2
SSM_GROUP = 16
SSM_GROUPS = SSM_WIDTH // SSM_GROUP
SSM_STATE = 64
CONV_WIDTH = D_MODEL
CONV_K = 3
DT_MIN = 1e-3
DT_MAX = 1e-1
RMS_EPS = 1e-6
IN_SPLITS = (SSM_WIDTH, SSM_WIDTH, CONV_WIDTH, CONV_WIDTH, CONV_WIDTH, CONV_WIDTH, D_MODEL, D_MODEL)
IN_WIDTH = sum(IN_SPLITS)

kernel_name = "hybrid_s5_shortconv_gated_block"

def rms_norm(x, gain):
    xf = x.astype(jnp.float32)
    y = xf * lax.rsqrt(jnp.mean(xf * xf, axis=-1, keepdims=True) + RMS_EPS)
    return (y * gain.astype(jnp.float32)).astype(x.dtype)

def _complex_affine_combine(e1, e2):
    a1r, a1i, b1r, b1i = e1
    a2r, a2i, b2r, b2i = e2
    ar = a1r * a2r - a1i * a2i
    ai = a1r * a2i + a1i * a2r
    br = a2r * b1r - a2i * b1i + b2r
    bi = a2r * b1i + a2i * b1r + b2i
    return (ar, ai, br, bi)

def s5_ssm(u, a_re, a_im, log_step, b_re, b_im, c_re, c_im, d_skip):
    f32 = jnp.float32
    bsz, seqlen, _ = u.shape
    uf = u.astype(f32).reshape(bsz, seqlen, SSM_GROUPS, SSM_GROUP)
    a_re = a_re.astype(f32); a_im = a_im.astype(f32)
    dt = jnp.exp(log_step.astype(f32))[:, None]
    mag = jnp.exp(a_re * dt)
    abar_r = mag * jnp.cos(a_im * dt)
    abar_i = mag * jnp.sin(a_im * dt)
    den = a_re * a_re + a_im * a_im
    nr = abar_r - 1.0
    fr = (nr * a_re + abar_i * a_im) / den
    fi = (abar_i * a_re - nr * a_im) / den
    b_re = b_re.astype(f32); b_im = b_im.astype(f32)
    bbar_r = fr[..., None] * b_re - fi[..., None] * b_im
    bbar_i = fr[..., None] * b_im + fi[..., None] * b_re
    bu_r = jnp.einsum('gph,blgh->blgp', bbar_r, uf)
    bu_i = jnp.einsum('gph,blgh->blgp', bbar_i, uf)
    ar = jnp.broadcast_to(abar_r, bu_r.shape)
    ai = jnp.broadcast_to(abar_i, bu_i.shape)
    _, _, s_r, s_i = lax.associative_scan(_complex_affine_combine, (ar, ai, bu_r, bu_i), axis=1)
    c_re = c_re.astype(f32); c_im = c_im.astype(f32)
    y = (jnp.einsum('ghp,blgp->blgh', c_re, s_r)
         - jnp.einsum('ghp,blgp->blgh', c_im, s_i)
         + d_skip.astype(f32).reshape(SSM_GROUPS, SSM_GROUP) * uf)
    return y.reshape(bsz, seqlen, SSM_WIDTH).astype(u.dtype)

def causal_dwconv(v, w):
    c = v.shape[-1]
    return lax.conv_general_dilated(
        v, w.astype(v.dtype)[:, None, :], window_strides=(1,), padding=[(CONV_K - 1, 0)],
        dimension_numbers=('NWC', 'WIO', 'NWC'), feature_group_count=c)

def setup_inputs(seed: int = 0) -> dict:
    key = jax.random.key(seed)
    ks = jax.random.split(key, 32)
    f32 = jnp.float32
    nrm = lambda k, s, sc: jax.random.normal(k, s, f32) * sc
    gain = lambda k, s: 1.0 + 0.02 * jax.random.normal(k, s, f32)
    G, P, H = SSM_GROUPS, SSM_STATE, SSM_GROUP
    n_idx = jnp.arange(P, dtype=f32)[None, :]
    return {
        "x": nrm(ks[0], (BATCH, SEQ, D_MODEL), 1.0),
        "p": nrm(ks[1], (DEPTH, BATCH, SEQ, PLE_DIM), 1.0),
        "pre_norm": gain(ks[2], (DEPTH, D_MODEL)),
        "w_in": nrm(ks[3], (DEPTH, D_MODEL, IN_WIDTH), D_MODEL ** -0.5),
        "a_re": -0.5 + 0.01 * jax.random.normal(ks[4], (DEPTH, G, P), f32),
        "a_im": math.pi * n_idx + 0.01 * jax.random.normal(ks[5], (DEPTH, G, P), f32),
        "log_step": jax.random.uniform(ks[6], (DEPTH, G), f32, math.log(DT_MIN), math.log(DT_MAX)),
        "b_re": nrm(ks[7], (DEPTH, G, P, H), (2.0 * H) ** -0.5),
        "b_im": nrm(ks[8], (DEPTH, G, P, H), (2.0 * H) ** -0.5),
        "c_re": nrm(ks[9], (DEPTH, G, H, P), (2.0 * P) ** -0.5),
        "c_im": nrm(ks[10], (DEPTH, G, H, P), (2.0 * P) ** -0.5),
        "d_skip": nrm(ks[11], (DEPTH, SSM_WIDTH), 1.0),
        "w_glu": nrm(ks[12], (DEPTH, SSM_WIDTH, SSM_WIDTH), SSM_WIDTH ** -0.5),
        "b_glu": nrm(ks[13], (DEPTH, SSM_WIDTH), 0.01),
        "w_ssm_out": nrm(ks[14], (DEPTH, SSM_WIDTH, D_MODEL), SSM_WIDTH ** -0.5),
        "conv_w": nrm(ks[15], (DEPTH, CONV_K, CONV_WIDTH), CONV_K ** -0.5),
        "w_conv_out": nrm(ks[16], (DEPTH, CONV_WIDTH, D_MODEL), CONV_WIDTH ** -0.5),
        "w_o": nrm(ks[17], (DEPTH, D_MODEL, D_MODEL), D_MODEL ** -0.5),
        "post_norm": gain(ks[18], (DEPTH, D_MODEL)),
        "w_ple": nrm(ks[19], (DEPTH, PLE_DIM, D_MODEL), PLE_DIM ** -0.5),
        "w_ple_gate": nrm(ks[20], (DEPTH, D_MODEL, D_MODEL), D_MODEL ** -0.5),
        "ple_norm": gain(ks[21], (DEPTH, D_MODEL)),
    }

def reference(x, p, pre_norm, w_in, a_re, a_im, log_step, b_re, b_im, c_re, c_im, d_skip,
              w_glu, b_glu, w_ssm_out, conv_w, w_conv_out, w_o, post_norm,
              w_ple, w_ple_gate, ple_norm):
    split_pts = list(np.cumsum(IN_SPLITS)[:-1])
    for i in range(DEPTH):
        h = rms_norm(x, pre_norm[i])
        proj = jnp.einsum('bld,de->ble', h, w_in[i])
        u_ssm, g_ssm, xc, bc, cc, g_conv, r_ssm, r_conv = jnp.split(proj, split_pts, axis=-1)

        y = s5_ssm(u_ssm, a_re[i], a_im[i], log_step[i], b_re[i], b_im[i], c_re[i], c_im[i], d_skip[i])
        y = jax.nn.gelu(y)
        y = y * jax.nn.sigmoid(jnp.einsum('blc,ce->ble', y, w_glu[i]) + b_glu[i])
        y = y * jax.nn.silu(g_ssm)
        y_a = jnp.einsum('blc,cd->bld', y, w_ssm_out[i])

        z = bc * causal_dwconv(cc * xc, conv_w[i])
        z = z * jax.nn.silu(g_conv)
        y_b = jnp.einsum('blc,cd->bld', z, w_conv_out[i])

        merged = jax.nn.sigmoid(r_ssm) * y_a + jax.nn.sigmoid(r_conv) * y_b
        o = jnp.einsum('bld,de->ble', merged, w_o[i])
        x = x + rms_norm(o, post_norm[i])

        e = jnp.einsum('blk,kd->bld', p[i], w_ple[i]) * jax.nn.sigmoid(
            jnp.einsum('bld,de->ble', x, w_ple_gate[i]))
        x = x + rms_norm(e, ple_norm[i])
    return x


_drawn_inputs = setup_inputs


def setup_inputs(seed=0):
    import zlib

    import numpy as np

    out = dict(_drawn_inputs(seed))
    spreads = {}
    factors = {'a_re': 64.0,
     'a_im': 33.136,
     'log_step': 34.336,
     'b_re': 46.728,
     'b_im': 46.592,
     'c_re': 46.4,
     'c_im': 46.128,
     'b_glu': 40.047,
     'post_norm': 15.133,
     'ple_norm': 18.671}
    for name, (base, spread) in spreads.items():
        noise = np.random.default_rng([zlib.crc32(name.encode()), seed]).standard_normal(out[name].shape)
        drawn = base * np.exp(spread * noise) if base else spread * noise
        out[name] = __import__('jax').numpy.asarray(drawn.astype(out[name].dtype))
    for name, factor in factors.items():
        out[name] = (out[name] * factor).astype(out[name].dtype)
    return out
```

```python
def build_block(nc, x, p, pre_norm, w_in, a_re, a_im, log_step, b_re, b_im, c_re, c_im, d_skip,
                w_glu, b_glu, w_ssm_out, conv_w, w_conv_out, w_o, post_norm, w_ple, w_ple_gate,
                ple_norm, out):
    import math
    from contextlib import ExitStack
    import concourse.bass as bass
    from concourse import mybir

    f32, f32r, i32 = mybir.dt.float32, mybir.dt.float32r, mybir.dt.int32
    ALU = mybir.AluOpType
    ACT = mybir.ActivationFunctionType

    P = 128
    L, D = x.shape[1], x.shape[2]
    SSM_W = w_glu.shape[1]
    G, N_STATE, GC = b_re.shape[1], b_re.shape[2], b_re.shape[3]
    PLE = p.shape[3]
    KD, KS, KP, LT = D // P, SSM_W // P, PLE // P, L // P
    HALF = 512
    T = P // GC
    C = L // T
    PAIRS = G // 2
    NP = T + 1
    EPS = 1e-6
    COL_G, COL_XC = SSM_W, 2 * SSM_W
    COL_BC, COL_CC, COL_GC = COL_XC + D, COL_XC + 2 * D, COL_XC + 3 * D
    COL_RS, COL_RC = COL_XC + 4 * D, COL_XC + 5 * D

    Q_CONV0, Q_CONV1, Q_GSSM, Q_GLU, Q_CONV3, Q_YA, Q_CONV4, Q_RC, Q_YB, Q_END = 0, 1, 3, 4, 5, 6, 10, 14, 16, 18

    ctx = ExitStack()
    with ctx:
        KB = 1024
        arena = ctx.enter_context(nc.sbuf_tensor("arena", [P, 207 * 256], f32))
        BASE = 16512

        def at(name, kb, shape, dt=f32):
            return nc.alloc_sbuf_tensor_at(name, shape, dt, offset=BASE + int(kb * KB))

        w_raw = [at(f"w_raw{i}", 4 * i, [P, KD, P]) for i in range(4)]
        w_hi = [at(f"w_hi{i}", 16 + 4 * i, [P, KD, P], f32r) for i in range(2)]
        w_lo = [at(f"w_lo{i}", 24 + 4 * i, [P, KD, P], f32r) for i in range(2)]
        big_hi = at("big_hi", 32, [P, KD, L], f32r)
        big_lo = at("big_lo", 64, [P, KD, L], f32r)
        z = at("z", 96, [P, KD, L])
        yam = at("yam", 128, [P, KD, L])
        rc_gate = at("rc_gate", 160, [P, KD, L])
        mx_hi = at("mx_hi", 96, [P, KD, L], f32r)
        mx_lo = at("mx_lo", 160, [P, KD, L], f32r)
        x_tile = [at(f"x_tile{i}", (174 if i < 4 else 124 - 16) + 4 * i, [P, D]) for i in range(LT)]
        sq_junk = at("sq_junk", 96, [P, D])
        wu_raw = at("wu_raw", 0, [P, KD // 2, SSM_W])
        wu_raw2 = at("wu_raw2", 16, [P, KD // 2, SSM_W])
        wu_hi = at("wu_hi", 158, [P, KD, SSM_W], f32r)
        wu_lo = at("wu_lo", 142, [P, KD, SSM_W], f32r)
        u_nat = at("u_nat", 174, [P, G, T, GC])
        u_chunk = at("u_chunk", 108, [P, G, C])
        ca = at("ca", 124, [P, G, NP, GC])
        pv = at("pv", 142, [P, G, T * GC])
        w_in_state = at("w_in_state", 158, [P, G, P])
        toep = at("toep", 158, [P, G, T * GC])
        kern = at("kern", 174, [GC, G, T * GC])
        w_c = at("w_c", 142, [P, 4, 2, 4, C])
        state = at("state", 142, [P, 4, 8, C])
        turn_r = at("turn_r", 174, [P, 8, C + 1])
        turn_i = at("turn_i", 174 + 4.03125, [P, 8, C + 1])
        q1, q2, q3, q4 = (at(f"q{i}", 182.0625 + 2 * i, [P, 4, C]) for i in range(4))
        q1q2 = at("q1q2", 182.0625, [P, 8 * C])
        q3q4 = at("q3q4", 186.0625, [P, 8 * C])
        d_diag = at("d_diag", 100, [GC, G, GC])
        y_nat = at("y_nat", 174, [P, T, SSM_W])
        y_f = at("y_f", 144, [P, KS, L])
        y_g = at("y_g", 128, [P, KS, L])
        y_hi = at("y_hi", 160, [P, KS, L], f32r)
        y_lo = at("y_lo", 176, [P, KS, L], f32r)
        small = at("small", 100, [P, 44, PAIRS])
        b_r = at("b_r", 103, [P, PAIRS, GC])
        b_i = at("b_i", 104, [P, PAIRS, GC])
        bb_stack = at("bb_stack", 103, [P, G, GC])
        c_nat = at("c_nat", 105, [P, 2, 4, P])
        bb_r = at("bb_r", 105, [P, PAIRS, GC])
        bb_i = at("bb_i", 106, [P, PAIRS, GC])
        c_t = at("c_t", 119, [P, 2, PAIRS, GC])
        t1 = at("t1", 108, [P, 8, NP * GC])
        t2 = at("t2", 112.5, [P, 8, NP * GC])
        pw_r = at("pw_r", 190.25, [P, PAIRS, NP])
        pw_i = at("pw_i", 190.8125, [P, PAIRS, NP])
        turn1_r = at("turn1_r", 191.375, [P, PAIRS])
        turn1_i = at("turn1_i", 191.4375, [P, PAIRS])
        mag8 = at("mag8", 191.5, [P, PAIRS])
        d_hg = at("d_hg", 191.5625, [GC, G])
        s1 = at("s1", 192, [P, L])
        v_pad = at("v_pad", 196, [P, L + 2])
        cv = at("cv", 200.0625, [P, L])
        ident = at("ident", 204.0625, [P, P])
        gain_pre = at("gain_pre", 204.5625, [P, KD])
        cw = at("cw", 204.625, [P, 3, KD])
        bg = at("bg", 204.75, [P, KS])
        ssq = at("ssq", 204.8125, [P, 3 * LT])
        va = at("va", 204.9375, [P, 3 * LT])
        vb = at("vb", 205.0625, [P, 3 * LT])
        vc = at("vc", 205.1875, [P, 3 * LT])
        rstd = at("rstd", 205.3125, [P, 3 * LT])
        RS = 5
        wb_raw = [at(f"wb_raw{i}", 128 + 4 * i, [P, D]) for i in range(RS)]
        p_nat = at("p_nat", 128, [P, LT, PLE])
        wp_raw = at("wp_raw", 136, [P, KP, D])
        x_in = [at(f"x_in{i}", 148 + 4 * i, [P, D]) for i in range(2)]
        x1 = [at("x1a", 156, [P, D]), at("x1b", 192, [P, D])]
        post_row = at("post_row", 196, [P, D])
        sig_row = at("sig_row", 196, [P, D])
        ple_row = at("ple_row", 200, [P, D])
        pt_hi = at("pt_hi", 0, [P, KP, L], f32r)
        pt_lo = at("pt_lo", 8, [P, KP, L], f32r)
        wp_hi = at("wp_hi", 16, [P, KP, D], f32r)
        wp_lo = at("wp_lo", 24, [P, KP, D], f32r)

        tile_ps = ctx.enter_context(nc.psum_tensor("tile_ps", [P, 4, HALF], f32))
        aux = ctx.enter_context(nc.psum_tensor("aux", [P, 4, HALF], f32))
        x1_dram = nc.dram_tensor("x1_dram", (L, D), f32, kind="Internal").ap()

        def slot_ps(s):
            return tile_ps[:, 2 * s:2 * s + 2, :]

        def flat(ap):
            return ap.rearrange("p a b -> p (a b)")

        def sem(name):
            return ctx.enter_context(nc.semaphore(name))

        x_loaded = [sem(f"x_loaded{i}") for i in range(LT)]
        wu_loaded = [sem("wu_loaded0"), sem("wu_loaded1")]
        consts_loaded = sem("consts_loaded")
        params_loaded = sem("params_loaded")
        ident_ready = sem("ident_ready")
        squares_done = sem("squares_done")
        var_ready = sem("var_ready")
        root_ready = sem("root_ready")
        xn_ready = sem("xn_ready")
        h_hi_ready = sem("h_hi_ready")
        h_ready = sem("h_ready")
        wu_hi_ready = sem("wu_hi_ready")
        wu_ready = sem("wu_ready")
        aux_full = sem("aux_full")
        aux_free = [sem(f"aux_free{i}") for i in range(4)]
        raw_full = [sem(f"raw_full{i}") for i in range(4)]
        w_hi_ready = sem("w_hi_ready")
        w_ready = sem("w_ready")
        tile_done = sem("tile_done")
        slot_free = [sem("slot_free0"), sem("slot_free1")]
        s1_full = sem("s1_full")
        s1_used = sem("s1_used")
        dve_chain = sem("dve_chain")
        conv_step = sem("conv_step")
        scan_step = sem("scan_step")
        pv_ready = sem("pv_ready")
        toep_zero = sem("toep_zero")
        kern_ready = sem("kern_ready")
        toep_ready = sem("toep_ready")
        state_ready = sem("state_ready")
        gelu_ready = sem("gelu_ready")
        y_hi_ready = sem("y_hi_ready")
        y_ready = sem("y_ready")
        gssm_ready = sem("gssm_ready")
        y2_ready = sem("y2_ready")
        z_done = sem("z_done")
        z_hi_ready = sem("z_hi_ready")
        z_ready = sem("z_ready")
        rc_ready = sem("rc_ready")
        sum_ready = sem("sum_ready")
        mx_hi_ready = sem("mx_hi_ready")
        mx_ready = sem("mx_ready")
        wb_full = [sem(f"wb_full{i}") for i in range(RS)]
        wb_hi_ready = sem("wb_hi_ready")
        wb_ready = sem("wb_ready")
        ple_in = sem("ple_in")
        wp_hi_ready = sem("wp_hi_ready")
        wp_ready = sem("wp_ready")
        pt_hi_ready = sem("pt_hi_ready")
        pt_ready = sem("pt_ready")
        x_in_full = [sem("x_in_full0"), sem("x_in_full1")]
        rows_loaded = sem("rows_loaded")
        o_ready = sem("o_ready")
        x1_ready = sem("x1_ready")
        x1_stored = [sem("x1_stored0"), sem("x1_stored1")]
        x1_hi_ready = sem("x1_hi_ready")
        x1_split = sem("x1_split")
        sig_ready = sem("sig_ready")
        e_ready = sem("e_ready")
        esq_done = sem("esq_done")
        out_ready = sem("out_ready")
        out_stored = [sem("out_stored0"), sem("out_stored1")]

        A_C = 0
        A_H = A_C + 2
        A_U = A_H + 2 * KD
        A_W = A_U + T
        A_UT = A_W + G // 4
        A_K = A_UT + G // 4
        A_WC = A_K + G // 4
        A_Y = A_WC + G // 4
        A_YT = A_Y + G // 4
        A_X1 = A_YT + 2 * KS
        P_AT = 3

        def a_x1(lt, half):
            return A_X1 + 2 * lt + half + (2 * KP if lt >= P_AT - 1 else 0)

        A_PT = A_X1 + 2 * (P_AT - 1)
        A_E = A_X1 + 2 * LT + 2 * KP

        block = ctx.enter_context(nc.Block())

        @block.sync
        def _(sp):
            for i in range(4):
                sp.dma_start(x_tile[i][:], x[0, i * P:(i + 1) * P, :]).then_inc(x_loaded[i], 16)
            wu_view = w_in[0].rearrange("(k p) e -> p k e", p=P)
            for i in range(4, LT):
                sp.dma_start(x_tile[i][:], x[0, i * P:(i + 1) * P, :]).then_inc(x_loaded[i], 16)
            sp.dma_start(wu_raw[:], wu_view[:, 0:KD // 2, 0:SSM_W]).then_inc(wu_loaded[0], 16)
            sp.dma_start(wu_raw2[:], wu_view[:, KD // 2:KD, 0:SSM_W]).then_inc(wu_loaded[1], 16)

            def load_tile(n_is_first, n, c, weights, col, kk):
                if n_is_first:
                    sp.wait_ge(wu_ready, 1)
                else:
                    sp.wait_ge(w_ready, n - 3)
                src = weights.rearrange("(k p) e -> p k e", p=P)
                sp.dma_start(w_raw[c][:, 0:kk, :], src[:, :, bass.ds(col, P)]).then_inc(raw_full[c], 16)

            def load_conv(q, ct, first=False):
                for c, col in enumerate((COL_XC, COL_CC, COL_GC, COL_BC)):
                    load_tile(first, 4 * q + c, c, w_in[0], col + ct * P, KD)

            load_conv(Q_CONV0, 0, first=True)
            with sp.Fori(Q_CONV1, Q_GSSM) as q:
                load_conv(q, q)
            sp.wait_ge(kern_ready, 1)
            sp.wait_ge(toep_zero, 1)
            for j in range(T):
                m = T - 1 - j
                sp.dma_start(toep[m * GC:(m + 1) * GC, :, j * GC:T * GC],
                             kern[:, :, 0:(T - j) * GC]).then_inc(toep_ready, 16)
            for c in range(4):
                load_tile(False, 4 * Q_GSSM + c, c, w_in[0], COL_G + c * P, KD)
            for c in range(4):
                load_tile(False, 4 * Q_GLU + c, c, w_glu[0], c * P, KS)
            load_conv(Q_CONV3, 3)
            with sp.Fori(Q_YA, Q_CONV4) as q:
                for c in range(4):
                    d = 2 * q + (c // 2 - 2 * Q_YA)
                    if c % 2 == 0:
                        load_tile(False, 4 * q + c, c, w_in[0], COL_RS + d * P, KD)
                    else:
                        load_tile(False, 4 * q + c, c, w_ssm_out[0], q * (2 * P) + (c // 2 - 2 * Q_YA) * P, KS)
            with sp.Fori(Q_CONV4, Q_RC) as q:
                load_conv(q, q - (Q_CONV4 - 4))
            with sp.Fori(Q_RC, Q_YB) as q:
                for c in range(4):
                    load_tile(False, 4 * q + c, c, w_in[0], COL_RC - 4 * Q_RC * P + c * P + q * 4 * P, KD)
            with sp.Fori(Q_YB, Q_END) as q:
                for c in range(4):
                    load_tile(False, 4 * q + c, c, w_conv_out[0], q * 4 * P + (c - 4 * Q_YB) * P, KD)

            sp.wait_ge(z_done, KD)
            sp.dma_start(post_row[:], post_norm[0].partition_broadcast(P)).then_inc(rows_loaded, 16)
            sp.dma_start(ple_row[:], ple_norm[0].partition_broadcast(P)).then_inc(rows_loaded, 16)

            def load_big(k, index, weights):
                sp.dma_start(wb_raw[k % RS][:], weights[k * P:(k + 1) * P, :]).then_inc(wb_full[k % RS], 16)

            for k in range(KD):
                if k < RS:
                    sp.wait_ge(mx_ready, k + 1)
                else:
                    sp.wait_ge(wb_ready, k - RS + 1)
                load_big(k, k, w_o[0])

            def load_x(lt):
                if lt == 0:
                    sp.wait_ge(mx_ready, KD)
                if lt >= 2:
                    sp.wait_ge(x1_ready, lt - 1)
                sp.dma_start(x_in[lt % 2][:], x[0, lt * P:(lt + 1) * P, :]).then_inc(x_in_full[lt % 2], 16)

            load_x(0)
            load_x(1)
            sp.wait_ge(wb_ready, KD)
            sp.dma_start(p_nat[:], p[0, 0].rearrange("(t q) k -> q t k", q=P)).then_inc(ple_in, 16)
            sp.dma_start(wp_raw[:], w_ple[0].rearrange("(k q) d -> q k d", q=P)).then_inc(ple_in, 16)
            for lt in range(LT):
                sp.wait_ge(x1_ready, lt + 1)
                sp.dma_start(x1_dram[lt * P:(lt + 1) * P, :], x1[lt % 2][:]).then_inc(x1_stored[lt % 2], 16)
                if lt + 2 < LT:
                    load_x(lt + 2)
                if lt == P_AT:
                    sp.wait_ge(pt_ready, 2 * KP)
                    sp.wait_ge(wp_ready, 1)
                    for k in range(RS):
                        load_big(k, KD + k, w_ple_gate[0])

            def load_x1(lt):
                sp.wait_ge(x1_stored[lt % 2], 16 * (lt // 2 + 1))
                if lt >= 2:
                    sp.wait_ge(out_ready, lt - 1)
                sp.dma_start(x_in[lt % 2][:], x1_dram[lt * P:(lt + 1) * P, :]).then_inc(x_in_full[lt % 2], 16)

            sp.wait_ge(x1_ready, LT)
            load_x1(0)
            load_x1(1)
            for k in range(RS, KD):
                sp.wait_ge(wb_ready, KD + k - RS + 1)
                load_big(k, KD + k, w_ple_gate[0])
            for lt in range(LT):
                sp.wait_ge(out_ready, lt + 1)
                sp.dma_start(out[0, lt * P:(lt + 1) * P, :], x1[lt % 2][:]).then_inc(out_stored[lt % 2], 16)
                if lt + 2 < LT:
                    load_x1(lt + 2)
            for i in range(2):
                sp.wait_ge(out_stored[i], 16 * (LT // 2))

        @block.gpsimd
        def _(pool):
            nc.gpsimd.memset(ident[:], 0.0).then_inc(ident_ready, 1)
            pool.wait_ge(ident_ready, 1)
            nc.gpsimd.affine_select(out=ident[:], in_=ident[:], compare_op=ALU.not_equal, fill=1.0, base=0,
                                    pattern=[[-1, P]], channel_multiplier=1).then_inc(ident_ready, 1)

            with nc.allow_non_contiguous_dma(reason="small parameter tables"):
                pool.dma_start(gain_pre[:], pre_norm[0].rearrange("(k p) -> p k", p=P)).then_inc(consts_loaded, 16)
                pool.dma_start(cw[:], conv_w[0].rearrange("t (k p) -> p t k", p=P)).then_inc(consts_loaded, 16)
                pool.dma_start(bg[:], b_glu[0].rearrange("(k p) -> p k", p=P)).then_inc(consts_loaded, 16)
                for ri, cc in enumerate((c_re, c_im)):
                    src = cc[0].rearrange("(f a) h s -> (a h) f s", f=4)
                    for b in range(2):
                        pool.dma_start(c_nat[:, ri, :, b * N_STATE:(b + 1) * N_STATE], src
                                       ).then_inc(params_loaded, 16)
                for b in range(2):
                    rows = slice(b * N_STATE, (b + 1) * N_STATE)
                    for n, aa in enumerate((a_re, a_im)):
                        pool.dma_start(small[rows, n, :],
                                       aa[0].rearrange("(a b) s -> b s a", b=2)[b]).then_inc(params_loaded, 16)
                    pool.dma_start(small[rows, 2, :], log_step[0].rearrange("(a b) -> b a", b=2)[b]
                                   .partition_broadcast(N_STATE)).then_inc(params_loaded, 16)
                    for dst, bb in ((b_r, b_re), (b_i, b_im)):
                        pool.dma_start(dst[rows, :, :],
                                       bb[0].rearrange("(a b) s h -> b s a h", b=2)[b]).then_inc(params_loaded, 16)
                pool.dma_start(d_hg[:], d_skip[0].rearrange("(g h) -> h g", h=GC)).then_inc(params_loaded, 16)

            def lo(n, c, kk):
                pool.wait_ge(w_hi_ready, n + 1)
                nc.gpsimd.tensor_tensor(w_lo[c % 2][:, 0:kk, :], w_raw[c][:, 0:kk, :],
                                        w_hi[c % 2][:, 0:kk, :].bitcast(f32), ALU.subtract).then_inc(w_ready, 1)

            def quad(q, kks=(KD, KD, KD, KD)):
                for c in range(4):
                    lo(4 * q + c, c, kks[c])

            quad(Q_CONV0)
            with pool.Fori(Q_CONV1, Q_GLU) as q:
                quad(q)
            quad(Q_GLU, (KS,) * 4)
            quad(Q_CONV3)
            with pool.Fori(Q_YA, Q_CONV4) as q:
                quad(q, (KD, KS, KD, KS))
            with pool.Fori(Q_CONV4, Q_END) as q:
                quad(q)

        @block.scalar
        def _(act):
            def evac_start(use):
                act.wait_ge(aux_full, use + 1)

            for half in range(2):
                for i in range(4 * half, 4 * half + 4):
                    act.wait_ge(x_loaded[i], 16)
                    if i:
                        act.wait_ge(squares_done, i)
                    nc.scalar.activation(sq_junk[:], x_tile[i][:], ACT.Square,
                                         accum_out=ssq[:, i:i + 1]).then_inc(squares_done, 1)
                act.wait_ge(var_ready, half + 1)
                nc.scalar.activation(vb[:, 4 * half:4 * half + 4], va[:, 4 * half:4 * half + 4],
                                     ACT.Sqrt).then_inc(root_ready, 1)
            act.wait_ge(consts_loaded, 48)
            for half in range(2):
                for k in range(KD):
                    use = A_H + half * KD + k
                    evac_start(use)
                    nc.scalar.activation(big_hi[:, k, half * HALF:(half + 1) * HALF], aux[:, use % 4, :], ACT.Copy,
                                         scale=gain_pre[:, k:k + 1]).then_inc(h_hi_ready, 1)
            for i, src in enumerate((wu_raw, wu_raw2)):
                act.wait_ge(wu_loaded[i], 16)
                nc.scalar.activation(wu_hi[:, i * (KD // 2):(i + 1) * (KD // 2), :], src[:],
                                     ACT.Copy).then_inc(wu_hi_ready, 1)

            def hi(n, c, kk, first=False):
                act.wait_ge(raw_full[c], 4 * n + (16 - 4 * c))
                if not first:
                    act.wait_ge(tile_done, n - 1)
                nc.scalar.activation(w_hi[c % 2][:, 0:kk, :], w_raw[c][:, 0:kk, :], ACT.Copy).then_inc(w_hi_ready, 1)

            def to_s1(func, n, c, w, first=False, **kw):
                act.wait_ge(tile_done, n + 1)
                if not first:
                    act.wait_ge(s1_used, w)
                nc.scalar.activation(s1[:], flat(slot_ps(c % 2)), func, **kw).then_inc(s1_full, 1)

            def conv_quad(q, w, first=False, next_kk=KD):
                n = 4 * q
                hi(n + 1, 1, KD, first)
                act.wait_ge(tile_done, n + 1)
                if not first:
                    act.wait_ge(s1_used, w)
                nc.scalar.activation(s1[:], flat(slot_ps(0)), ACT.Copy).then_inc(s1_full, 1)
                act.wait_ge(s1_full, w + 1)
                act.sem_inc(slot_free[0], 1)
                hi(n + 2, 2, KD)
                hi(n + 3, 3, KD)
                act.wait_ge(tile_done, n + 3)
                act.wait_ge(s1_used, w + 1)
                nc.scalar.activation(s1[:], flat(slot_ps(0)), ACT.Silu).then_inc(s1_full, 1)
                act.wait_ge(s1_full, w + 2)
                act.sem_inc(slot_free[0], 1)
                hi(n + 4, 0, next_kk)

            hi(0, 0, KD, first=True)
            conv_quad(Q_CONV0, 0, first=True)

            def copy_bank(use, dst, src):
                evac_start(use)
                nc.scalar.activation(dst, src, ACT.Copy).then_inc(aux_free[use % 4], 1)

            for b in range(0, G // 4, 2):
                copy_bank(A_W + b, flat(w_in_state[:, 4 * b:4 * b + 4, :]), aux[:, (A_W + b) % 4, :])
            for b in range(0, G // 4, 2):
                copy_bank(A_UT + b, flat(u_chunk[:, 4 * b:4 * b + 4, :]), aux[:, (A_UT + b) % 4, :])
            for b in range(0, G // 4, 2):
                copy_bank(A_K + b, flat(kern[:, 4 * b:4 * b + 4, :]), aux[0:GC, (A_K + b) % 4, :])
            for b in range(0, G // 4, 2):
                use = A_WC + b
                evac_start(use)
                nc.scalar.activation(flat(w_c[0:N_STATE, b // 2, 0]), aux[0:N_STATE, use % 4, :], ACT.Copy)
                nc.scalar.activation(flat(w_c[0:N_STATE, b // 2, 1]), aux[N_STATE:P, use % 4, :],
                                     ACT.Copy).then_inc(aux_free[use % 4], 1)

            with act.Fori(Q_CONV1, Q_GSSM) as q:
                conv_quad(q, 2 * q)

            for b in range(0, G // 4, 2):
                use = A_Y + b
                evac_start(use)
                nc.scalar.activation(
                    y_nat[:, :, 4 * b * GC:4 * (b + 1) * GC].rearrange("c j (g h) -> c g j h", h=GC),
                    aux[:, use % 4, :].rearrange("c (g j h) -> c g j h", g=4, h=GC),
                    ACT.Copy).then_inc(aux_free[use % 4], 1)
            for ct in range(KS):
                for jb in range(2):
                    use = A_YT + 2 * ct + jb
                    evac_start(use)
                    ins = nc.scalar.activation(
                        y_f[:, ct, :].rearrange("p (c j) -> p j c", j=T)[:, 4 * jb:4 * jb + 4, :],
                        aux[:, use % 4, :].rearrange("p (j c) -> p j c", c=C), ACT.Gelu_apprx_tanh)
                    ins.then_inc(gelu_ready, 1)
                    act.wait_ge(gelu_ready, 2 * ct + jb + 1)
                    act.sem_inc(aux_free[use % 4], 1)
            for ct in range(KS):
                nc.scalar.activation(y_hi[:, ct, :], y_f[:, ct, :], ACT.Copy).then_inc(y_hi_ready, 1)

            for c in range(4):
                n = 4 * Q_GSSM + c
                hi(n + 1, (c + 1) % 4, KD if c < 3 else KS)
                act.wait_ge(tile_done, n + 1)
                nc.scalar.activation(y_g[:, c, :], flat(slot_ps(c % 2)), ACT.Silu).then_inc(gssm_ready, 1)
                act.wait_ge(gssm_ready, c + 1)
                act.sem_inc(slot_free[c % 2], 1)
            for c in range(4):
                n = 4 * Q_GLU + c
                hi(n + 1, (c + 1) % 4, KS if c < 3 else KD)
                to_s1(ACT.Sigmoid, n, c, 6 + c, bias=bg[:, c:c + 1])
                act.wait_ge(s1_full, 7 + c)
                act.sem_inc(slot_free[c % 2], 1)
            for ct in range(KS):
                act.wait_ge(y2_ready, ct + 1)
                nc.scalar.activation(y_hi[:, ct, :], y_g[:, ct, :], ACT.Copy).then_inc(y_hi_ready, 1)

            conv_quad(Q_CONV3, 10)

            with act.Fori(Q_YA, Q_CONV4) as q:
                for c in range(4):
                    n = 4 * q + c
                    hi(n + 1, (c + 1) % 4, KS if c % 2 == 0 else KD)
                    if c % 2 == 0:
                        w = 2 * q + (12 + c // 2 - 2 * Q_YA)
                        to_s1(ACT.Sigmoid, n, c, w)
                        act.wait_ge(s1_full, w + 1)
                        act.sem_inc(slot_free[0], 1)
            with act.Fori(Q_CONV4, Q_RC) as q:
                conv_quad(q, 2 * q + (20 - 2 * Q_CONV4))

            with act.Fori(Q_RC, Q_YB) as q:
                for c in range(4):
                    n = 4 * q + c
                    hi(n + 1, (c + 1) % 4, KD)
                    act.wait_ge(tile_done, n + 1)
                    nc.scalar.activation(rc_gate[:, bass.ds(4 * q + (c - 4 * Q_RC), 1), :].rearrange("p a l -> p (a l)"),
                                         flat(slot_ps(c % 2)), ACT.Sigmoid).then_inc(rc_ready, 1)
                    act.wait_ge(rc_ready, 4 * q + (c + 1 - 4 * Q_RC))
                    act.sem_inc(slot_free[c % 2], 1)

            act.wait_ge(z_done, KD)
            for k in range(KD):
                nc.scalar.activation(big_hi[:, k, :], z[:, k, :], ACT.Copy).then_inc(z_hi_ready, 1)

            def merge_hi(q, c, d):
                act.wait_ge(sum_ready, d + 1)
                nc.scalar.activation(mx_hi[:, bass.ds(d, 1), :].rearrange("p a l -> p (a l)"),
                                     yam[:, bass.ds(d, 1), :].rearrange("p a l -> p (a l)"),
                                     ACT.Copy).then_inc(mx_hi_ready, 1)

            act.wait_ge(z_ready, KD)
            with act.Fori(Q_YB, Q_END - 1) as q:
                for c in range(4):
                    hi(4 * q + c + 1, (c + 1) % 4, KD)
                    merge_hi(q, c, 4 * q + (c - 4 * Q_YB))
            for c in range(4):
                if c < 3:
                    hi(4 * (Q_END - 1) + c + 1, c + 1, KD)
                merge_hi(Q_END - 1, c, 4 + c)

            def big_part(k, index):
                act.wait_ge(wb_full[k % RS], 16 * wb_round(k, index))
                nc.scalar.activation(big_hi[:, k, :], wb_raw[k % RS][:], ACT.Copy).then_inc(wb_hi_ready, 1)

            def wb_round(k, index):
                per = [len(range(s, KD, RS)) for s in range(RS)]
                return index * per[k % RS] + k // RS + 1

            for k in range(KD):
                big_part(k, 0)

            def root(i):
                act.wait_ge(var_ready, 2 + i + 1)
                j = LT + i
                nc.scalar.activation(vb[:, j:j + 1], va[:, j:j + 1], ACT.Sqrt).then_inc(root_ready, 1)

            def x1_hi(lt):
                for half in range(2):
                    use = a_x1(lt, half)
                    evac_start(use)
                    nc.scalar.activation(mx_hi[:, 4 * half:4 * half + 4, lt * P:(lt + 1) * P],
                                         aux[:, use % 4, :].rearrange("p (k l) -> p k l", l=P),
                                         ACT.Copy).then_inc(x1_hi_ready, 1)

            for lt in range(LT):
                act.wait_ge(tile_done, 4 * Q_END + lt + 1)
                if lt >= 2:
                    act.wait_ge(x1_stored[lt % 2], 16 * (lt // 2))
                    act.wait_ge(aux_full, a_x1(lt - 2, 1) + 1)
                nc.scalar.activation(x1[lt % 2][:], flat(slot_ps(lt % 2)), ACT.Square,
                                     accum_out=ssq[:, LT + lt:LT + lt + 1]).then_inc(squares_done, 1)
                root(lt)
                if lt == P_AT - 1:
                    act.wait_ge(ple_in, 32)
                    nc.scalar.activation(wp_hi[:], wp_raw[:], ACT.Copy).then_inc(wp_hi_ready, 1)
                if lt == P_AT:
                    for u in range(2 * KP):
                        use = A_PT + u
                        evac_start(use)
                        nc.scalar.activation(pt_hi[:, u // 2, (u % 2) * HALF:(u % 2 + 1) * HALF], aux[:, use % 4, :],
                                             ACT.Copy).then_inc(pt_hi_ready, 1)
                if lt >= 1:
                    x1_hi(lt - 1)
            for k in range(KD):
                big_part(k, 1)
                if k == 3:
                    x1_hi(LT - 1)

            for lt in range(LT):
                act.wait_ge(tile_done, 4 * Q_END + LT + lt + 1)
                if lt >= 1:
                    act.wait_ge(esq_done, lt)
                nc.scalar.activation(sig_row[:], flat(slot_ps(lt % 2)), ACT.Sigmoid).then_inc(sig_ready, 1)
                act.wait_ge(sig_ready, lt + 1)
                act.sem_inc(slot_free[lt % 2], 1)
                act.wait_ge(e_ready, lt + 1)
                j = 2 * LT + lt
                nc.scalar.activation(sig_row[:], x1[lt % 2][:], ACT.Square,
                                     accum_out=ssq[:, j:j + 1]).then_inc(esq_done, 1)
                root(LT + lt)

        @block.vector
        def _(dve):
            V = nc.vector
            count = [0]

            def link(ins):
                count[0] += 1
                ins.then_inc(dve_chain, 1)
                dve.wait_ge(dve_chain, count[0])

            def tt(o, a, b, op):
                link(V.tensor_tensor(o, a, b, op))

            def ts(o, a, s0, op0, s1_=None, op1=None):
                if op1 is None:
                    link(V.tensor_scalar(o, a, s0, None, op0))
                else:
                    link(V.tensor_scalar(o, a, s0, s1_, op0, op1))

            def stt(o, a, s, b, op0, op1):
                link(V.scalar_tensor_tensor(out=o, in0=a, scalar=s, in1=b, op0=op0, op1=op1))

            def inverse(j0, j1, n):
                ts(vc[:, j0:j1], ssq[:, j0:j1], 1.0 / D, ALU.mult, EPS, ALU.add)
                V.reciprocal(va[:, j0:j1], vc[:, j0:j1]).then_inc(var_ready, 1)

            def refine(j0, j1, n):
                dve.wait_ge(root_ready, n)
                s = slice(j0, j1)
                tt(rstd[:, s], vb[:, s], vb[:, s], ALU.mult)
                tt(rstd[:, s], rstd[:, s], vc[:, s], ALU.mult)
                ts(rstd[:, s], rstd[:, s], -0.5, ALU.mult, 1.5, ALU.add)
                tt(rstd[:, s], rstd[:, s], vb[:, s], ALU.mult)

            for half in range(2):
                dve.wait_ge(squares_done, 4 * half + 4)
                inverse(4 * half, 4 * half + 4, half)
                refine(4 * half, 4 * half + 4, half + 1)
                for i in range(4 * half, 4 * half + 4):
                    V.tensor_scalar(x_tile[i][:], x_tile[i][:], rstd[:, i:i + 1], None,
                                    ALU.mult).then_inc(xn_ready, 1)
            for ri in range(2):
                dve.wait_ge(aux_full, A_C + ri + 1)
                for par in range(2):
                    rows = slice(par * N_STATE, (par + 1) * N_STATE)
                    last = V.tensor_copy(c_t[rows, ri], aux[rows, A_C + ri, :].rearrange(
                        "s (a b h) -> s a b h", b=2, h=GC)[:, :, par, :])
                last.then_inc(aux_free[A_C + ri], 1)
            dve.wait_ge(consts_loaded, 48)
            for half in range(2):
                for k in range(KD):
                    use = A_H + half * KD + k
                    dve.wait_ge(h_hi_ready, half * KD + k + 1)
                    cols = slice(half * HALF, (half + 1) * HALF)
                    V.scalar_tensor_tensor(out=big_lo[:, k, cols], in0=aux[:, use % 4, :],
                                           scalar=gain_pre[:, k:k + 1], in1=big_hi[:, k, cols].bitcast(f32),
                                           op0=ALU.mult, op1=ALU.subtract).then_inc(aux_free[use % 4], 1)
            for i, src in enumerate((wu_raw, wu_raw2)):
                dve.wait_ge(wu_hi_ready, i + 1)
                ks = slice(i * (KD // 2), (i + 1) * (KD // 2))
                last = V.tensor_tensor(wu_lo[:, ks, :], src[:], wu_hi[:, ks, :].bitcast(f32), ALU.subtract)
            link(last)
            dve.sem_inc(wu_ready, 1)

            names = {}

            def t(name):
                if name not in names:
                    names[name] = len(names)
                return small[:, names[name], :]

            for n in ("are", "aim", "ls"):
                t(n)

            def exp_to(o, a):
                LN2_HI, LN2_LO = 0.693359375, -2.12194440e-4
                ROUND = 12582912.0
                ts(t("ea"), a, -170.0, ALU.max, 170.0, ALU.min)
                ts(t("en"), t("ea"), 1.0 / math.log(2.0), ALU.mult, ROUND, ALU.add)
                ts(t("en"), t("en"), ROUND, ALU.subtract)
                stt(t("er"), t("en"), -LN2_HI, t("ea"), ALU.mult, ALU.add)
                stt(t("er"), t("en"), -LN2_LO, t("er"), ALU.mult, ALU.add)
                ts(t("ep"), t("er"), 1.0 / math.factorial(7), ALU.mult)
                for i in range(6, 0, -1):
                    stt(t("ep"), t("ep"), 1.0 / math.factorial(i), t("er"), ALU.add, ALU.mult)
                ts(t("ep"), t("ep"), 1.0, ALU.add)
                ts(t("e1"), t("en"), -126.0, ALU.max, 127.0, ALU.min)
                tt(t("e2"), t("en"), t("e1"), ALU.subtract)
                ts(t("e2"), t("e2"), -126.0, ALU.max, 127.0, ALU.min)
                for e in ("e1", "e2"):
                    ts(t(e + "i").bitcast(i32), t(e), 127.0, ALU.add, 8388608.0, ALU.mult)
                    tt(t("ep"), t("ep"), t(e + "i"), ALU.mult)
                link(V.tensor_copy(o, t("ep")))

            def cmul(o_r, o_i, a_r, a_i, b_r_, b_i_, u, v):
                tt(u, a_r, b_r_, ALU.mult)
                tt(v, a_i, b_i_, ALU.mult)
                tt(o_r, u, v, ALU.subtract)
                tt(u, a_r, b_i_, ALU.mult)
                tt(v, a_i, b_r_, ALU.mult)
                tt(o_i, u, v, ALU.add)

            def discretise():
                dve.wait_ge(params_loaded, 16 * 15)
                exp_to(t("dt"), t("ls"))
                tt(t("arg"), t("are"), t("dt"), ALU.mult)
                exp_to(t("mag"), t("arg"))
                tt(t("th"), t("aim"), t("dt"), ALU.mult)
                ts(t("en"), t("th"), 1.0 / (2 * math.pi), ALU.mult, 12582912.0, ALU.add)
                ts(t("en"), t("en"), 12582912.0, ALU.subtract)
                C1 = 6.28125
                C2 = float(round((2 * math.pi - C1) * 2 ** 22)) / 2 ** 22
                C3 = 2 * math.pi - C1 - C2
                for cst in (C1, C2, C3):
                    stt(t("th"), t("en"), -cst, t("th"), ALU.mult, ALU.add)
                ts(t("q"), t("th"), 0.25, ALU.mult, 0.8, ALU.min)
                ts(t("q"), t("q"), -0.8, ALU.max)
                tt(t("qq"), t("q"), t("q"), ALU.mult)
                ts(t("s"), t("qq"), 1.0 / math.factorial(9), ALU.mult)
                for i in (7, 5, 3):
                    sign = 1.0 if i == 5 else -1.0
                    stt(t("s"), t("s"), sign / math.factorial(i), t("qq"), ALU.add, ALU.mult)
                stt(t("s"), t("s"), 1.0, t("q"), ALU.add, ALU.mult)
                ts(t("c"), t("qq"), -1.0 / math.factorial(10), ALU.mult)
                for i in (8, 6, 4, 2):
                    sign = 1.0 if i % 4 == 0 else -1.0
                    stt(t("c"), t("c"), sign / math.factorial(i), t("qq"), ALU.add, ALU.mult)
                ts(t("c"), t("c"), 1.0, ALU.add)
                for _ in range(2):
                    stt(t("c2"), t("s"), -2.0, t("s"), ALU.mult, ALU.mult)
                    stt(t("s"), t("s"), 2.0, t("c"), ALU.mult, ALU.mult)
                    ts(t("c"), t("c2"), 1.0, ALU.add)
                tt(t("ar"), t("mag"), t("c"), ALU.mult)
                tt(t("ai"), t("mag"), t("s"), ALU.mult)
                ts(t("nr"), t("ar"), 1.0, ALU.subtract)
                tt(t("u"), t("are"), t("are"), ALU.mult)
                tt(t("v"), t("aim"), t("aim"), ALU.mult)
                tt(t("u"), t("u"), t("v"), ALU.add)
                link(V.reciprocal(t("rd"), t("u")))
                tt(t("u"), t("nr"), t("are"), ALU.mult)
                tt(t("v"), t("ai"), t("aim"), ALU.mult)
                tt(t("u"), t("u"), t("v"), ALU.add)
                tt(t("fr"), t("u"), t("rd"), ALU.mult)
                tt(t("u"), t("ai"), t("are"), ALU.mult)
                tt(t("v"), t("nr"), t("aim"), ALU.mult)
                tt(t("u"), t("u"), t("v"), ALU.subtract)
                tt(t("fi"), t("u"), t("rd"), ALU.mult)

            def powers():
                tt(t("u"), t("mag"), t("mag"), ALU.mult)
                tt(t("u"), t("u"), t("u"), ALU.mult)
                tt(mag8[:], t("u"), t("u"), ALU.mult)
                cmul(t("x2"), t("y2"), t("c"), t("s"), t("c"), t("s"), t("u"), t("v"))
                cmul(t("x4"), t("y4"), t("x2"), t("y2"), t("x2"), t("y2"), t("u"), t("v"))
                cmul(turn1_r[:], turn1_i[:], t("x4"), t("y4"), t("x4"), t("y4"), t("u"), t("v"))
                V.memset(pw_r[:, :, 0:1], 1.0)
                V.memset(pw_i[:, :, 0:1], 0.0)
                V.tensor_copy(pw_r[:, :, 1:2], t("ar").unsqueeze(2))
                link(V.tensor_copy(pw_i[:, :, 1:2], t("ai").unsqueeze(2)))
                m = 1
                while m < T:
                    uu = t1[:].rearrange("p a b -> p (a b)")[:, 0:PAIRS * m].rearrange("p (a b) -> p a b", b=m)
                    vv = t2[:].rearrange("p a b -> p (a b)")[:, 0:PAIRS * m].rearrange("p (a b) -> p a b", b=m)
                    lo_, hi_ = slice(1, m + 1), slice(m + 1, 2 * m + 1)
                    by = [w[:, :, m:m + 1].to_broadcast([P, PAIRS, m]) for w in (pw_r, pw_i)]
                    cmul(pw_r[:, :, hi_], pw_i[:, :, hi_], pw_r[:, :, lo_], pw_i[:, :, lo_], by[0], by[1], uu, vv)
                    m *= 2

            def per_row(ap):
                return ap.unsqueeze(2).to_broadcast([P, PAIRS, GC])

            def bbar():
                u = t1[:].rearrange("p a b -> p (a b)")[:, 0:PAIRS * GC].rearrange("p (a b) -> p a b", b=GC)
                v = t2[:].rearrange("p a b -> p (a b)")[:, 0:PAIRS * GC].rearrange("p (a b) -> p a b", b=GC)
                cmul(bb_r[:], bb_i[:], b_r[:], b_i[:], per_row(t("fr")), per_row(t("fi")), u, v)
                for ri, src in enumerate((bb_r, bb_i)):
                    for par in range(2):
                        link(V.tensor_copy(
                            bb_stack[ri * N_STATE:(ri + 1) * N_STATE, :, :]
                            .rearrange("s (a b) h -> s a b h", b=2)[:, :, par, :],
                            src[par * N_STATE:(par + 1) * N_STATE, :, :]))

            def table(dst, n_pow, coef_r, coef_i, half, im_sign):
                prs = slice(8 * half, 8 * half + 8)
                cols = n_pow * GC
                u = t1[:].rearrange("p a b -> p (a b)")[:, 0:8 * cols]
                v = t2[:].rearrange("p a b -> p (a b)")[:, 0:8 * cols]
                view = lambda w: w.rearrange("p (a n h) -> p a n h", a=8, h=GC)
                pw = [w[:, prs, 0:n_pow].unsqueeze(3).to_broadcast([P, 8, n_pow, GC]) for w in (pw_r, pw_i)]
                co = [w[:, prs, :].unsqueeze(2).to_broadcast([P, 8, n_pow, GC]) for w in (coef_r, coef_i)]
                for ri in range(2):
                    V.tensor_tensor(view(u), pw[0], co[ri], ALU.mult)
                    tt(view(v), pw[1], co[1 - ri], ALU.mult)
                    for par in range(2):
                        rows = slice(par * N_STATE, (par + 1) * N_STATE)
                        o = dst[ri * N_STATE:(ri + 1) * N_STATE].rearrange("s (a b) c -> s a b c", b=2)[:, prs, par, :]
                        uu = u[rows].rearrange("s (a c) -> s a c", a=8)
                        vv = v[rows].rearrange("s (a c) -> s a c", a=8)
                        if ri == 0:
                            last = V.tensor_tensor(o, uu, vv, ALU.subtract)
                        elif im_sign > 0:
                            last = V.tensor_tensor(o, uu, vv, ALU.add)
                        else:
                            last = V.scalar_tensor_tensor(out=o, in0=uu, scalar=-1.0, in1=vv, op0=ALU.mult,
                                                          op1=ALU.subtract)
                    link(last)

            ca_flat = ca[:].rearrange("p g n h -> p g (n h)")

            def u_bank(j):
                use = A_U + j
                dve.wait_ge(aux_full, use + 1)
                V.tensor_copy(u_nat[:, :, T - 1 - j, :],
                              aux[:, use % 4, :].rearrange("c (g h) -> c g h", h=GC)).then_inc(aux_free[use % 4], 1)

            discretise()
            for j in range(4):
                u_bank(j)
            powers()
            bbar()
            u_bank(4)
            table(ca_flat, NP, c_t[:, 0], c_t[:, 1], 0, -1)
            u_bank(5)
            table(ca_flat, NP, c_t[:, 0], c_t[:, 1], 1, -1)
            u_bank(6)
            u_bank(7)

            link(V.memset(v_pad[:, 0:2], 0.0))

            def tap(n_tap, ct):
                return cw[:, n_tap, bass.ds(ct, 1)]

            def conv_cc(q, ct, w, chain):
                n = 4 * q
                dve.wait_ge(tile_done, n + 2)
                dve.wait_ge(s1_full, w + 1)
                V.tensor_tensor(v_pad[:, 2:L + 2], flat(slot_ps(1)), s1[:], ALU.mult).then_inc(s1_used, 1)
                dve.wait_ge(s1_used, w + 1)
                dve.sem_inc(slot_free[1], 1)
                V.tensor_scalar(cv[:], v_pad[:, 2:L + 2], tap(2, ct), None, ALU.mult).then_inc(conv_step, 1)
                dve.wait_ge(conv_step, chain + 1)
                V.scalar_tensor_tensor(out=cv[:], in0=v_pad[:, 1:L + 1], scalar=tap(1, ct), in1=cv[:],
                                       op0=ALU.mult, op1=ALU.add).then_inc(conv_step, 1)
                dve.wait_ge(conv_step, chain + 2)
                V.scalar_tensor_tensor(out=cv[:], in0=v_pad[:, 0:L], scalar=tap(0, ct), in1=cv[:],
                                       op0=ALU.mult, op1=ALU.add).then_inc(conv_step, 1)

            def conv_bc(q, ct, w, chain):
                n = 4 * q
                dve.wait_ge(tile_done, n + 4)
                dve.wait_ge(conv_step, chain + 3)
                V.tensor_tensor(cv[:], flat(slot_ps(1)), cv[:], ALU.mult).then_inc(conv_step, 1)
                dve.wait_ge(conv_step, chain + 4)
                dve.sem_inc(slot_free[1], 1)
                dve.wait_ge(s1_full, w + 2)
                V.tensor_tensor(z[:, bass.ds(ct, 1), :].rearrange("p a l -> p (a l)"), cv[:], s1[:],
                                ALU.mult).then_inc(z_done, 1)
                dve.wait_ge(z_done, ct + 1)
                dve.sem_inc(s1_used, 1)

            def pv_half(half):
                if half == 0:
                    dve.wait_ge(aux_full, A_U + T)
                table(pv[:], T, bb_r[:], bb_i[:], half, 1)

            pv_half(0)
            conv_cc(Q_CONV0, 0, 0, 0)
            pv_half(1)
            dve.sem_inc(pv_ready, 1)
            conv_bc(Q_CONV0, 0, 0, 0)

            for b in range(1, G // 4, 2):
                use = A_W + b
                dve.wait_ge(aux_full, use + 1)
                V.tensor_copy(flat(w_in_state[:, 4 * b:4 * b + 4, :]), aux[:, use % 4, :]).then_inc(aux_free[use % 4], 1)
            for b in range(1, G // 4, 2):
                use = A_UT + b
                dve.wait_ge(aux_full, use + 1)
                V.tensor_copy(flat(u_chunk[:, 4 * b:4 * b + 4, :]), aux[:, use % 4, :]).then_inc(aux_free[use % 4], 1)
            for b in range(1, G // 4, 2):
                use = A_K + b
                dve.wait_ge(aux_full, use + 1)
                V.tensor_copy(flat(kern[:, 4 * b:4 * b + 4, :]), aux[0:GC, use % 4, :]).then_inc(aux_free[use % 4], 1)
            for i in range(4):
                uses = [u for u in range(A_K, A_K + G // 4) if u % 4 == i]
                dve.wait_ge(aux_free[i], uses[-1] // 4 + 1)
            diag = ident[0:GC, 0:GC].unsqueeze(1).to_broadcast([GC, G, GC])
            dk = d_diag[:]
            tt(dk, diag, d_hg[:].unsqueeze(2).to_broadcast([GC, G, GC]), ALU.mult)
            link(V.tensor_tensor(kern[:, :, 0:GC], kern[:, :, 0:GC], dk, ALU.add))
            dve.sem_inc(kern_ready, 1)
            for b in range(1, G // 4, 2):
                use = A_WC + b
                dve.wait_ge(aux_full, use + 1)
                V.tensor_copy(flat(w_c[N_STATE:P, b // 2, 0]), aux[0:N_STATE, use % 4, :])
                V.tensor_copy(flat(w_c[N_STATE:P, b // 2, 1]), aux[N_STATE:P, use % 4, :]).then_inc(aux_free[use % 4], 1)
            dve.wait_ge(aux_full, A_WC + G // 4)
            V.memset(toep[:], 0.0).then_inc(toep_zero, 1)
            for i in range(4):
                uses = [u for u in range(A_WC, A_WC + G // 4) if u % 4 == i]
                dve.wait_ge(aux_free[i], uses[-1] // 4 + 1)
            dve.wait_ge(toep_ready, 16 * T)

            local = [0]

            def turns(q, half):
                prs = bass.ds(8 * half, 8)
                V.memset(turn_r[:, :, 0:1], 1.0)
                V.memset(turn_i[:, :, 0:1], 0.0)
                V.tensor_copy(turn_r[:, :, 1:2], turn1_r[:, prs].unsqueeze(2))
                slink(q, V.tensor_copy(turn_i[:, :, 1:2], turn1_i[:, prs].unsqueeze(2)))
                m = 1
                while m < C:
                    uu = q1q2[:, 0:8 * m].rearrange("p (a b) -> p a b", b=m)
                    vv = q3q4[:, 0:8 * m].rearrange("p (a b) -> p a b", b=m)
                    lo_, hi_ = slice(1, m + 1), slice(m + 1, 2 * m + 1)
                    b0, b1 = (w[:, :, m:m + 1].to_broadcast([P, 8, m]) for w in (turn_r, turn_i))
                    V.tensor_tensor(uu, turn_r[:, :, lo_], b0, ALU.mult)
                    slink(q, V.tensor_tensor(vv, turn_i[:, :, lo_], b1, ALU.mult))
                    slink(q, V.tensor_tensor(turn_r[:, :, hi_], uu, vv, ALU.subtract))
                    V.tensor_tensor(uu, turn_r[:, :, lo_], b1, ALU.mult)
                    slink(q, V.tensor_tensor(vv, turn_i[:, :, lo_], b0, ALU.mult))
                    slink(q, V.tensor_tensor(turn_i[:, :, hi_], uu, vv, ALU.add))
                    m *= 2

            def slink(q, ins):
                local[0] += 1
                ins.then_inc(scan_step, 1)
                dve.wait_ge(scan_step, (q - Q_CONV1) * PER_TURN + local[0])

            PER_TURN = 1 + 7 * 4 + 2 * 7

            def scan_block(q, half, b):
                qd = 2 * half + b
                wr, wi = (w_c[:, bass.ds(qd, 1), r].rearrange("p q a c -> p (q a) c") for r in range(2))
                ps = slice(4 * b, 4 * b + 4)
                er, ei = turn_r[:, ps, 1:C + 1], turn_i[:, ps, 1:C + 1]
                V.tensor_tensor(q1[:], er, wr, ALU.mult)
                V.tensor_tensor(q2[:], ei, wi, ALU.mult)
                V.tensor_tensor(q3[:], er, wi, ALU.mult)
                slink(q, V.tensor_tensor(q4[:], ei, wr, ALU.mult))
                V.tensor_tensor(q1[:], q1[:], q2[:], ALU.add)
                slink(q, V.tensor_tensor(q3[:], q3[:], q4[:], ALU.subtract))
                for src, dst in ((q1, q2), (q3, q4)):
                    for a in range(4):
                        last = V.tensor_tensor_scan(dst[:, a, :],
                                                    mag8[:, bass.ds(4 * qd + a, 1)].to_broadcast([P, C]),
                                                    src[:, a, :], 0.0, ALU.mult, ALU.add)
                slink(q, last)
                er, ei = turn_r[:, ps, 1:C], turn_i[:, ps, 1:C]
                zr, zi = q2[:, :, 0:C - 1], q4[:, :, 0:C - 1]
                o1, o3 = q1[:, :, 0:C - 1], q3[:, :, 0:C - 1]
                for ri in range(2):
                    V.tensor_tensor(o1, er, zr if ri == 0 else zi, ALU.mult)
                    slink(q, V.tensor_tensor(o3, ei, zi if ri == 0 else zr, ALU.mult))
                    for par in range(2):
                        rows = slice(par * N_STATE, (par + 1) * N_STATE)
                        dst = state[ri * N_STATE:(ri + 1) * N_STATE, bass.ds(qd, 1), :, :].rearrange(
                            "s q (a b) c -> s (q a) b c", b=2)[:, :, par, :]
                        last = V.tensor_tensor(dst[:, :, 1:C], o1[rows], o3[rows],
                                               ALU.subtract if ri == 0 else ALU.add)
                        last = V.tensor_copy(dst[:, :, 0:1], v_pad[rows, 0:1].unsqueeze(1).to_broadcast([N_STATE, 4, 1]))
                    slink(q, last)
                dve.sem_inc(state_ready, 1)

            with dve.Fori(Q_CONV1, Q_GSSM) as q:
                half = q - Q_CONV1
                w, chain = 2 * q, 4 * q
                turns(q, half)
                scan_block(q, half, 0)
                conv_cc(q, q, w, chain)
                scan_block(q, half, 1)
                conv_bc(q, q, w, chain)
            assert local[0] == PER_TURN, local[0]

            for b in range(1, G // 4, 2):
                use = A_Y + b
                dve.wait_ge(aux_full, use + 1)
                V.tensor_copy(y_nat[:, :, 4 * b * GC:4 * (b + 1) * GC].rearrange("c j (g h) -> c g j h", h=GC),
                              aux[:, use % 4, :].rearrange("c (g j h) -> c g j h", g=4, h=GC)
                              ).then_inc(aux_free[use % 4], 1)

            def y_split(ct, src, n):
                dve.wait_ge(y_hi_ready, n)
                V.tensor_tensor(y_lo[:, ct, :], src[:, ct, :], y_hi[:, ct, :].bitcast(f32),
                                ALU.subtract).then_inc(y_ready, 1)

            for ct in range(KS):
                y_split(ct, y_f, ct + 1)
            for c in range(4):
                dve.wait_ge(s1_full, 7 + c)
                tt(s1[:], s1[:], y_f[:, c, :], ALU.mult)
                tt(y_g[:, c, :], s1[:], y_g[:, c, :], ALU.mult)
                dve.sem_inc(s1_used, 1)
            dve.wait_ge(tile_done, 4 * Q_GLU + 4)
            dve.sem_inc(y2_ready, KS)
            for ct in range(KS):
                y_split(ct, y_g, KS + ct + 1)

            conv_cc(Q_CONV3, 3, 10, 12)
            conv_bc(Q_CONV3, 3, 10, 12)

            with dve.Fori(Q_YA, Q_CONV4) as q:
                for c in (1, 3):
                    n = 4 * q + c
                    d = 2 * q + (c // 2 - 2 * Q_YA)
                    dve.wait_ge(s1_full, d + 13)
                    dve.wait_ge(tile_done, n + 1)
                    V.tensor_tensor(yam[:, bass.ds(d, 1), :].rearrange("p a l -> p (a l)"), flat(slot_ps(1)), s1[:],
                                    ALU.mult).then_inc(s1_used, 1)
                    dve.wait_ge(s1_used, d + 13)
                    dve.sem_inc(slot_free[1], 1)
            with dve.Fori(Q_CONV4, Q_RC) as q:
                ct = q - (Q_CONV4 - 4)
                conv_cc(q, ct, 2 * q + (20 - 2 * Q_CONV4), 4 * q + (16 - 4 * Q_CONV4))
                conv_bc(q, ct, 2 * q + (20 - 2 * Q_CONV4), 4 * q + (16 - 4 * Q_CONV4))

            for k in range(KD):
                dve.wait_ge(z_hi_ready, k + 1)
                V.tensor_tensor(big_lo[:, k, :], z[:, k, :], big_hi[:, k, :].bitcast(f32),
                                ALU.subtract).then_inc(z_ready, 1)

            with dve.Fori(Q_YB, Q_END) as q:
                for c in range(4):
                    n = 4 * q + c
                    d = 4 * q + (c - 4 * Q_YB)
                    row = lambda ap: ap[:, bass.ds(d, 1), :].rearrange("p a l -> p (a l)")
                    dve.wait_ge(tile_done, n + 1)
                    V.tensor_tensor(s1[:], flat(slot_ps(c % 2)), row(rc_gate), ALU.mult).then_inc(slot_free[c % 2], 1)
                    dve.wait_ge(slot_free[c % 2], 2 * q + (c // 2 + 1))
                    V.tensor_tensor(row(yam), row(yam), s1[:], ALU.add).then_inc(sum_ready, 1)
                    dve.wait_ge(mx_hi_ready, d + 1)
                    V.tensor_tensor(row(mx_lo), row(yam), row(mx_hi).bitcast(f32), ALU.subtract).then_inc(mx_ready, 1)
                    dve.wait_ge(mx_ready, d + 1)

            def big_lo_part(k, index):
                dve.wait_ge(wb_hi_ready, index * KD + k + 1)
                V.tensor_tensor(big_lo[:, k, :], wb_raw[k % RS][:], big_hi[:, k, :].bitcast(f32),
                                ALU.subtract).then_inc(wb_ready, 1)

            for k in range(KD):
                big_lo_part(k, 0)

            def x1_lo(lt):
                for half in range(2):
                    use = a_x1(lt, half)
                    dve.wait_ge(x1_hi_ready, 2 * lt + half + 1)
                    ks = slice(4 * half, 4 * half + 4)
                    ls = slice(lt * P, (lt + 1) * P)
                    V.tensor_tensor(mx_lo[:, ks, ls], aux[:, use % 4, :].rearrange("p (k l) -> p k l", l=P),
                                    mx_hi[:, ks, ls].bitcast(f32), ALU.subtract).then_inc(x1_split, 1)
                    dve.wait_ge(x1_split, 2 * lt + half + 1)
                    dve.sem_inc(aux_free[use % 4], 1)

            dve.wait_ge(rows_loaded, 32)
            for lt in range(LT):
                j = LT + lt
                dve.wait_ge(squares_done, LT + lt + 1)
                inverse(j, j + 1, 2 + lt)
                refine(j, j + 1, 2 + lt + 1)
                stt(x1[lt % 2][:], flat(slot_ps(lt % 2)), rstd[:, j:j + 1], post_row[:], ALU.mult, ALU.mult)
                dve.sem_inc(slot_free[lt % 2], 1)
                dve.wait_ge(x_in_full[lt % 2], 16 * (lt // 2 + 1))
                V.tensor_tensor(x1[lt % 2][:], x1[lt % 2][:], x_in[lt % 2][:], ALU.add).then_inc(x1_ready, 1)
                if lt == P_AT - 1:
                    dve.wait_ge(wp_hi_ready, 1)
                    V.tensor_tensor(wp_lo[:], wp_raw[:], wp_hi[:].bitcast(f32), ALU.subtract).then_inc(wp_ready, 1)
                if lt == P_AT:
                    for u in range(2 * KP):
                        use = A_PT + u
                        cols = slice((u % 2) * HALF, (u % 2 + 1) * HALF)
                        dve.wait_ge(pt_hi_ready, u + 1)
                        V.tensor_tensor(pt_lo[:, u // 2, cols], aux[:, use % 4, :],
                                        pt_hi[:, u // 2, cols].bitcast(f32), ALU.subtract).then_inc(pt_ready, 1)
                        dve.wait_ge(pt_ready, u + 1)
                        dve.sem_inc(aux_free[use % 4], 1)
                if lt >= 1:
                    x1_lo(lt - 1)
            for k in range(KD):
                big_lo_part(k, 1)
                if k == 3:
                    x1_lo(LT - 1)

            for lt in range(LT):
                j = 2 * LT + lt
                b0 = (A_E + 2 * lt) % 4
                dve.wait_ge(sig_ready, lt + 1)
                dve.wait_ge(aux_full, A_E + 2 * lt + 2)
                if lt >= 2:
                    dve.wait_ge(out_stored[lt % 2], 16 * (lt // 2))
                else:
                    dve.wait_ge(x1_stored[lt % 2], 16 * (LT // 2))
                V.tensor_tensor(x1[lt % 2][:], flat(aux[:, b0:b0 + 2, :]), sig_row[:], ALU.mult).then_inc(e_ready, 1)
                dve.wait_ge(e_ready, lt + 1)
                dve.sem_inc(aux_free[b0], 1)
                dve.sem_inc(aux_free[b0 + 1], 1)
                dve.wait_ge(esq_done, lt + 1)
                inverse(j, j + 1, 0)
                refine(j, j + 1, 2 + LT + lt + 1)
                stt(x1[lt % 2][:], x1[lt % 2][:], rstd[:, j:j + 1], ple_row[:], ALU.mult, ALU.mult)
                dve.wait_ge(x_in_full[lt % 2], 16 * ((LT + lt) // 2 + 1))
                V.tensor_tensor(x1[lt % 2][:], x1[lt % 2][:], x_in[lt % 2][:], ALU.add).then_inc(out_ready, 1)

        @block.tensor
        def _(pe):
            M = nc.tensor

            def bank(use):
                if use >= 4:
                    pe.wait_ge(aux_free[use % 4], use // 4)
                return aux[:, use % 4, :]

            pe.wait_ge(ident_ready, 2)
            pe.wait_ge(params_loaded, 16 * 15)
            for ri in range(2):
                o = bank(A_C + ri)
                for f in range(4):
                    last = M.transpose(o[:, f * P:(f + 1) * P], c_nat[:, ri, f, :], ident[:])
                last.then_inc(aux_full, 1)
            for half in range(2):
                pe.wait_ge(xn_ready, 4 * half + 4)
                for k in range(KD):
                    o = bank(A_H + half * KD + k)
                    for i in range(4):
                        last = M.transpose(o[:, i * P:(i + 1) * P],
                                           x_tile[4 * half + i][:, k * P:(k + 1) * P], ident[:])
                    last.then_inc(aux_full, 1)

            def three(o, s_hi, s_lo, m_hi, m_lo, first, last):
                M.matmul(o, s_hi, m_hi, start=first, stop=False)
                M.matmul(o, s_hi, m_lo, start=False, stop=False)
                return M.matmul(o, s_lo, m_hi, start=False, stop=last)

            for i in range(4):
                uses = [u for u in range(A_H, A_H + 2 * KD) if u % 4 == i]
                pe.wait_ge(aux_free[i], uses[-1] // 4 + 1)
            pe.wait_ge(wu_ready, 1)
            h_pos = [w[:].rearrange("p k (c j) -> p k j c", j=T) for w in (big_hi, big_lo)]
            for j in range(T):
                o = bank(A_U + j)
                for k in range(KD):
                    last = three(o, h_pos[0][:, k, j, :], h_pos[1][:, k, j, :], wu_hi[:, k, :], wu_lo[:, k, :],
                                 k == 0, k == KD - 1)
                last.then_inc(aux_full, 1)

            def quad(q, moving=None, kks=(KD,) * 4, first=False):
                for c in range(4):
                    m_hi, m_lo = (moving or {}).get(c, (big_hi, big_lo))
                    pe_tile(q, c, kks[c], m_hi, m_lo, first and c < 2)

            def pe_tile(q, c, kk, m_hi, m_lo, first):
                pe.wait_ge(w_ready, 4 * q + c + 1)
                if not first:
                    pe.wait_ge(slot_free[c % 2], 2 * q + c // 2)
                for half in range(2):
                    cols = slice(half * HALF, (half + 1) * HALF)
                    for k in range(kk):
                        last = three(slot_ps(c % 2)[:, half, :], w_hi[c % 2][:, k, :], w_lo[c % 2][:, k, :],
                                     m_hi[:, k, cols], m_lo[:, k, cols], k == 0, k == kk - 1)
                last.then_inc(tile_done, 1)

            quad(Q_CONV0, first=True)

            pe.wait_ge(pv_ready, 1)
            for b in range(G // 4):
                o = bank(A_W + b)
                for i in range(4):
                    last = M.transpose(o[:, i * P:(i + 1) * P], pv[:, 4 * b + i, :], ident[:])
                last.then_inc(aux_full, 1)
            for b in range(G // 4):
                o = bank(A_UT + b)
                for i in range(4):
                    last = M.transpose(o[:, i * P:(i + 1) * P],
                                       u_nat[:, 4 * b + i].rearrange("c m h -> c (m h)"), ident[:])
                last.then_inc(aux_full, 1)
            for b in range(G // 4):
                o = bank(A_K + b)
                for i in range(4):
                    g = 4 * b + i
                    last = M.matmul(o[0:GC, i * P:(i + 1) * P], bb_stack[:, g, :],
                                    ca[:, g, 0:T, :].rearrange("p n h -> p (n h)"), start=True, stop=True)
                last.then_inc(aux_full, 1)
            for i in range(4):
                uses = [u for u in range(A_W, A_K) if u % 4 == i]
                pe.wait_ge(aux_free[i], uses[-1] // 4 + 1)
            for b in range(G // 4):
                o = bank(A_WC + b)
                for i in range(4):
                    g = 2 * (4 * (b // 2) + i) + b % 2
                    last = M.matmul(o[:, i * P:(i + 1) * P], w_in_state[:, g, :], u_chunk[:, g, :],
                                    start=True, stop=True)
                last.then_inc(aux_full, 1)

            with pe.Fori(Q_CONV1, Q_GSSM) as q:
                quad(q)

            pe.wait_ge(state_ready, 4)
            pe.wait_ge(toep_ready, 16 * T)
            for b in range(G // 4):
                o = bank(A_Y + b)
                for i in range(4):
                    g = 4 * b + i
                    s = slice(i * P, (i + 1) * P)
                    M.matmul(o[:, s], u_chunk[:, g, :], toep[:, g, :], start=True, stop=False)
                    last = M.matmul(o[:, s], state[:, g // 8, g % 8, :],
                                    ca[:, g, 1:NP, :].rearrange("p n h -> p (n h)"), start=False, stop=True)
                last.then_inc(aux_full, 1)
            for i in range(4):
                uses = [u for u in range(A_Y, A_YT) if u % 4 == i]
                pe.wait_ge(aux_free[i], uses[-1] // 4 + 1)
            for ct in range(KS):
                for jb in range(2):
                    o = bank(A_YT + 2 * ct + jb)
                    for i in range(4):
                        last = M.transpose(o[:, i * P:(i + 1) * P], y_nat[:, 4 * jb + i, ct * P:(ct + 1) * P],
                                           ident[:])
                    last.then_inc(aux_full, 1)

            quad(Q_GSSM)
            pe.wait_ge(y_ready, KS)
            y_mov = {c: (y_hi, y_lo) for c in range(4)}
            quad(Q_GLU, y_mov, (KS,) * 4)
            quad(Q_CONV3)
            pe.wait_ge(y_ready, 2 * KS)
            with pe.Fori(Q_YA, Q_CONV4) as q:
                quad(q, {1: (y_hi, y_lo), 3: (y_hi, y_lo)}, (KD, KS, KD, KS))
            with pe.Fori(Q_CONV4, Q_YB) as q:
                quad(q)
            pe.wait_ge(z_ready, KD)
            with pe.Fori(Q_YB, Q_END) as q:
                quad(q)

            def transposes_x1(lt):
                pe.wait_ge(x1_ready, lt + 1)
                for half in range(2):
                    o = bank(a_x1(lt, half))
                    for i in range(4):
                        k = 4 * half + i
                        last = M.transpose(o[:, i * P:(i + 1) * P], x1[lt % 2][:, k * P:(k + 1) * P], ident[:])
                    last.then_inc(aux_full, 1)

            def row_tile(lt, base, index):
                pe.wait_ge(slot_free[lt % 2], (4 * Q_END + base + lt) // 2)
                ls = slice(lt * P, (lt + 1) * P)
                for k in range(KD):
                    if lt == 0:
                        pe.wait_ge(wb_ready, index * KD + k + 1)
                    for half in range(2):
                        cols = slice(half * HALF, (half + 1) * HALF)
                        last = three(slot_ps(lt % 2)[:, half, :], mx_hi[:, k, ls], mx_lo[:, k, ls],
                                     big_hi[:, k, cols], big_lo[:, k, cols], k == 0, k == KD - 1)
                last.then_inc(tile_done, 1)

            pe.wait_ge(mx_ready, KD)
            for lt in range(LT):
                if lt == P_AT:
                    pe.wait_ge(ple_in, 32)
                    for u in range(2 * KP):
                        o = bank(A_PT + u)
                        for i in range(4):
                            last = M.transpose(o[:, i * P:(i + 1) * P],
                                               p_nat[:, 4 * (u % 2) + i, (u // 2) * P:(u // 2 + 1) * P], ident[:])
                        last.then_inc(aux_full, 1)
                row_tile(lt, 0, 0)
                if lt >= 1:
                    transposes_x1(lt - 1)

            def e_tile(lt):
                ls = slice(lt * P, (lt + 1) * P)
                for half in range(2):
                    o = bank(A_E + 2 * lt + half)
                    cols = slice(half * HALF, (half + 1) * HALF)
                    for k in range(KP):
                        last = three(o, pt_hi[:, k, ls], pt_lo[:, k, ls], wp_hi[:, k, cols], wp_lo[:, k, cols],
                                     k == 0, k == KP - 1)
                    last.then_inc(aux_full, 1)

            transposes_x1(LT - 1)
            pe.wait_ge(pt_ready, 2 * KP)
            pe.wait_ge(wp_ready, 1)
            for lt in range(LT):
                e_tile(lt)
                pe.wait_ge(x1_split, 2 * lt + 2)
                row_tile(lt, LT, 1)


def kernel(**inputs):
    import numpy as np
    import concourse.bacc as bacc
    from concourse import mybir
    from concourse.bass_utils import run_bass_kernel_spmd as run

    nc = bacc.Bacc("TRN2", target_bir_lowering=False, num_devices=1)
    names = ["x", "p", "pre_norm", "w_in", "a_re", "a_im", "log_step", "b_re", "b_im", "c_re", "c_im", "d_skip",
             "w_glu", "b_glu", "w_ssm_out", "conv_w", "w_conv_out", "w_o", "post_norm", "w_ple", "w_ple_gate",
             "ple_norm"]
    arrays, args = {}, []
    for name in names:
        a = np.ascontiguousarray(inputs[name])
        arrays[f"in_{name}"] = a
        args.append(nc.dram_tensor(f"in_{name}", a.shape, mybir.dt.from_np(a.dtype), kind="ExternalInput").ap())
    shape = inputs["x"].shape
    args.append(nc.dram_tensor("out_x", shape, mybir.dt.float32, kind="ExternalOutput").ap())
    build_block(nc, *args)
    return run(nc, [arrays], core_ids=[0]).results[0]["out_x"]
```

```python
def build_block(nc, x, p, pre_norm, w_in, a_re, a_im, log_step, b_re, b_im, c_re, c_im, d_skip,
                w_glu, b_glu, w_ssm_out, conv_w, w_conv_out, w_o, post_norm, w_ple, w_ple_gate,
                ple_norm, out):
    import math
    from contextlib import ExitStack
    import concourse.bass as bass
    from concourse import mybir

    f32, f32r, i32 = mybir.dt.float32, mybir.dt.float32r, mybir.dt.int32
    ALU = mybir.AluOpType
    ACT = mybir.ActivationFunctionType

    P = 128
    L, D = x.shape[1], x.shape[2]
    SSM_W = w_glu.shape[1]
    G, N_STATE, GC = b_re.shape[1], b_re.shape[2], b_re.shape[3]
    PLE = p.shape[3]
    KD, KS, KP, LT = D // P, SSM_W // P, PLE // P, L // P
    HALF = 512
    T = P // GC
    C = L // T
    PAIRS = G // 2
    NP = T + 1
    EPS = 1e-6
    COL_G, COL_XC = SSM_W, 2 * SSM_W
    COL_BC, COL_CC, COL_GC = COL_XC + D, COL_XC + 2 * D, COL_XC + 3 * D
    COL_RS, COL_RC = COL_XC + 4 * D, COL_XC + 5 * D

    Q_CONV0, Q_CONV1, Q_GSSM, Q_GLU, Q_CONV3, Q_YA, Q_CONV4, Q_RC, Q_YB, Q_END = 0, 1, 3, 4, 5, 6, 10, 14, 16, 18

    ctx = ExitStack()
    with ctx:
        KB = 1024
        arena = ctx.enter_context(nc.sbuf_tensor("arena", [P, 207 * 256], f32))
        BASE = 16512

        def at(name, kb, shape, dt=f32):
            return nc.alloc_sbuf_tensor_at(name, shape, dt, offset=BASE + int(kb * KB))

        w_raw = [at(f"w_raw{i}", 4 * i, [P, KD, P]) for i in range(4)]
        w_hi = [at(f"w_hi{i}", 16 + 4 * i, [P, KD, P], f32r) for i in range(2)]
        w_lo = [at(f"w_lo{i}", 24 + 4 * i, [P, KD, P], f32r) for i in range(2)]
        big_hi = at("big_hi", 32, [P, KD, L], f32r)
        big_lo = at("big_lo", 64, [P, KD, L], f32r)
        z = at("z", 96, [P, KD, L])
        yam = at("yam", 128, [P, KD, L])
        rc_gate = at("rc_gate", 160, [P, KD, L])
        mx_hi = at("mx_hi", 96, [P, KD, L], f32r)
        mx_lo = at("mx_lo", 160, [P, KD, L], f32r)
        x_tile = [at(f"x_tile{i}", (174 if i < 4 else 124 - 16) + 4 * i, [P, D]) for i in range(LT)]
        sq_junk = at("sq_junk", 96, [P, D])
        wu_raw = at("wu_raw", 0, [P, KD // 2, SSM_W])
        wu_raw2 = at("wu_raw2", 16, [P, KD // 2, SSM_W])
        wu_hi = at("wu_hi", 158, [P, KD, SSM_W], f32r)
        wu_lo = at("wu_lo", 142, [P, KD, SSM_W], f32r)
        u_nat = at("u_nat", 174, [P, G, T, GC])
        u_chunk = at("u_chunk", 108, [P, G, C])
        ca = at("ca", 124, [P, G, NP, GC])
        pv = at("pv", 142, [P, G, T * GC])
        w_in_state = at("w_in_state", 158, [P, G, P])
        toep = at("toep", 158, [P, G, T * GC])
        kern = at("kern", 174, [GC, G, T * GC])
        w_c = at("w_c", 142, [P, 4, 2, 4, C])
        state = at("state", 142, [P, 4, 8, C])
        turn_r = at("turn_r", 174, [P, 8, C + 1])
        turn_i = at("turn_i", 174 + 4.03125, [P, 8, C + 1])
        q1, q2, q3, q4 = (at(f"q{i}", 182.0625 + 2 * i, [P, 4, C]) for i in range(4))
        q1q2 = at("q1q2", 182.0625, [P, 8 * C])
        q3q4 = at("q3q4", 186.0625, [P, 8 * C])
        d_diag = at("d_diag", 100, [GC, G, GC])
        y_nat = at("y_nat", 174, [P, T, SSM_W])
        y_f = at("y_f", 144, [P, KS, L])
        y_g = at("y_g", 128, [P, KS, L])
        y_hi = at("y_hi", 160, [P, KS, L], f32r)
        y_lo = at("y_lo", 176, [P, KS, L], f32r)
        small = at("small", 100, [P, 44, PAIRS])
        b_r = at("b_r", 103, [P, PAIRS, GC])
        b_i = at("b_i", 104, [P, PAIRS, GC])
        bb_stack = at("bb_stack", 103, [P, G, GC])
        c_nat = at("c_nat", 105, [P, 2, 4, P])
        bb_r = at("bb_r", 105, [P, PAIRS, GC])
        bb_i = at("bb_i", 106, [P, PAIRS, GC])
        c_t = at("c_t", 119, [P, 2, PAIRS, GC])
        t1 = at("t1", 108, [P, 8, NP * GC])
        t2 = at("t2", 112.5, [P, 8, NP * GC])
        pw_r = at("pw_r", 190.25, [P, PAIRS, NP])
        pw_i = at("pw_i", 190.8125, [P, PAIRS, NP])
        turn1_r = at("turn1_r", 191.375, [P, PAIRS])
        turn1_i = at("turn1_i", 191.4375, [P, PAIRS])
        mag8 = at("mag8", 191.5, [P, PAIRS])
        d_hg = at("d_hg", 191.5625, [GC, G])
        s1 = at("s1", 192, [P, L])
        v_pad = at("v_pad", 196, [P, L + 2])
        cv = at("cv", 200.0625, [P, L])
        ident = at("ident", 204.0625, [P, P])
        gain_pre = at("gain_pre", 204.5625, [P, KD])
        cw = at("cw", 204.625, [P, 3, KD])
        bg = at("bg", 204.75, [P, KS])
        ssq = at("ssq", 204.8125, [P, 3 * LT])
        va = at("va", 204.9375, [P, 3 * LT])
        vb = at("vb", 205.0625, [P, 3 * LT])
        rstd = at("rstd", 205.3125, [P, 3 * LT])
        RS = 5
        wb_raw = [at(f"wb_raw{i}", 128 + 4 * i, [P, D]) for i in range(RS)]
        p_nat = at("p_nat", 128, [P, LT, PLE])
        wp_raw = at("wp_raw", 136, [P, KP, D])
        x_in = [at(f"x_in{i}", 148 + 4 * i, [P, D]) for i in range(2)]
        x1 = [at("x1a", 156, [P, D]), at("x1b", 192, [P, D])]
        post_row = at("post_row", 196, [P, D])
        sig_row = at("sig_row", 196, [P, D])
        ple_row = at("ple_row", 200, [P, D])
        pt_hi = at("pt_hi", 0, [P, KP, L], f32r)
        pt_lo = at("pt_lo", 8, [P, KP, L], f32r)
        wp_hi = at("wp_hi", 16, [P, KP, D], f32r)
        wp_lo = at("wp_lo", 24, [P, KP, D], f32r)

        tile_ps = ctx.enter_context(nc.psum_tensor("tile_ps", [P, 4, HALF], f32))
        aux = ctx.enter_context(nc.psum_tensor("aux", [P, 4, HALF], f32))
        x1_dram = nc.dram_tensor("x1_dram", (L, D), f32, kind="Internal").ap()

        def slot_ps(s):
            return tile_ps[:, 2 * s:2 * s + 2, :]

        def flat(ap):
            return ap.rearrange("p a b -> p (a b)")

        def sem(name):
            return ctx.enter_context(nc.semaphore(name))

        x_loaded = [sem(f"x_loaded{i}") for i in range(LT)]
        wu_loaded = [sem("wu_loaded0"), sem("wu_loaded1")]
        consts_loaded = sem("consts_loaded")
        params_loaded = sem("params_loaded")
        ident_ready = sem("ident_ready")
        squares_done = sem("squares_done")
        xn_ready = sem("xn_ready")
        h_hi_ready = sem("h_hi_ready")
        h_ready = sem("h_ready")
        wu_hi_ready = sem("wu_hi_ready")
        wu_ready = sem("wu_ready")
        aux_full = sem("aux_full")
        aux_free = [sem(f"aux_free{i}") for i in range(4)]
        raw_full = [sem(f"raw_full{i}") for i in range(4)]
        w_hi_ready = sem("w_hi_ready")
        w_ready = sem("w_ready")
        tile_done = sem("tile_done")
        slot_free = [sem("slot_free0"), sem("slot_free1")]
        s1_full = sem("s1_full")
        s1_used = sem("s1_used")
        dve_chain = sem("dve_chain")
        conv_step = sem("conv_step")
        scan_step = sem("scan_step")
        pv_ready = sem("pv_ready")
        toep_zero = sem("toep_zero")
        kern_ready = sem("kern_ready")
        toep_ready = sem("toep_ready")
        state_ready = sem("state_ready")
        gelu_ready = sem("gelu_ready")
        y_hi_ready = sem("y_hi_ready")
        y_ready = sem("y_ready")
        gssm_ready = sem("gssm_ready")
        y2_ready = sem("y2_ready")
        z_done = sem("z_done")
        z_hi_ready = sem("z_hi_ready")
        z_ready = sem("z_ready")
        rc_ready = sem("rc_ready")
        sum_ready = sem("sum_ready")
        mx_hi_ready = sem("mx_hi_ready")
        mx_ready = sem("mx_ready")
        wb_full = [sem(f"wb_full{i}") for i in range(RS)]
        wb_hi_ready = sem("wb_hi_ready")
        wb_ready_v = sem("wb_ready_v")
        wb_ready_p = sem("wb_ready_p")
        ple_in = sem("ple_in")
        wp_hi_ready = sem("wp_hi_ready")
        wp_ready = sem("wp_ready")
        pt_hi_ready = sem("pt_hi_ready")
        pt_ready = sem("pt_ready")
        x_in_full = [sem("x_in_full0"), sem("x_in_full1")]
        rows_loaded = sem("rows_loaded")
        o_ready = sem("o_ready")
        x1_ready = sem("x1_ready")
        x1_stored = [sem("x1_stored0"), sem("x1_stored1")]
        x1_hi_ready = sem("x1_hi_ready")
        x1_split = sem("x1_split")
        sig_ready = sem("sig_ready")
        e_ready = sem("e_ready")
        esq_done = sem("esq_done")
        out_ready = sem("out_ready")
        out_stored = [sem("out_stored0"), sem("out_stored1")]

        BIG_LO_V, BIG_LO_P = (0, 2, 3, 5, 6), (1, 4, 7)

        def wait_big_lo(engine, k, index):
            if k in BIG_LO_V:
                engine.wait_ge(wb_ready_v, index * len(BIG_LO_V) + BIG_LO_V.index(k) + 1)
            else:
                engine.wait_ge(wb_ready_p, index * len(BIG_LO_P) + BIG_LO_P.index(k) + 1)

        A_H = 0
        A_C = A_H + 2 * KD
        A_U = A_C + 2
        A_W = A_U + T
        A_UT = A_W + G // 4
        A_K = A_UT + G // 4
        A_WC = A_K + G // 4
        A_Y = A_WC + G // 4
        A_YT = A_Y + G // 4
        PAIR_ORDER = (["x1", "x1", "p", "x1", "p"] + ["x1"] * (LT - 4) + ["e", "x1"] + ["e"] * (LT - 1))
        P_AT = 3
        A_PAIR = A_YT + 2 * KS

        def pair_use(kind, n):
            at_pair = [i for i, what in enumerate(PAIR_ORDER) if what == kind][n]
            return A_PAIR + 2 * at_pair

        block = ctx.enter_context(nc.Block())

        @block.sync
        def _(sp):
            for i in range(4):
                sp.dma_start(x_tile[i][:], x[0, i * P:(i + 1) * P, :]).then_inc(x_loaded[i], 16)
            wu_view = w_in[0].rearrange("(k p) e -> p k e", p=P)
            for i in range(4, LT):
                sp.dma_start(x_tile[i][:], x[0, i * P:(i + 1) * P, :]).then_inc(x_loaded[i], 16)
            sp.dma_start(wu_raw[:], wu_view[:, 0:KD // 2, 0:SSM_W]).then_inc(wu_loaded[0], 16)
            sp.dma_start(wu_raw2[:], wu_view[:, KD // 2:KD, 0:SSM_W]).then_inc(wu_loaded[1], 16)

            def load_tile(n_is_first, n, c, weights, col, kk):
                if n_is_first:
                    sp.wait_ge(wu_ready, 2)
                else:
                    sp.wait_ge(w_ready, n - 3)
                src = weights.rearrange("(k p) e -> p k e", p=P)
                sp.dma_start(w_raw[c][:, 0:kk, :], src[:, :, bass.ds(col, P)]).then_inc(raw_full[c], 16)

            def load_conv(q, ct, first=False):
                for c, col in enumerate((COL_XC, COL_CC, COL_GC, COL_BC)):
                    load_tile(first, 4 * q + c, c, w_in[0], col + ct * P, KD)

            load_conv(Q_CONV0, 0, first=True)
            with sp.Fori(Q_CONV1, Q_GSSM) as q:
                load_conv(q, q)
            for c in range(4):
                load_tile(False, 4 * Q_GSSM + c, c, w_in[0], COL_G + c * P, KD)
            for c in range(4):
                load_tile(False, 4 * Q_GLU + c, c, w_glu[0], c * P, KS)
            load_conv(Q_CONV3, 3)
            with sp.Fori(Q_YA, Q_CONV4) as q:
                for c in range(4):
                    d = 2 * q + (c // 2 - 2 * Q_YA)
                    if c % 2 == 0:
                        load_tile(False, 4 * q + c, c, w_in[0], COL_RS + d * P, KD)
                    else:
                        load_tile(False, 4 * q + c, c, w_ssm_out[0], q * (2 * P) + (c // 2 - 2 * Q_YA) * P, KS)
            with sp.Fori(Q_CONV4, Q_RC) as q:
                load_conv(q, q - (Q_CONV4 - 4))
            with sp.Fori(Q_RC, Q_YB) as q:
                for c in range(4):
                    load_tile(False, 4 * q + c, c, w_in[0], COL_RC - 4 * Q_RC * P + c * P + q * 4 * P, KD)
            with sp.Fori(Q_YB, Q_END) as q:
                for c in range(4):
                    load_tile(False, 4 * q + c, c, w_conv_out[0], q * 4 * P + (c - 4 * Q_YB) * P, KD)

            sp.wait_ge(z_done, KD)
            sp.dma_start(post_row[:], post_norm[0].partition_broadcast(P)).then_inc(rows_loaded, 16)
            sp.dma_start(ple_row[:], ple_norm[0].partition_broadcast(P)).then_inc(rows_loaded, 16)

            def load_big(k, weights):
                sp.dma_start(wb_raw[k % RS][:], weights[k * P:(k + 1) * P, :]).then_inc(wb_full[k % RS], 16)

            for k in range(KD):
                if k < RS:
                    sp.wait_ge(mx_ready, k + 1)
                else:
                    wait_big_lo(sp, k - RS, 0)
                load_big(k, w_o[0])

            def load_x(lt):
                if lt == 0:
                    sp.wait_ge(mx_ready, KD)
                if lt >= 2:
                    sp.wait_ge(x1_ready, lt - 1)
                sp.dma_start(x_in[lt % 2][:], x[0, lt * P:(lt + 1) * P, :]).then_inc(x_in_full[lt % 2], 16)

            load_x(0)
            load_x(1)
            for k in range(KD):
                wait_big_lo(sp, k, 0)
            sp.dma_start(p_nat[:], p[0, 0].rearrange("(t q) k -> q t k", q=P)).then_inc(ple_in, 16)
            sp.dma_start(wp_raw[:], w_ple[0].rearrange("(k q) d -> q k d", q=P)).then_inc(ple_in, 16)
            for lt in range(LT):
                if lt == LT - 1:
                    for k in range(RS, KD):
                        wait_big_lo(sp, k - RS, 1)
                        load_big(k, w_ple_gate[0])
                sp.wait_ge(x1_ready, lt + 1)
                sp.dma_start(x1_dram[lt * P:(lt + 1) * P, :], x1[lt % 2][:]).then_inc(x1_stored[lt % 2], 16)
                if lt + 2 < LT:
                    load_x(lt + 2)
                if lt == P_AT + KP - 1:
                    sp.wait_ge(pt_ready, 2 * KP)
                    sp.wait_ge(wp_ready, 1)
                    for k in range(RS):
                        load_big(k, w_ple_gate[0])

            def load_x1(lt):
                sp.wait_ge(x1_stored[lt % 2], 16 * (lt // 2 + 1))
                if lt >= 2:
                    sp.wait_ge(out_ready, 2 * lt - 2)
                sp.dma_start(x_in[lt % 2][:], x1_dram[lt * P:(lt + 1) * P, :]).then_inc(x_in_full[lt % 2], 16)

            sp.wait_ge(x1_ready, LT)
            load_x1(0)
            load_x1(1)
            for lt in range(LT):
                for half in range(2):
                    cols = slice(half * HALF, (half + 1) * HALF)
                    sp.wait_ge(out_ready, 2 * lt + half + 1)
                    sp.dma_start(out[0, lt * P:(lt + 1) * P, cols], x1[lt % 2][:, cols]).then_inc(out_stored[lt % 2], 16)
                if lt + 2 < LT:
                    load_x1(lt + 2)
            for i in range(2):
                sp.wait_ge(out_stored[i], 32 * (LT // 2))

        @block.gpsimd
        def _(pool):
            nc.gpsimd.memset(ident[:], 0.0).then_inc(ident_ready, 1)
            pool.wait_ge(ident_ready, 1)
            nc.gpsimd.affine_select(out=ident[:], in_=ident[:], compare_op=ALU.not_equal, fill=1.0, base=0,
                                    pattern=[[-1, P]], channel_multiplier=1).then_inc(ident_ready, 1)

            with nc.allow_non_contiguous_dma(reason="small parameter tables"):
                pool.dma_start(gain_pre[:], pre_norm[0].rearrange("(k p) -> p k", p=P)).then_inc(consts_loaded, 16)
                pool.dma_start(cw[:], conv_w[0].rearrange("t (k p) -> p t k", p=P)).then_inc(consts_loaded, 16)
                pool.dma_start(bg[:], b_glu[0].rearrange("(k p) -> p k", p=P)).then_inc(consts_loaded, 16)
                for ri, cc in enumerate((c_re, c_im)):
                    src = cc[0].rearrange("(f a) h s -> (a h) f s", f=4)
                    for b in range(2):
                        pool.dma_start(c_nat[:, ri, :, b * N_STATE:(b + 1) * N_STATE], src
                                       ).then_inc(params_loaded, 16)
                for b in range(2):
                    rows = slice(b * N_STATE, (b + 1) * N_STATE)
                    for n, aa in enumerate((a_re, a_im)):
                        pool.dma_start(small[rows, n, :],
                                       aa[0].rearrange("(a b) s -> b s a", b=2)[b]).then_inc(params_loaded, 16)
                    pool.dma_start(small[rows, 2, :], log_step[0].rearrange("(a b) -> b a", b=2)[b]
                                   .partition_broadcast(N_STATE)).then_inc(params_loaded, 16)
                    for dst, bb in ((b_r, b_re), (b_i, b_im)):
                        pool.dma_start(dst[rows, :, :],
                                       bb[0].rearrange("(a b) s h -> b s a h", b=2)[b]).then_inc(params_loaded, 16)
                pool.dma_start(d_hg[:], d_skip[0].rearrange("(g h) -> h g", h=GC)).then_inc(params_loaded, 16)

            pool.wait_ge(wu_hi_ready, 1)
            nc.gpsimd.tensor_tensor(wu_lo[:, 0:KD // 2, :], wu_raw[:], wu_hi[:, 0:KD // 2, :].bitcast(f32),
                                    ALU.subtract).then_inc(wu_ready, 1)

            def lo(n, c, kk):
                pool.wait_ge(w_hi_ready, n + 1)
                nc.gpsimd.tensor_tensor(w_lo[c % 2][:, 0:kk, :], w_raw[c][:, 0:kk, :],
                                        w_hi[c % 2][:, 0:kk, :].bitcast(f32), ALU.subtract).then_inc(w_ready, 1)

            def quad(q, kks=(KD, KD, KD, KD)):
                for c in range(4):
                    lo(4 * q + c, c, kks[c])

            quad(Q_CONV0)
            with pool.Fori(Q_CONV1, Q_GLU) as q:
                quad(q)
            quad(Q_GLU, (KS,) * 4)
            quad(Q_CONV3)
            with pool.Fori(Q_YA, Q_CONV4) as q:
                quad(q, (KD, KS, KD, KS))
            with pool.Fori(Q_CONV4, Q_END) as q:
                quad(q)

            def big_lo_part(k, index):
                pool.wait_ge(wb_hi_ready, index * KD + k + 1)
                nc.gpsimd.tensor_tensor(big_lo[:, k, :], wb_raw[k % RS][:], big_hi[:, k, :].bitcast(f32),
                                        ALU.subtract).then_inc(wb_ready_p, 1)

            for k in BIG_LO_P:
                big_lo_part(k, 0)
            pool.wait_ge(wp_hi_ready, 1)
            nc.gpsimd.tensor_tensor(wp_lo[:], wp_raw[:], wp_hi[:].bitcast(f32), ALU.subtract).then_inc(wp_ready, 1)
            for k in BIG_LO_P:
                big_lo_part(k, 1)

        @block.scalar
        def _(act):
            def evac_start(use):
                act.wait_ge(aux_full, use + 1)

            for half in range(2):
                for i in range(4 * half, 4 * half + 4):
                    act.wait_ge(x_loaded[i], 16)
                    if i:
                        act.wait_ge(squares_done, i)
                    nc.scalar.activation(sq_junk[:], x_tile[i][:], ACT.Square,
                                         accum_out=ssq[:, i:i + 1]).then_inc(squares_done, 1)
            act.wait_ge(consts_loaded, 48)
            for half in range(2):
                for k in range(KD):
                    use = A_H + half * KD + k
                    evac_start(use)
                    nc.scalar.activation(big_hi[:, k, half * HALF:(half + 1) * HALF], aux[:, use % 4, :], ACT.Copy,
                                         scale=gain_pre[:, k:k + 1]).then_inc(h_hi_ready, 1)
                act.wait_ge(wu_loaded[half], 16)
                nc.scalar.activation(wu_hi[:, half * (KD // 2):(half + 1) * (KD // 2), :],
                                     (wu_raw, wu_raw2)[half][:], ACT.Copy).then_inc(wu_hi_ready, 1)

            def hi(n, c, kk, first=False):
                act.wait_ge(raw_full[c], 4 * n + (16 - 4 * c))
                if not first:
                    act.wait_ge(tile_done, n - 1)
                nc.scalar.activation(w_hi[c % 2][:, 0:kk, :], w_raw[c][:, 0:kk, :], ACT.Copy).then_inc(w_hi_ready, 1)

            def to_s1(func, n, c, w, first=False, **kw):
                act.wait_ge(tile_done, n + 1)
                if not first:
                    act.wait_ge(s1_used, w)
                nc.scalar.activation(s1[:], flat(slot_ps(c % 2)), func, **kw).then_inc(s1_full, 1)

            def conv_quad(q, w, first=False, next_kk=KD):
                n = 4 * q
                hi(n + 1, 1, KD, first)
                act.wait_ge(tile_done, n + 1)
                if not first:
                    act.wait_ge(s1_used, w)
                nc.scalar.activation(s1[:], flat(slot_ps(0)), ACT.Copy).then_inc(s1_full, 1)
                act.wait_ge(s1_full, w + 1)
                act.sem_inc(slot_free[0], 1)
                hi(n + 2, 2, KD)
                hi(n + 3, 3, KD)
                act.wait_ge(tile_done, n + 3)
                act.wait_ge(s1_used, w + 1)
                nc.scalar.activation(s1[:], flat(slot_ps(0)), ACT.Silu).then_inc(s1_full, 1)
                act.wait_ge(s1_full, w + 2)
                act.sem_inc(slot_free[0], 1)
                hi(n + 4, 0, next_kk)

            hi(0, 0, KD, first=True)
            conv_quad(Q_CONV0, 0, first=True)

            def copy_bank(use, dst, src):
                evac_start(use)
                nc.scalar.activation(dst, src, ACT.Copy).then_inc(aux_free[use % 4], 1)

            for b in range(0, G // 4, 2):
                copy_bank(A_W + b, flat(w_in_state[:, 4 * b:4 * b + 4, :]), aux[:, (A_W + b) % 4, :])
            for b in range(0, G // 4, 2):
                copy_bank(A_UT + b, flat(u_chunk[:, 4 * b:4 * b + 4, :]), aux[:, (A_UT + b) % 4, :])
            for b in range(0, G // 4, 2):
                copy_bank(A_K + b, flat(kern[:, 4 * b:4 * b + 4, :]), aux[0:GC, (A_K + b) % 4, :])
            for b in range(0, G // 4, 2):
                use = A_WC + b
                evac_start(use)
                nc.scalar.activation(flat(w_c[0:N_STATE, b // 2, 0]), aux[0:N_STATE, use % 4, :], ACT.Copy)
                nc.scalar.activation(flat(w_c[0:N_STATE, b // 2, 1]), aux[N_STATE:P, use % 4, :],
                                     ACT.Copy).then_inc(aux_free[use % 4], 1)

            act.wait_ge(kern_ready, 1)
            act.wait_ge(toep_zero, 1)
            for j in range(T):
                m = T - 1 - j
                act.dma_start(toep[m * GC:(m + 1) * GC, :, j * GC:T * GC],
                             kern[:, :, 0:(T - j) * GC]).then_inc(toep_ready, 16)
            with act.Fori(Q_CONV1, Q_GSSM) as q:
                conv_quad(q, 2 * q)

            act.wait_ge(state_ready, 4)
            for b in range(G // 4):
                use = A_Y + b
                evac_start(use)
                nc.scalar.activation(
                    y_nat[:, :, 4 * b * GC:4 * (b + 1) * GC].rearrange("c j (g h) -> c g j h", h=GC),
                    aux[:, use % 4, :].rearrange("c (g j h) -> c g j h", g=4, h=GC),
                    ACT.Copy).then_inc(aux_free[use % 4], 1)
            for ct in range(KS):
                for jb in range(2):
                    use = A_YT + 2 * ct + jb
                    evac_start(use)
                    ins = nc.scalar.activation(
                        y_f[:, ct, :].rearrange("p (c j) -> p j c", j=T)[:, 4 * jb:4 * jb + 4, :],
                        aux[:, use % 4, :].rearrange("p (j c) -> p j c", c=C), ACT.Gelu_apprx_tanh)
                    ins.then_inc(gelu_ready, 1)
                    act.wait_ge(gelu_ready, 2 * ct + jb + 1)
                    act.sem_inc(aux_free[use % 4], 1)
            for ct in range(KS):
                nc.scalar.activation(y_hi[:, ct, :], y_f[:, ct, :], ACT.Copy).then_inc(y_hi_ready, 1)

            for c in range(4):
                n = 4 * Q_GSSM + c
                hi(n + 1, (c + 1) % 4, KD if c < 3 else KS)
                act.wait_ge(tile_done, n + 1)
                nc.scalar.activation(y_g[:, c, :], flat(slot_ps(c % 2)), ACT.Silu).then_inc(gssm_ready, 1)
                act.wait_ge(gssm_ready, c + 1)
                act.sem_inc(slot_free[c % 2], 1)
            for c in range(4):
                n = 4 * Q_GLU + c
                hi(n + 1, (c + 1) % 4, KS if c < 3 else KD)
                to_s1(ACT.Sigmoid, n, c, 6 + c, bias=bg[:, c:c + 1])
                act.wait_ge(s1_full, 7 + c)
                act.sem_inc(slot_free[c % 2], 1)
            for ct in range(KS):
                act.wait_ge(y2_ready, ct + 1)
                nc.scalar.activation(y_hi[:, ct, :], y_g[:, ct, :], ACT.Copy).then_inc(y_hi_ready, 1)

            conv_quad(Q_CONV3, 10)

            with act.Fori(Q_YA, Q_CONV4) as q:
                for c in range(4):
                    n = 4 * q + c
                    hi(n + 1, (c + 1) % 4, KS if c % 2 == 0 else KD)
                    if c % 2 == 0:
                        w = 2 * q + (12 + c // 2 - 2 * Q_YA)
                        to_s1(ACT.Sigmoid, n, c, w)
                        act.wait_ge(s1_full, w + 1)
                        act.sem_inc(slot_free[0], 1)
            with act.Fori(Q_CONV4, Q_RC) as q:
                conv_quad(q, 2 * q + (20 - 2 * Q_CONV4))

            def rc_tile(q, c):
                act.wait_ge(tile_done, 4 * q + c + 1)
                nc.scalar.activation(rc_gate[:, bass.ds(4 * q + (c - 4 * Q_RC), 1), :].rearrange("p a l -> p (a l)"),
                                     flat(slot_ps(c % 2)), ACT.Sigmoid).then_inc(rc_ready, 1)
                act.wait_ge(rc_ready, 4 * q + (c + 1 - 4 * Q_RC))
                act.sem_inc(slot_free[c % 2], 1)

            with act.Fori(Q_RC, Q_YB - 1) as q:
                for c in range(4):
                    hi(4 * q + c + 1, (c + 1) % 4, KD)
                    rc_tile(q, c)
            for c in range(4):
                hi(4 * (Q_YB - 1) + c + 1, (c + 1) % 4, KD)
                if c < 3:
                    rc_tile(Q_YB - 1, c)

            act.wait_ge(z_done, KD)
            act.wait_ge(tile_done, 4 * Q_YB)
            for k in range(KD):
                nc.scalar.activation(big_hi[:, k, :], z[:, k, :], ACT.Copy).then_inc(z_hi_ready, 1)

            rc_tile(Q_YB - 1, 3)

            def merge_hi(q, c, d):
                act.wait_ge(sum_ready, d + 1)
                nc.scalar.activation(mx_hi[:, bass.ds(d, 1), :].rearrange("p a l -> p (a l)"),
                                     yam[:, bass.ds(d, 1), :].rearrange("p a l -> p (a l)"),
                                     ACT.Copy).then_inc(mx_hi_ready, 1)

            act.wait_ge(z_ready, KD)
            with act.Fori(Q_YB, Q_END - 1) as q:
                for c in range(4):
                    hi(4 * q + c + 1, (c + 1) % 4, KD)
                    merge_hi(q, c, 4 * q + (c - 4 * Q_YB))
            for c in range(3):
                hi(4 * (Q_END - 1) + c + 1, c + 1, KD)
                merge_hi(Q_END - 1, c, 4 + c)

            def big_part(k, index):
                act.wait_ge(wb_full[k % RS], 16 * wb_round(k, index))
                nc.scalar.activation(big_hi[:, k, :], wb_raw[k % RS][:], ACT.Copy).then_inc(wb_hi_ready, 1)

            def wb_round(k, index):
                per = [len(range(s, KD, RS)) for s in range(RS)]
                return index * per[k % RS] + k // RS + 1

            act.wait_ge(tile_done, 4 * Q_END)
            for k in range(KD):
                big_part(k, 0)
                if k == 1:
                    merge_hi(Q_END - 1, 3, 7)

            def x1_hi(lt):
                for half in range(2):
                    use = pair_use("x1", lt) + half
                    evac_start(use)
                    nc.scalar.activation(mx_hi[:, 4 * half:4 * half + 4, lt * P:(lt + 1) * P],
                                         aux[:, use % 4, :].rearrange("p (k l) -> p k l", l=P),
                                         ACT.Copy).then_inc(x1_hi_ready, 1)

            def pt_hi_part(part):
                for half in range(2):
                    use = pair_use("p", part) + half
                    evac_start(use)
                    nc.scalar.activation(pt_hi[:, part, half * HALF:(half + 1) * HALF], aux[:, use % 4, :],
                                         ACT.Copy).then_inc(pt_hi_ready, 1)

            for lt in range(LT):
                if lt >= P_AT and lt - P_AT < KP:
                    pt_hi_part(lt - P_AT)
                act.wait_ge(tile_done, 4 * Q_END + lt + 1)
                if lt == LT - 1:
                    for k in range(KD):
                        big_part(k, 1)
                if lt >= 2:
                    act.wait_ge(x1_stored[lt % 2], 16 * (lt // 2))
                    act.wait_ge(aux_full, pair_use("x1", lt - 2) + 2)
                nc.scalar.activation(x1[lt % 2][:], flat(slot_ps(lt % 2)), ACT.Square,
                                     accum_out=ssq[:, LT + lt:LT + lt + 1]).then_inc(squares_done, 1)
                if lt >= 1:
                    x1_hi(lt - 1)
                if lt == P_AT - 1:
                    act.wait_ge(ple_in, 32)
                    nc.scalar.activation(wp_hi[:], wp_raw[:], ACT.Copy).then_inc(wp_hi_ready, 1)

            for lt in range(LT):
                act.wait_ge(tile_done, 4 * Q_END + LT + lt + 1)
                if lt >= 1:
                    act.wait_ge(esq_done, lt)
                else:
                    act.wait_ge(x1_ready, LT)
                nc.scalar.activation(sig_row[:], flat(slot_ps(lt % 2)), ACT.Sigmoid).then_inc(sig_ready, 1)
                act.wait_ge(sig_ready, lt + 1)
                act.sem_inc(slot_free[lt % 2], 1)
                if lt == 0:
                    x1_hi(LT - 1)
                act.wait_ge(e_ready, lt + 1)
                j = 2 * LT + lt
                nc.scalar.activation(sig_row[:], x1[lt % 2][:], ACT.Square,
                                     accum_out=ssq[:, j:j + 1]).then_inc(esq_done, 1)
        @block.vector
        def _(dve):
            V = nc.vector
            count = [0]

            def link(ins):
                count[0] += 1
                ins.then_inc(dve_chain, 1)
                dve.wait_ge(dve_chain, count[0])

            def tt(o, a, b, op):
                link(V.tensor_tensor(o, a, b, op))

            def ts(o, a, s0, op0, s1_=None, op1=None):
                if op1 is None:
                    link(V.tensor_scalar(o, a, s0, None, op0))
                else:
                    link(V.tensor_scalar(o, a, s0, s1_, op0, op1))

            def stt(o, a, s, b, op0, op1):
                link(V.scalar_tensor_tensor(out=o, in0=a, scalar=s, in1=b, op0=op0, op1=op1))

            def inverse_rms(j0, j1):
                s = slice(j0, j1)
                ts(va[:, s], ssq[:, s], 1.0 / D, ALU.mult, EPS, ALU.add)
                link(V.tensor_single_scalar(vb[:, s].bitcast(i32), va[:, s].bitcast(i32), 1,
                                            ALU.arith_shift_right))
                ts(rstd[:, s].bitcast(i32), vb[:, s].bitcast(i32), -1.0, ALU.mult, 1597463007.0, ALU.add)
                for _ in range(4):
                    tt(vb[:, s], rstd[:, s], rstd[:, s], ALU.mult)
                    stt(vb[:, s], vb[:, s], -0.5, va[:, s], ALU.mult, ALU.mult)
                    stt(rstd[:, s], vb[:, s], 1.5, rstd[:, s], ALU.add, ALU.mult)

            for half in range(2):
                dve.wait_ge(squares_done, 4 * half + 4)
                inverse_rms(4 * half, 4 * half + 4)
                for i in range(4 * half, 4 * half + 4):
                    V.tensor_scalar(x_tile[i][:], x_tile[i][:], rstd[:, i:i + 1], None,
                                    ALU.mult).then_inc(xn_ready, 1)
            dve.wait_ge(consts_loaded, 48)
            for half in range(2):
                for k in range(KD):
                    use = A_H + half * KD + k
                    dve.wait_ge(h_hi_ready, half * KD + k + 1)
                    cols = slice(half * HALF, (half + 1) * HALF)
                    V.scalar_tensor_tensor(out=big_lo[:, k, cols], in0=aux[:, use % 4, :],
                                           scalar=gain_pre[:, k:k + 1], in1=big_hi[:, k, cols].bitcast(f32),
                                           op0=ALU.mult, op1=ALU.subtract).then_inc(aux_free[use % 4], 1)
            for ri in range(2):
                dve.wait_ge(aux_full, A_C + ri + 1)
                for par in range(2):
                    rows = slice(par * N_STATE, (par + 1) * N_STATE)
                    last = V.tensor_copy(c_t[rows, ri], aux[rows, (A_C + ri) % 4, :].rearrange(
                        "s (a b h) -> s a b h", b=2, h=GC)[:, :, par, :])
                last.then_inc(aux_free[(A_C + ri) % 4], 1)
            dve.wait_ge(wu_hi_ready, 2)
            V.tensor_tensor(wu_lo[:, KD // 2:KD, :], wu_raw2[:], wu_hi[:, KD // 2:KD, :].bitcast(f32),
                            ALU.subtract).then_inc(wu_ready, 1)

            names = {}

            def t(name):
                if name not in names:
                    names[name] = len(names)
                return small[:, names[name], :]

            for n in ("are", "aim", "ls"):
                t(n)

            def exp_to(o, a):
                LN2_HI, LN2_LO = 0.693359375, -2.12194440e-4
                ROUND = 12582912.0
                ts(t("ea"), a, -170.0, ALU.max, 170.0, ALU.min)
                ts(t("en"), t("ea"), 1.0 / math.log(2.0), ALU.mult, ROUND, ALU.add)
                ts(t("en"), t("en"), ROUND, ALU.subtract)
                stt(t("er"), t("en"), -LN2_HI, t("ea"), ALU.mult, ALU.add)
                stt(t("er"), t("en"), -LN2_LO, t("er"), ALU.mult, ALU.add)
                ts(t("ep"), t("er"), 1.0 / math.factorial(7), ALU.mult)
                for i in range(6, 0, -1):
                    stt(t("ep"), t("ep"), 1.0 / math.factorial(i), t("er"), ALU.add, ALU.mult)
                ts(t("ep"), t("ep"), 1.0, ALU.add)
                ts(t("e1"), t("en"), -126.0, ALU.max, 127.0, ALU.min)
                tt(t("e2"), t("en"), t("e1"), ALU.subtract)
                ts(t("e2"), t("e2"), -126.0, ALU.max, 127.0, ALU.min)
                for e in ("e1", "e2"):
                    ts(t(e + "i").bitcast(i32), t(e), 127.0, ALU.add, 8388608.0, ALU.mult)
                    tt(t("ep"), t("ep"), t(e + "i"), ALU.mult)
                link(V.tensor_copy(o, t("ep")))

            def cmul(o_r, o_i, a_r, a_i, b_r_, b_i_, u, v):
                tt(u, a_r, b_r_, ALU.mult)
                tt(v, a_i, b_i_, ALU.mult)
                tt(o_r, u, v, ALU.subtract)
                tt(u, a_r, b_i_, ALU.mult)
                tt(v, a_i, b_r_, ALU.mult)
                tt(o_i, u, v, ALU.add)

            def discretise():
                dve.wait_ge(params_loaded, 16 * 15)
                exp_to(t("dt"), t("ls"))
                tt(t("arg"), t("are"), t("dt"), ALU.mult)
                exp_to(t("mag"), t("arg"))
                tt(t("th"), t("aim"), t("dt"), ALU.mult)
                ts(t("en"), t("th"), 1.0 / (2 * math.pi), ALU.mult, 12582912.0, ALU.add)
                ts(t("en"), t("en"), 12582912.0, ALU.subtract)
                C1 = 6.28125
                C2 = float(round((2 * math.pi - C1) * 2 ** 22)) / 2 ** 22
                C3 = 2 * math.pi - C1 - C2
                for cst in (C1, C2, C3):
                    stt(t("th"), t("en"), -cst, t("th"), ALU.mult, ALU.add)
                ts(t("q"), t("th"), 0.25, ALU.mult, 0.8, ALU.min)
                ts(t("q"), t("q"), -0.8, ALU.max)
                tt(t("qq"), t("q"), t("q"), ALU.mult)
                ts(t("s"), t("qq"), 1.0 / math.factorial(9), ALU.mult)
                for i in (7, 5, 3):
                    sign = 1.0 if i == 5 else -1.0
                    stt(t("s"), t("s"), sign / math.factorial(i), t("qq"), ALU.add, ALU.mult)
                stt(t("s"), t("s"), 1.0, t("q"), ALU.add, ALU.mult)
                ts(t("c"), t("qq"), -1.0 / math.factorial(10), ALU.mult)
                for i in (8, 6, 4, 2):
                    sign = 1.0 if i % 4 == 0 else -1.0
                    stt(t("c"), t("c"), sign / math.factorial(i), t("qq"), ALU.add, ALU.mult)
                ts(t("c"), t("c"), 1.0, ALU.add)
                for _ in range(2):
                    stt(t("c2"), t("s"), -2.0, t("s"), ALU.mult, ALU.mult)
                    stt(t("s"), t("s"), 2.0, t("c"), ALU.mult, ALU.mult)
                    ts(t("c"), t("c2"), 1.0, ALU.add)
                tt(t("ar"), t("mag"), t("c"), ALU.mult)
                tt(t("ai"), t("mag"), t("s"), ALU.mult)
                ts(t("nr"), t("ar"), 1.0, ALU.subtract)
                tt(t("u"), t("are"), t("are"), ALU.mult)
                tt(t("v"), t("aim"), t("aim"), ALU.mult)
                tt(t("u"), t("u"), t("v"), ALU.add)
                link(V.reciprocal(t("rd"), t("u")))
                tt(t("u"), t("nr"), t("are"), ALU.mult)
                tt(t("v"), t("ai"), t("aim"), ALU.mult)
                tt(t("u"), t("u"), t("v"), ALU.add)
                tt(t("fr"), t("u"), t("rd"), ALU.mult)
                tt(t("u"), t("ai"), t("are"), ALU.mult)
                tt(t("v"), t("nr"), t("aim"), ALU.mult)
                tt(t("u"), t("u"), t("v"), ALU.subtract)
                tt(t("fi"), t("u"), t("rd"), ALU.mult)

            def powers():
                tt(t("u"), t("mag"), t("mag"), ALU.mult)
                tt(t("u"), t("u"), t("u"), ALU.mult)
                tt(mag8[:], t("u"), t("u"), ALU.mult)
                cmul(t("x2"), t("y2"), t("c"), t("s"), t("c"), t("s"), t("u"), t("v"))
                cmul(t("x4"), t("y4"), t("x2"), t("y2"), t("x2"), t("y2"), t("u"), t("v"))
                cmul(turn1_r[:], turn1_i[:], t("x4"), t("y4"), t("x4"), t("y4"), t("u"), t("v"))
                V.memset(pw_r[:, :, 0:1], 1.0)
                V.memset(pw_i[:, :, 0:1], 0.0)
                V.tensor_copy(pw_r[:, :, 1:2], t("ar").unsqueeze(2))
                link(V.tensor_copy(pw_i[:, :, 1:2], t("ai").unsqueeze(2)))
                m = 1
                while m < T:
                    uu = t1[:].rearrange("p a b -> p (a b)")[:, 0:PAIRS * m].rearrange("p (a b) -> p a b", b=m)
                    vv = t2[:].rearrange("p a b -> p (a b)")[:, 0:PAIRS * m].rearrange("p (a b) -> p a b", b=m)
                    lo_, hi_ = slice(1, m + 1), slice(m + 1, 2 * m + 1)
                    by = [w[:, :, m:m + 1].to_broadcast([P, PAIRS, m]) for w in (pw_r, pw_i)]
                    cmul(pw_r[:, :, hi_], pw_i[:, :, hi_], pw_r[:, :, lo_], pw_i[:, :, lo_], by[0], by[1], uu, vv)
                    m *= 2

            def per_row(ap):
                return ap.unsqueeze(2).to_broadcast([P, PAIRS, GC])

            def bbar():
                u = t1[:].rearrange("p a b -> p (a b)")[:, 0:PAIRS * GC].rearrange("p (a b) -> p a b", b=GC)
                v = t2[:].rearrange("p a b -> p (a b)")[:, 0:PAIRS * GC].rearrange("p (a b) -> p a b", b=GC)
                cmul(bb_r[:], bb_i[:], b_r[:], b_i[:], per_row(t("fr")), per_row(t("fi")), u, v)
                for ri, src in enumerate((bb_r, bb_i)):
                    for par in range(2):
                        link(V.tensor_copy(
                            bb_stack[ri * N_STATE:(ri + 1) * N_STATE, :, :]
                            .rearrange("s (a b) h -> s a b h", b=2)[:, :, par, :],
                            src[par * N_STATE:(par + 1) * N_STATE, :, :]))

            def table(dst, n_pow, coef_r, coef_i, half, im_sign):
                prs = slice(8 * half, 8 * half + 8)
                cols = n_pow * GC
                u = t1[:].rearrange("p a b -> p (a b)")[:, 0:8 * cols]
                v = t2[:].rearrange("p a b -> p (a b)")[:, 0:8 * cols]
                view = lambda w: w.rearrange("p (a n h) -> p a n h", a=8, h=GC)
                pw = [w[:, prs, 0:n_pow].unsqueeze(3).to_broadcast([P, 8, n_pow, GC]) for w in (pw_r, pw_i)]
                co = [w[:, prs, :].unsqueeze(2).to_broadcast([P, 8, n_pow, GC]) for w in (coef_r, coef_i)]
                for ri in range(2):
                    V.tensor_tensor(view(u), pw[0], co[ri], ALU.mult)
                    tt(view(v), pw[1], co[1 - ri], ALU.mult)
                    for par in range(2):
                        rows = slice(par * N_STATE, (par + 1) * N_STATE)
                        o = dst[ri * N_STATE:(ri + 1) * N_STATE].rearrange("s (a b) c -> s a b c", b=2)[:, prs, par, :]
                        uu = u[rows].rearrange("s (a c) -> s a c", a=8)
                        vv = v[rows].rearrange("s (a c) -> s a c", a=8)
                        if ri == 0:
                            last = V.tensor_tensor(o, uu, vv, ALU.subtract)
                        elif im_sign > 0:
                            last = V.tensor_tensor(o, uu, vv, ALU.add)
                        else:
                            last = V.scalar_tensor_tensor(out=o, in0=uu, scalar=-1.0, in1=vv, op0=ALU.mult,
                                                          op1=ALU.subtract)
                    link(last)

            ca_flat = ca[:].rearrange("p g n h -> p g (n h)")

            def u_bank(j):
                use = A_U + j
                dve.wait_ge(aux_full, use + 1)
                V.tensor_copy(u_nat[:, :, T - 1 - j, :],
                              aux[:, use % 4, :].rearrange("c (g h) -> c g h", h=GC)).then_inc(aux_free[use % 4], 1)

            discretise()
            for j in range(4):
                u_bank(j)
            powers()
            bbar()
            u_bank(4)
            table(ca_flat, NP, c_t[:, 0], c_t[:, 1], 0, -1)
            u_bank(5)
            table(ca_flat, NP, c_t[:, 0], c_t[:, 1], 1, -1)
            u_bank(6)
            u_bank(7)

            link(V.memset(v_pad[:, 0:2], 0.0))

            def tap(n_tap, ct):
                return cw[:, n_tap, bass.ds(ct, 1)]

            def conv_cc(q, ct, w, chain):
                n = 4 * q
                dve.wait_ge(tile_done, n + 2)
                dve.wait_ge(s1_full, w + 1)
                V.tensor_tensor(v_pad[:, 2:L + 2], flat(slot_ps(1)), s1[:], ALU.mult).then_inc(s1_used, 1)
                dve.wait_ge(s1_used, w + 1)
                dve.sem_inc(slot_free[1], 1)
                V.tensor_scalar(cv[:], v_pad[:, 2:L + 2], tap(2, ct), None, ALU.mult).then_inc(conv_step, 1)
                dve.wait_ge(conv_step, chain + 1)
                V.scalar_tensor_tensor(out=cv[:], in0=v_pad[:, 1:L + 1], scalar=tap(1, ct), in1=cv[:],
                                       op0=ALU.mult, op1=ALU.add).then_inc(conv_step, 1)
                dve.wait_ge(conv_step, chain + 2)
                V.scalar_tensor_tensor(out=cv[:], in0=v_pad[:, 0:L], scalar=tap(0, ct), in1=cv[:],
                                       op0=ALU.mult, op1=ALU.add).then_inc(conv_step, 1)

            def conv_bc(q, ct, w, chain):
                n = 4 * q
                dve.wait_ge(tile_done, n + 4)
                dve.wait_ge(conv_step, chain + 3)
                V.tensor_tensor(cv[:], flat(slot_ps(1)), cv[:], ALU.mult).then_inc(conv_step, 1)
                dve.wait_ge(conv_step, chain + 4)
                dve.sem_inc(slot_free[1], 1)
                dve.wait_ge(s1_full, w + 2)
                V.tensor_tensor(z[:, bass.ds(ct, 1), :].rearrange("p a l -> p (a l)"), cv[:], s1[:],
                                ALU.mult).then_inc(z_done, 1)
                dve.wait_ge(z_done, ct + 1)
                dve.sem_inc(s1_used, 1)

            def pv_half(half):
                if half == 0:
                    dve.wait_ge(aux_full, A_U + T)
                table(pv[:], T, bb_r[:], bb_i[:], half, 1)

            pv_half(0)
            conv_cc(Q_CONV0, 0, 0, 0)
            pv_half(1)
            dve.sem_inc(pv_ready, 1)
            conv_bc(Q_CONV0, 0, 0, 0)

            for b in range(1, G // 4, 2):
                use = A_W + b
                dve.wait_ge(aux_full, use + 1)
                V.tensor_copy(flat(w_in_state[:, 4 * b:4 * b + 4, :]), aux[:, use % 4, :]).then_inc(aux_free[use % 4], 1)
            for b in range(1, G // 4, 2):
                use = A_UT + b
                dve.wait_ge(aux_full, use + 1)
                V.tensor_copy(flat(u_chunk[:, 4 * b:4 * b + 4, :]), aux[:, use % 4, :]).then_inc(aux_free[use % 4], 1)
            for b in range(1, G // 4, 2):
                use = A_K + b
                dve.wait_ge(aux_full, use + 1)
                V.tensor_copy(flat(kern[:, 4 * b:4 * b + 4, :]), aux[0:GC, use % 4, :]).then_inc(aux_free[use % 4], 1)
            for i in range(4):
                uses = [u for u in range(A_K, A_K + G // 4) if u % 4 == i]
                dve.wait_ge(aux_free[i], uses[-1] // 4 + 1)
            diag = ident[0:GC, 0:GC].unsqueeze(1).to_broadcast([GC, G, GC])
            dk = d_diag[:]
            tt(dk, diag, d_hg[:].unsqueeze(2).to_broadcast([GC, G, GC]), ALU.mult)
            link(V.tensor_tensor(kern[:, :, 0:GC], kern[:, :, 0:GC], dk, ALU.add))
            dve.sem_inc(kern_ready, 1)
            for b in range(1, G // 4, 2):
                use = A_WC + b
                dve.wait_ge(aux_full, use + 1)
                V.tensor_copy(flat(w_c[N_STATE:P, b // 2, 0]), aux[0:N_STATE, use % 4, :])
                V.tensor_copy(flat(w_c[N_STATE:P, b // 2, 1]), aux[N_STATE:P, use % 4, :]).then_inc(aux_free[use % 4], 1)
            dve.wait_ge(aux_full, A_WC + G // 4)
            V.memset(toep[:], 0.0).then_inc(toep_zero, 1)
            for i in range(4):
                uses = [u for u in range(A_WC, A_WC + G // 4) if u % 4 == i]
                dve.wait_ge(aux_free[i], uses[-1] // 4 + 1)
            dve.wait_ge(toep_ready, 16 * T)

            local = [0]

            def turns(q, half):
                prs = bass.ds(8 * half, 8)
                V.memset(turn_r[:, :, 0:1], 1.0)
                V.memset(turn_i[:, :, 0:1], 0.0)
                V.tensor_copy(turn_r[:, :, 1:2], turn1_r[:, prs].unsqueeze(2))
                slink(q, V.tensor_copy(turn_i[:, :, 1:2], turn1_i[:, prs].unsqueeze(2)))
                m = 1
                while m < C:
                    uu = q1q2[:, 0:8 * m].rearrange("p (a b) -> p a b", b=m)
                    vv = q3q4[:, 0:8 * m].rearrange("p (a b) -> p a b", b=m)
                    lo_, hi_ = slice(1, m + 1), slice(m + 1, 2 * m + 1)
                    b0, b1 = (w[:, :, m:m + 1].to_broadcast([P, 8, m]) for w in (turn_r, turn_i))
                    V.tensor_tensor(uu, turn_r[:, :, lo_], b0, ALU.mult)
                    slink(q, V.tensor_tensor(vv, turn_i[:, :, lo_], b1, ALU.mult))
                    slink(q, V.tensor_tensor(turn_r[:, :, hi_], uu, vv, ALU.subtract))
                    V.tensor_tensor(uu, turn_r[:, :, lo_], b1, ALU.mult)
                    slink(q, V.tensor_tensor(vv, turn_i[:, :, lo_], b0, ALU.mult))
                    slink(q, V.tensor_tensor(turn_i[:, :, hi_], uu, vv, ALU.add))
                    m *= 2

            def slink(q, ins):
                local[0] += 1
                ins.then_inc(scan_step, 1)
                dve.wait_ge(scan_step, (q - Q_CONV1) * PER_TURN + local[0])

            PER_TURN = 1 + 7 * 4 + 2 * 7

            def scan_block(q, half, b):
                qd = 2 * half + b
                wr, wi = (w_c[:, bass.ds(qd, 1), r].rearrange("p q a c -> p (q a) c") for r in range(2))
                ps = slice(4 * b, 4 * b + 4)
                er, ei = turn_r[:, ps, 1:C + 1], turn_i[:, ps, 1:C + 1]
                V.tensor_tensor(q1[:], er, wr, ALU.mult)
                V.tensor_tensor(q2[:], ei, wi, ALU.mult)
                V.tensor_tensor(q3[:], er, wi, ALU.mult)
                slink(q, V.tensor_tensor(q4[:], ei, wr, ALU.mult))
                V.tensor_tensor(q1[:], q1[:], q2[:], ALU.add)
                slink(q, V.tensor_tensor(q3[:], q3[:], q4[:], ALU.subtract))
                for src, dst in ((q1, q2), (q3, q4)):
                    for a in range(4):
                        last = V.tensor_tensor_scan(dst[:, a, :],
                                                    mag8[:, bass.ds(4 * qd + a, 1)].to_broadcast([P, C]),
                                                    src[:, a, :], 0.0, ALU.mult, ALU.add)
                slink(q, last)
                er, ei = turn_r[:, ps, 1:C], turn_i[:, ps, 1:C]
                zr, zi = q2[:, :, 0:C - 1], q4[:, :, 0:C - 1]
                o1, o3 = q1[:, :, 0:C - 1], q3[:, :, 0:C - 1]
                for ri in range(2):
                    V.tensor_tensor(o1, er, zr if ri == 0 else zi, ALU.mult)
                    slink(q, V.tensor_tensor(o3, ei, zi if ri == 0 else zr, ALU.mult))
                    for par in range(2):
                        rows = slice(par * N_STATE, (par + 1) * N_STATE)
                        dst = state[ri * N_STATE:(ri + 1) * N_STATE, bass.ds(qd, 1), :, :].rearrange(
                            "s q (a b) c -> s (q a) b c", b=2)[:, :, par, :]
                        last = V.tensor_tensor(dst[:, :, 1:C], o1[rows], o3[rows],
                                               ALU.subtract if ri == 0 else ALU.add)
                        last = V.tensor_copy(dst[:, :, 0:1], v_pad[rows, 0:1].unsqueeze(1).to_broadcast([N_STATE, 4, 1]))
                    slink(q, last)
                dve.sem_inc(state_ready, 1)

            with dve.Fori(Q_CONV1, Q_GSSM) as q:
                half = q - Q_CONV1
                w, chain = 2 * q, 4 * q
                turns(q, half)
                conv_cc(q, q, w, chain)
                scan_block(q, half, 0)
                conv_bc(q, q, w, chain)
                scan_block(q, half, 1)
            assert local[0] == PER_TURN, local[0]

            def y_split(ct, src, n):
                dve.wait_ge(y_hi_ready, n)
                V.tensor_tensor(y_lo[:, ct, :], src[:, ct, :], y_hi[:, ct, :].bitcast(f32),
                                ALU.subtract).then_inc(y_ready, 1)

            for ct in range(KS):
                y_split(ct, y_f, ct + 1)
            for c in range(4):
                dve.wait_ge(s1_full, 7 + c)
                tt(s1[:], s1[:], y_f[:, c, :], ALU.mult)
                tt(y_g[:, c, :], s1[:], y_g[:, c, :], ALU.mult)
                dve.sem_inc(s1_used, 1)
            dve.wait_ge(tile_done, 4 * Q_GLU + 4)
            dve.sem_inc(y2_ready, KS)
            for ct in range(KS):
                y_split(ct, y_g, KS + ct + 1)

            conv_cc(Q_CONV3, 3, 10, 12)
            conv_bc(Q_CONV3, 3, 10, 12)

            with dve.Fori(Q_YA, Q_CONV4) as q:
                for c in (1, 3):
                    n = 4 * q + c
                    d = 2 * q + (c // 2 - 2 * Q_YA)
                    dve.wait_ge(s1_full, d + 13)
                    dve.wait_ge(tile_done, n + 1)
                    V.tensor_tensor(yam[:, bass.ds(d, 1), :].rearrange("p a l -> p (a l)"), flat(slot_ps(1)), s1[:],
                                    ALU.mult).then_inc(s1_used, 1)
                    dve.wait_ge(s1_used, d + 13)
                    dve.sem_inc(slot_free[1], 1)
            with dve.Fori(Q_CONV4, Q_RC) as q:
                ct = q - (Q_CONV4 - 4)
                conv_cc(q, ct, 2 * q + (20 - 2 * Q_CONV4), 4 * q + (16 - 4 * Q_CONV4))
                conv_bc(q, ct, 2 * q + (20 - 2 * Q_CONV4), 4 * q + (16 - 4 * Q_CONV4))

            for k in range(KD):
                dve.wait_ge(z_hi_ready, k + 1)
                V.tensor_tensor(big_lo[:, k, :], z[:, k, :], big_hi[:, k, :].bitcast(f32),
                                ALU.subtract).then_inc(z_ready, 1)

            def row(ap, d):
                return ap[:, bass.ds(d, 1), :].rearrange("p a l -> p (a l)")

            def merge_gate(q, c, d):
                dve.wait_ge(tile_done, 4 * q + c + 1)
                V.tensor_tensor(s1[:], flat(slot_ps(c % 2)), row(rc_gate, d), ALU.mult).then_inc(slot_free[c % 2], 1)
                dve.wait_ge(slot_free[c % 2], 2 * q + (c // 2 + 1))

            def merge_sum(d):
                V.tensor_tensor(row(yam, d), row(yam, d), s1[:], ALU.add).then_inc(sum_ready, 1)

            def merge_lo(d):
                dve.wait_ge(mx_hi_ready, d + 1)
                V.tensor_tensor(row(mx_lo, d), row(yam, d), row(mx_hi, d).bitcast(f32),
                                ALU.subtract).then_inc(mx_ready, 1)

            def merge(q, c):
                d = 4 * q + (c - 4 * Q_YB)
                merge_gate(q, c, d)
                merge_sum(d)
                merge_lo(d)
                dve.wait_ge(mx_ready, d + 1)

            def big_lo_part(k, index):
                dve.wait_ge(wb_hi_ready, index * KD + k + 1)
                V.tensor_tensor(big_lo[:, k, :], wb_raw[k % RS][:], big_hi[:, k, :].bitcast(f32),
                                ALU.subtract).then_inc(wb_ready_v, 1)

            with dve.Fori(Q_YB, Q_END - 1) as q:
                for c in range(4):
                    merge(q, c)
            for c in range(3):
                merge(Q_END - 1, c)
            merge_gate(Q_END - 1, 3, KD - 1)
            for i, k in enumerate(BIG_LO_V):
                big_lo_part(k, 0)
                if i == 0:
                    merge_sum(KD - 1)
                if i == 1:
                    merge_lo(KD - 1)

            def x1_lo(lt):
                for half in range(2):
                    use = pair_use("x1", lt) + half
                    dve.wait_ge(x1_hi_ready, 2 * lt + half + 1)
                    ks = slice(4 * half, 4 * half + 4)
                    ls = slice(lt * P, (lt + 1) * P)
                    V.tensor_tensor(mx_lo[:, ks, ls], aux[:, use % 4, :].rearrange("p (k l) -> p k l", l=P),
                                    mx_hi[:, ks, ls].bitcast(f32), ALU.subtract).then_inc(x1_split, 1)
                    dve.wait_ge(x1_split, 2 * lt + half + 1)
                    dve.sem_inc(aux_free[use % 4], 1)

            def pt_lo_part(part):
                for half in range(2):
                    use = pair_use("p", part) + half
                    cols = slice(half * HALF, (half + 1) * HALF)
                    dve.wait_ge(pt_hi_ready, 2 * part + half + 1)
                    V.tensor_tensor(pt_lo[:, part, cols], aux[:, use % 4, :], pt_hi[:, part, cols].bitcast(f32),
                                    ALU.subtract).then_inc(pt_ready, 1)
                    dve.wait_ge(pt_ready, 2 * part + half + 1)
                    dve.sem_inc(aux_free[use % 4], 1)

            dve.wait_ge(rows_loaded, 32)
            for lt in range(LT):
                j = LT + lt
                if lt >= P_AT and lt - P_AT < KP:
                    pt_lo_part(lt - P_AT)
                if lt == LT - 1:
                    for k in BIG_LO_V:
                        big_lo_part(k, 1)
                dve.wait_ge(squares_done, LT + lt + 1)
                inverse_rms(j, j + 1)
                stt(x1[lt % 2][:], flat(slot_ps(lt % 2)), rstd[:, j:j + 1], post_row[:], ALU.mult, ALU.mult)
                dve.sem_inc(slot_free[lt % 2], 1)
                dve.wait_ge(x_in_full[lt % 2], 16 * (lt // 2 + 1))
                V.tensor_tensor(x1[lt % 2][:], x1[lt % 2][:], x_in[lt % 2][:], ALU.add).then_inc(x1_ready, 1)
                if lt >= 1:
                    x1_lo(lt - 1)

            for lt in range(LT):
                j = 2 * LT + lt
                b0 = pair_use("e", lt) % 4
                if lt == 0:
                    x1_lo(LT - 1)
                dve.wait_ge(sig_ready, lt + 1)
                dve.wait_ge(aux_full, pair_use("e", lt) + 2)
                if lt >= 2:
                    dve.wait_ge(out_stored[lt % 2], 32 * (lt // 2))
                else:
                    dve.wait_ge(x1_stored[lt % 2], 16 * (LT // 2))
                V.tensor_tensor(x1[lt % 2][:], flat(aux[:, b0:b0 + 2, :]), sig_row[:], ALU.mult).then_inc(e_ready, 1)
                dve.wait_ge(e_ready, lt + 1)
                dve.sem_inc(aux_free[b0], 1)
                dve.sem_inc(aux_free[b0 + 1], 1)
                dve.wait_ge(esq_done, lt + 1)
                inverse_rms(j, j + 1)
                dve.wait_ge(x_in_full[lt % 2], 16 * ((LT + lt) // 2 + 1))
                for half in range(2):
                    cols = slice(half * HALF, (half + 1) * HALF)
                    stt(x1[lt % 2][:, cols], x1[lt % 2][:, cols], rstd[:, j:j + 1], ple_row[:, cols],
                        ALU.mult, ALU.mult)
                    V.tensor_tensor(x1[lt % 2][:, cols], x1[lt % 2][:, cols], x_in[lt % 2][:, cols],
                                    ALU.add).then_inc(out_ready, 1)

        @block.tensor
        def _(pe):
            M = nc.tensor

            def bank(use):
                if use >= 4:
                    pe.wait_ge(aux_free[use % 4], use // 4)
                return aux[:, use % 4, :]

            pe.wait_ge(ident_ready, 2)
            for half in range(2):
                pe.wait_ge(xn_ready, 4 * half + 4)
                for k in range(KD):
                    o = bank(A_H + half * KD + k)
                    for i in range(4):
                        last = M.transpose(o[:, i * P:(i + 1) * P],
                                           x_tile[4 * half + i][:, k * P:(k + 1) * P], ident[:])
                    last.then_inc(aux_full, 1)

            pe.wait_ge(params_loaded, 16 * 15)
            for ri in range(2):
                o = bank(A_C + ri)
                for f in range(4):
                    last = M.transpose(o[:, f * P:(f + 1) * P], c_nat[:, ri, f, :], ident[:])
                last.then_inc(aux_full, 1)
            def three(o, s_hi, s_lo, m_hi, m_lo, first, last):
                M.matmul(o, s_hi, m_hi, start=first, stop=False)
                M.matmul(o, s_hi, m_lo, start=False, stop=False)
                return M.matmul(o, s_lo, m_hi, start=False, stop=last)

            for i in range(4):
                uses = [u for u in range(A_H, A_H + 2 * KD) if u % 4 == i]
                pe.wait_ge(aux_free[i], uses[-1] // 4 + 1)
            pe.wait_ge(wu_ready, 2)
            h_pos = [w[:].rearrange("p k (c j) -> p k j c", j=T) for w in (big_hi, big_lo)]
            for j in range(T):
                o = bank(A_U + j)
                for k in range(KD):
                    last = three(o, h_pos[0][:, k, j, :], h_pos[1][:, k, j, :], wu_hi[:, k, :], wu_lo[:, k, :],
                                 k == 0, k == KD - 1)
                last.then_inc(aux_full, 1)

            def quad(q, moving=None, kks=(KD,) * 4, first=False, by_k=None):
                for c in range(4):
                    m_hi, m_lo = (moving or {}).get(c, (big_hi, big_lo))
                    tile(q, c, kks[c], m_hi, m_lo, first and c < 2, by_k)

            def tile(q, c, kk, m_hi, m_lo, first, by_k):
                pe.wait_ge(w_ready, 4 * q + c + 1)
                if not first:
                    pe.wait_ge(slot_free[c % 2], 2 * q + c // 2)
                for k in range(kk):
                    if by_k is not None and c == 0:
                        pe.wait_ge(by_k, k + 1)
                    for half in range(2):
                        cols = slice(half * HALF, (half + 1) * HALF)
                        last = three(slot_ps(c % 2)[:, half, :], w_hi[c % 2][:, k, :], w_lo[c % 2][:, k, :],
                                     m_hi[:, k, cols], m_lo[:, k, cols], k == 0, k == kk - 1)
                last.then_inc(tile_done, 1)

            quad(Q_CONV0, first=True)

            pe.wait_ge(pv_ready, 1)
            for b in range(G // 4):
                o = bank(A_W + b)
                for i in range(4):
                    last = M.transpose(o[:, i * P:(i + 1) * P], pv[:, 4 * b + i, :], ident[:])
                last.then_inc(aux_full, 1)
            for b in range(G // 4):
                o = bank(A_UT + b)
                for i in range(4):
                    last = M.transpose(o[:, i * P:(i + 1) * P],
                                       u_nat[:, 4 * b + i].rearrange("c m h -> c (m h)"), ident[:])
                last.then_inc(aux_full, 1)
            for b in range(G // 4):
                o = bank(A_K + b)
                for i in range(4):
                    g = 4 * b + i
                    last = M.matmul(o[0:GC, i * P:(i + 1) * P], bb_stack[:, g, :],
                                    ca[:, g, 0:T, :].rearrange("p n h -> p (n h)"), start=True, stop=True)
                last.then_inc(aux_full, 1)
            for i in range(4):
                uses = [u for u in range(A_W, A_K) if u % 4 == i]
                pe.wait_ge(aux_free[i], uses[-1] // 4 + 1)
            for b in range(G // 4):
                o = bank(A_WC + b)
                for i in range(4):
                    g = 2 * (4 * (b // 2) + i) + b % 2
                    last = M.matmul(o[:, i * P:(i + 1) * P], w_in_state[:, g, :], u_chunk[:, g, :],
                                    start=True, stop=True)
                last.then_inc(aux_full, 1)

            with pe.Fori(Q_CONV1, Q_GSSM) as q:
                quad(q)

            pe.wait_ge(toep_ready, 16 * T)
            for b in range(G // 4):
                pe.wait_ge(state_ready, b // 2 + 1)
                o = bank(A_Y + b)
                for i in range(4):
                    g = 4 * b + i
                    s = slice(i * P, (i + 1) * P)
                    M.matmul(o[:, s], u_chunk[:, g, :], toep[:, g, :], start=True, stop=False)
                    last = M.matmul(o[:, s], state[:, g // 8, g % 8, :],
                                    ca[:, g, 1:NP, :].rearrange("p n h -> p (n h)"), start=False, stop=True)
                last.then_inc(aux_full, 1)
            for i in range(4):
                uses = [u for u in range(A_Y, A_YT) if u % 4 == i]
                pe.wait_ge(aux_free[i], uses[-1] // 4 + 1)
            for ct in range(KS):
                for jb in range(2):
                    o = bank(A_YT + 2 * ct + jb)
                    for i in range(4):
                        last = M.transpose(o[:, i * P:(i + 1) * P], y_nat[:, 4 * jb + i, ct * P:(ct + 1) * P],
                                           ident[:])
                    last.then_inc(aux_full, 1)

            quad(Q_GSSM)
            pe.wait_ge(y_ready, KS)
            y_mov = {c: (y_hi, y_lo) for c in range(4)}
            quad(Q_GLU, y_mov, (KS,) * 4)
            quad(Q_CONV3)
            pe.wait_ge(y_ready, 2 * KS)
            with pe.Fori(Q_YA, Q_CONV4) as q:
                quad(q, {1: (y_hi, y_lo), 3: (y_hi, y_lo)}, (KD, KS, KD, KS))
            with pe.Fori(Q_CONV4, Q_YB) as q:
                quad(q)
            with pe.Fori(Q_YB, Q_END) as q:
                quad(q, by_k=z_ready)

            def transposes_x1(lt):
                pe.wait_ge(x1_ready, lt + 1)
                for half in range(2):
                    o = bank(pair_use("x1", lt) + half)
                    for i in range(4):
                        k = 4 * half + i
                        last = M.transpose(o[:, i * P:(i + 1) * P], x1[lt % 2][:, k * P:(k + 1) * P], ident[:])
                    last.then_inc(aux_full, 1)

            def row_tile(lt, base, index):
                pe.wait_ge(slot_free[lt % 2], (4 * Q_END + base + lt) // 2)
                ls = slice(lt * P, (lt + 1) * P)
                for k in range(KD):
                    if lt == 0:
                        wait_big_lo(pe, k, index)
                        if index == 0:
                            pe.wait_ge(mx_ready, k + 1)
                    for half in range(2):
                        cols = slice(half * HALF, (half + 1) * HALF)
                        last = three(slot_ps(lt % 2)[:, half, :], mx_hi[:, k, ls], mx_lo[:, k, ls],
                                     big_hi[:, k, cols], big_lo[:, k, cols], k == 0, k == KD - 1)
                last.then_inc(tile_done, 1)

            for lt in range(LT):
                if lt >= P_AT and lt - P_AT < KP:
                    k = lt - P_AT
                    pe.wait_ge(ple_in, 32)
                    for half in range(2):
                        o = bank(pair_use("p", k) + half)
                        for i in range(4):
                            last = M.transpose(o[:, i * P:(i + 1) * P],
                                               p_nat[:, 4 * half + i, k * P:(k + 1) * P], ident[:])
                        last.then_inc(aux_full, 1)
                row_tile(lt, 0, 0)
                if lt >= 1:
                    transposes_x1(lt - 1)

            def e_tile(lt):
                ls = slice(lt * P, (lt + 1) * P)
                for half in range(2):
                    o = bank(pair_use("e", lt) + half)
                    cols = slice(half * HALF, (half + 1) * HALF)
                    for k in range(KP):
                        last = three(o, pt_hi[:, k, ls], pt_lo[:, k, ls], wp_hi[:, k, cols], wp_lo[:, k, cols],
                                     k == 0, k == KP - 1)
                    last.then_inc(aux_full, 1)

            pe.wait_ge(pt_ready, 2 * KP)
            pe.wait_ge(wp_ready, 1)
            e_tile(0)
            for lt in range(LT):
                if lt == 1:
                    transposes_x1(LT - 1)
                pe.wait_ge(x1_split, 2 * lt + 2)
                row_tile(lt, LT, 1)
                if lt >= 1:
                    e_tile(lt)


def kernel(**inputs):
    import numpy as np
    import concourse.bacc as bacc
    from concourse import mybir
    from concourse.bass_utils import run_bass_kernel_spmd as run

    nc = bacc.Bacc("TRN2", target_bir_lowering=False, num_devices=1)
    names = ["x", "p", "pre_norm", "w_in", "a_re", "a_im", "log_step", "b_re", "b_im", "c_re", "c_im", "d_skip",
             "w_glu", "b_glu", "w_ssm_out", "conv_w", "w_conv_out", "w_o", "post_norm", "w_ple", "w_ple_gate",
             "ple_norm"]
    arrays, args = {}, []
    for name in names:
        a = np.ascontiguousarray(inputs[name])
        arrays[f"in_{name}"] = a
        args.append(nc.dram_tensor(f"in_{name}", a.shape, mybir.dt.from_np(a.dtype), kind="ExternalInput").ap())
    shape = inputs["x"].shape
    args.append(nc.dram_tensor("out_x", shape, mybir.dt.float32, kind="ExternalOutput").ap())
    build_block(nc, *args)
    return run(nc, [arrays], core_ids=[0]).results[0]["out_x"]
```

```python
def build_block(nc, x, p, pre_norm, w_in, a_re, a_im, log_step, b_re, b_im, c_re, c_im, d_skip,
                w_glu, b_glu, w_ssm_out, conv_w, w_conv_out, w_o, post_norm, w_ple, w_ple_gate,
                ple_norm, out):
    import math
    from contextlib import ExitStack
    import concourse.bass as bass
    from concourse import mybir

    f32, f32r, i32 = mybir.dt.float32, mybir.dt.float32r, mybir.dt.int32
    ALU = mybir.AluOpType
    ACT = mybir.ActivationFunctionType

    P = 128
    L, D = x.shape[1], x.shape[2]
    SSM_W = w_glu.shape[1]
    G, N_STATE, GC = b_re.shape[1], b_re.shape[2], b_re.shape[3]
    PLE = p.shape[3]
    KD, KS, KP, LT = D // P, SSM_W // P, PLE // P, L // P
    HALF = 512
    T = P // GC
    C = L // T
    PAIRS = G // 2
    NP = T + 1
    EPS = 1e-6
    COL_G, COL_XC = SSM_W, 2 * SSM_W
    COL_BC, COL_CC, COL_GC = COL_XC + D, COL_XC + 2 * D, COL_XC + 3 * D
    COL_RS, COL_RC = COL_XC + 4 * D, COL_XC + 5 * D

    Q_U, Q_CONV0, Q_CONV1, Q_CONV3, Q_GSSM, Q_GLU, Q_CONV4 = 0, 1, 2, 4, 5, 6, 7
    Q_YA, Q_CONV5, Q_RC, Q_YB, Q_END = 8, 12, 15, 17, 19

    ctx = ExitStack()
    with ctx:
        KB = 1024
        arena = ctx.enter_context(nc.sbuf_tensor("arena", [P, 207 * 256], f32))
        BASE = 16512

        def at(name, kb, shape, dt=f32):
            return nc.alloc_sbuf_tensor_at(name, shape, dt, offset=BASE + int(kb * KB))

        w_raw = [at(f"w_raw{i}", 4 * i, [P, KD, P]) for i in range(4)]
        w_hi = [at(f"w_hi{i}", 16 + 4 * i, [P, KD, P], f32r) for i in range(2)]
        w_lo = [at(f"w_lo{i}", 24 + 4 * i, [P, KD, P], f32r) for i in range(2)]
        big_hi = at("big_hi", 32, [P, KD, L], f32r)
        big_lo = at("big_lo", 64, [P, KD, L], f32r)
        z = at("z", 96, [P, KD, L])
        yam = at("yam", 128, [P, KD, L])
        rc_gate = at("rc_gate", 160, [P, KD, L])
        mx_hi = at("mx_hi", 96, [P, KD, L], f32r)
        mx_lo = at("mx_lo", 160, [P, KD, L], f32r)
        x_tile = [at(f"x_tile{i}", (174 if i < 4 else 126 - 16) + 4 * i, [P, D]) for i in range(LT)]
        sq_junk = at("sq_junk", 96, [P, D])
        u_f = at("u_f", 174, [P, KS, T, C])
        u_chunk = at("u_chunk", 108, [P, G, C])
        ca = at("ca", 124, [P, G, NP, GC])
        pv = at("pv", 142, [P, G, T * GC])
        w_in_state = at("w_in_state", 158, [P, G, P])
        toep = at("toep", 158, [P, G, T * GC])
        kern = at("kern", 174, [GC, G, T * GC])
        w_c = at("w_c", 142, [P, 4, 2, 4, C])
        state = at("state", 142, [P, 4, 8, C])
        turn_r = at("turn_r", 174, [P, 8, C + 1])
        turn_i = at("turn_i", 174 + 4.03125, [P, 8, C + 1])
        q1, q2, q3, q4 = (at(f"q{i}", 182.0625 + 2 * i, [P, 4, C]) for i in range(4))
        q1q2 = at("q1q2", 182.0625, [P, 8 * C])
        q3q4 = at("q3q4", 186.0625, [P, 8 * C])
        d_diag = at("d_diag", 100, [GC, G, GC])
        y_nat = at("y_nat", 174, [P, T, SSM_W])
        y_f = at("y_f", 144, [P, KS, L])
        y_g = at("y_g", 128, [P, KS, L])
        y_hi = at("y_hi", 160, [P, KS, L], f32r)
        y_lo = at("y_lo", 176, [P, KS, L], f32r)
        small = at("small", 100, [P, 44, PAIRS])
        b_r = at("b_r", 103, [P, PAIRS, GC])
        b_i = at("b_i", 104, [P, PAIRS, GC])
        bb_stack = at("bb_stack", 103, [P, G, GC])
        c_nat = at("c_nat", 105, [P, 2, 4, P])
        bb_r = at("bb_r", 105, [P, PAIRS, GC])
        bb_i = at("bb_i", 106, [P, PAIRS, GC])
        c_t = at("c_t", 167, [P, 2, PAIRS, GC])
        t1 = at("t1", 158, [P, 8, NP * GC])
        t2 = at("t2", 162.5, [P, 8, NP * GC])
        t3 = at("t3", 171.75, [P, 4, NP, GC])
        t4 = at("t4", 169.5, [P, 4, NP, GC])
        c_neg = at("c_neg", 169, [P, PAIRS // 2, GC])
        pw_r = at("pw_r", 190.25, [P, PAIRS, NP])
        pw_i = at("pw_i", 190.8125, [P, PAIRS, NP])
        turn1_r = at("turn1_r", 191.375, [P, PAIRS])
        turn1_i = at("turn1_i", 191.4375, [P, PAIRS])
        mag8 = at("mag8", 191.5, [P, PAIRS])
        d_hg = at("d_hg", 191.5625, [GC, G])
        s1 = at("s1", 192, [P, L])
        v_pad = at("v_pad", 196, [P, L + 2])
        cv = at("cv", 200.0625, [P, L])
        ident = at("ident", 204.0625, [P, P])
        gain_pre = at("gain_pre", 204.5625, [P, KD])
        cw = at("cw", 204.625, [P, 3, KD])
        bg = at("bg", 204.75, [P, KS])
        ssq = at("ssq", 204.8125, [P, 3 * LT + 1])
        va = at("va", 204.9375, [P, 3 * LT])
        vb = at("vb", 205.0625, [P, 3 * LT])
        rstd = at("rstd", 205.3125, [P, 3 * LT])
        z0_hi = at("z0_hi", 196, [P, L], f32r)
        z0_lo = at("z0_lo", 200, [P, L], f32r)
        gate0_hi = at("gate0_hi", 144, [P, D], f32r)
        gate0_lo = at("gate0_lo", 200, [P, D], f32r)
        wb_raw = [at(f"wb_raw{i}", 128 + 4 * i, [P, D]) for i in range(5)]
        p_nat = at("p_nat", 128, [P, LT, PLE])
        wp_raw = at("wp_raw", 136, [P, KP, D])
        x_in = [at(f"x_in{i}", 148 + 4 * i, [P, D]) for i in range(2)]
        x1 = [at("x1a", 156, [P, D]), at("x1b", 192, [P, D])]
        post_row = at("post_row", 196, [P, D])
        sig_row = at("sig_row", 196, [P, D])
        ple_row = at("ple_row", 128, [P, D])
        e_gain = at("e_gain", 132, [P, D])
        block1_hi = at("block1_hi", 0, [P, D], f32r)
        block1_lo = at("block1_lo", 4, [P, D], f32r)
        pt_lo = at("pt_lo", 8, [P, KP, L], f32r)
        wp_hi = at("wp_hi", 16, [P, KP, D], f32r)
        wp_lo = at("wp_lo", 24, [P, KP, D], f32r)

        tile_ps = ctx.enter_context(nc.psum_tensor("tile_ps", [P, 4, HALF], f32))
        aux = ctx.enter_context(nc.psum_tensor("aux", [P, 4, HALF], f32))
        u_dram = nc.dram_tensor("u_dram", (SSM_W, T, C), f32, kind="Internal").ap()
        x1_dram = nc.dram_tensor("x1_dram", (L, D), f32, kind="Internal").ap()

        def slot_ps(s):
            return tile_ps[:, 2 * s:2 * s + 2, :]

        def flat(ap):
            return ap.rearrange("p a b -> p (a b)")

        def sem(name):
            return ctx.enter_context(nc.semaphore(name))

        x_loaded = [sem(f"x_loaded{i}") for i in range(LT)]
        gain_loaded = sem("gain_loaded")
        consts_loaded = sem("consts_loaded")
        params_loaded = sem("params_loaded")
        ident_ready = sem("ident_ready")
        squares_done = sem("squares_done")
        rstd_ready = sem("rstd_ready")
        xn_ready = sem("xn_ready")
        xn_ready_a = sem("xn_ready_a")
        powers_ready = sem("powers_ready")
        ca_step = sem("ca_step")
        ca_ready = sem("ca_ready")
        h_hi_ready = sem("h_hi_ready")
        u_f_ready = sem("u_f_ready")
        u_stored = sem("u_stored")
        u_chunk_ready = sem("u_chunk_ready")
        aux_full = sem("aux_full")
        aux_free = [sem(f"aux_free{i}") for i in range(4)]
        raw_full = [sem(f"raw_full{i}") for i in range(4)]
        w_hi_ready = sem("w_hi_ready")
        w_ready = sem("w_ready")
        tile_done = sem("tile_done")
        slot_free = [sem("slot_free0"), sem("slot_free1")]
        s1_full = sem("s1_full")
        s1_used = sem("s1_used")
        dve_chain = sem("dve_chain")
        conv_step = sem("conv_step")
        scan_step = sem("scan_step")
        pv_ready = sem("pv_ready")
        toep_zero = sem("toep_zero")
        kern_ready = sem("kern_ready")
        toep_ready = sem("toep_ready")
        state_ready = sem("state_ready")
        gelu_ready = sem("gelu_ready")
        y_hi_ready = sem("y_hi_ready")
        y_ready = sem("y_ready")
        gssm_ready = sem("gssm_ready")
        y2_ready = sem("y2_ready")
        z_done = sem("z_done")
        z_hi_ready = sem("z_hi_ready")
        z_ready = sem("z_ready")
        rc_ready = sem("rc_ready")
        sum_ready = sem("sum_ready")
        mx_hi_ready = sem("mx_hi_ready")
        mx_ready = sem("mx_ready")
        wb_full = [sem(f"wb_full{i}") for i in range(KD)]
        wb_hi_ready = sem("wb_hi_ready")
        wb_ready_v = sem("wb_ready_v")
        wb_ready_p = sem("wb_ready_p")
        ple_in = sem("ple_in")
        wp_hi_ready = sem("wp_hi_ready")
        wp_ready = sem("wp_ready")
        pt_hi_ready = sem("pt_hi_ready")
        pt_ready = sem("pt_ready")
        x_in_full = [sem("x_in_full0"), sem("x_in_full1")]
        post_loaded = sem("post_loaded")
        ple_loaded = sem("ple_loaded")
        x1_ready = sem("x1_ready")
        x1_stored = [sem("x1_stored0"), sem("x1_stored1")]
        x1_hi_ready = sem("x1_hi_ready")
        x1_split = sem("x1_split")
        sig_ready = sem("sig_ready")
        e_ready = sem("e_ready")
        esq_done = sem("esq_done")
        out_ready = sem("out_ready")
        out_stored = [sem("out_stored0"), sem("out_stored1")]

        BIG_LO_V, BIG_LO_P = (0, 1, 2, 4, 5, 7), (3, 6)

        def big_block(k, index):
            if index == 1 and k == 0:
                return gate0_hi[:], gate0_lo[:]
            if k == 1:
                return block1_hi[:], block1_lo[:]
            return big_hi[:, k, :], big_lo[:, k, :]

        pt_hi = [big_hi[:, 1, :], big_lo[:, 1, :]]

        def raw_block(k, index):
            places = ((0, 1, 2, 3, 4, 5, 6, 0), (0, 1, 2, 3, 0, 5, 1, 2))[index]
            return (wb_raw + x_in)[places[k]][:]

        def hi_part(k, index, part):
            return index * (KD + 1) + k + 1 + (k > 1) + part

        def wait_big_lo(engine, k, index, part=None):
            if part is None:
                part = len(halves_of(k)) - 1
            if k in BIG_LO_V:
                engine.wait_ge(wb_ready_v, index * (len(BIG_LO_V) + 1) + BIG_LO_V.index(k) + 1 + (k > 1) + part)
            else:
                engine.wait_ge(wb_ready_p, index * len(BIG_LO_P) + BIG_LO_P.index(k) + 1)

        def halves_of(k):
            return [slice(0, HALF), slice(HALF, D)] if k == 1 else [slice(0, D)]

        def z_part(k, part):
            return k + 1 + (k > 1) + part

        A_H = 0
        A_C = A_H + 2 * KD
        A_W = A_C + 2
        A_K = A_W + G // 4
        A_WC = A_K + G // 4
        A_Y = A_WC + G // 4
        A_YT = A_Y + G // 4
        PAIR_ORDER = (["x1", "x1", "p", "x1", "p"] + ["x1"] * (LT - 4) + ["e", "x1"] + ["e"] * (LT - 1))
        P_AT = 3
        A_PAIR = A_YT + 2 * KS

        def pair_use(kind, n):
            at_pair = [i for i, what in enumerate(PAIR_ORDER) if what == kind][n]
            return A_PAIR + 2 * at_pair

        block = ctx.enter_context(nc.Block())

        @block.sync
        def _(sp):
            def load_x_tile(i):
                sp.dma_start(x_tile[i][:], x[0, i * P:(i + 1) * P, :]).then_inc(x_loaded[i], 16)

            for i in range(6):
                load_x_tile(i)

            def load_tile(n_is_first, n, c, weights, col, kk):
                if not n_is_first:
                    sp.wait_ge(w_ready, n - 3)
                src = weights.rearrange("(k p) e -> p k e", p=P)
                sp.dma_start(w_raw[c][:, 0:kk, :], src[:, :, bass.ds(col, P)]).then_inc(raw_full[c], 16)

            def load_conv(q, ct):
                for c, col in enumerate((COL_XC, COL_CC, COL_GC, COL_BC)):
                    load_tile(False, 4 * q + c, c, w_in[0], col + ct * P, KD)

            load_tile(True, 0, 0, w_in[0], 0, KD)
            load_x_tile(6)
            load_x_tile(7)
            for c in range(1, KS):
                load_tile(True, c, c, w_in[0], c * P, KD)
            with nc.allow_non_contiguous_dma(reason="small parameter tables"):
                for ri, cc in enumerate((c_re, c_im)):
                    src = cc[0].rearrange("(f a) h s -> (a h) f s", f=4)
                    for b in range(2):
                        sp.dma_start(c_nat[:, ri, :, b * N_STATE:(b + 1) * N_STATE], src).then_inc(params_loaded, 16)
                for b in range(2):
                    rows = slice(b * N_STATE, (b + 1) * N_STATE)
                    for n, aa in enumerate((a_re, a_im)):
                        sp.dma_start(small[rows, n, :],
                                     aa[0].rearrange("(a b) s -> b s a", b=2)[b]).then_inc(params_loaded, 16)
                    sp.dma_start(small[rows, 2, :], log_step[0].rearrange("(a b) -> b a", b=2)[b]
                                 .partition_broadcast(N_STATE)).then_inc(params_loaded, 16)
                    for dst, bb in ((b_r, b_re), (b_i, b_im)):
                        sp.dma_start(dst[rows, :, :],
                                     bb[0].rearrange("(a b) s h -> b s a h", b=2)[b]).then_inc(params_loaded, 16)
                sp.dma_start(cw[:], conv_w[0].rearrange("t (k p) -> p t k", p=P)).then_inc(consts_loaded, 16)
                sp.dma_start(bg[:], b_glu[0].rearrange("(k p) -> p k", p=P)).then_inc(consts_loaded, 16)
                sp.dma_start(d_hg[:], d_skip[0].rearrange("(g h) -> h g", h=GC)).then_inc(params_loaded, 16)
            load_conv(Q_CONV0, 0)

            for ct in range(KS):
                sp.wait_ge(u_f_ready, ct + 1)
                sp.dma_start(u_dram[ct * P:(ct + 1) * P], u_f[:, ct]).then_inc(u_stored, 16)
            load_conv(Q_CONV1, 1)
            sp.wait_ge(u_stored, 16 * KS)
            u_view = u_dram.rearrange("(g h) j c -> j h g c", h=GC)
            for j in range(T):
                m = T - 1 - j
                sp.dma_start(u_chunk[m * GC:(m + 1) * GC, :, :], u_view[j]).then_inc(u_chunk_ready, 16)

            sp.wait_ge(kern_ready, 1)
            sp.wait_ge(toep_zero, 1)
            for j in range(T):
                m = T - 1 - j
                sp.dma_start(toep[m * GC:(m + 1) * GC, :, j * GC:T * GC],
                             kern[:, :, 0:(T - j) * GC]).then_inc(toep_ready, 16)
            with sp.Fori(Q_CONV1 + 1, Q_GSSM) as q:
                load_conv(q, q - Q_CONV0)
            for c in range(4):
                load_tile(False, 4 * Q_GSSM + c, c, w_in[0], COL_G + c * P, KD)
            for c in range(4):
                load_tile(False, 4 * Q_GLU + c, c, w_glu[0], c * P, KS)
            load_conv(Q_CONV4, 4)
            with sp.Fori(Q_YA, Q_CONV5) as q:
                for c in range(4):
                    d = 2 * q + (c // 2 - 2 * Q_YA)
                    if c % 2 == 0:
                        load_tile(False, 4 * q + c, c, w_in[0], COL_RS + d * P, KD)
                    else:
                        load_tile(False, 4 * q + c, c, w_ssm_out[0], q * (2 * P) + (c // 2 - 2 * Q_YA) * P, KS)
            with sp.Fori(Q_CONV5, Q_RC) as q:
                load_conv(q, q - (Q_CONV5 - 5))
            with sp.Fori(Q_RC, Q_YB) as q:
                for c in range(4):
                    load_tile(False, 4 * q + c, c, w_in[0], COL_RC - 4 * Q_RC * P + c * P + q * 4 * P, KD)
            with sp.Fori(Q_YB, Q_END) as q:
                for c in range(4):
                    load_tile(False, 4 * q + c, c, w_conv_out[0], q * 4 * P + (c - 4 * Q_YB) * P, KD)

            def load_big(k, index):
                weights = (w_o, w_ple_gate)[index][0]
                sp.dma_start(raw_block(k, index), weights[k * P:(k + 1) * P, :]).then_inc(wb_full[k], 16)

            for k in range(KD - 1):
                sp.wait_ge(mx_ready, k + 1)
                load_big(k, 0)
            wait_big_lo(sp, 0, 0)
            load_big(KD - 1, 0)

            def load_x(lt):
                if lt >= 2:
                    sp.wait_ge(x1_ready, lt - 1)
                sp.dma_start(x_in[lt % 2][:], x[0, lt * P:(lt + 1) * P, :]).then_inc(x_in_full[lt % 2], 16)

            sp.wait_ge(tile_done, 4 * Q_END)
            sp.dma_start(post_row[:], post_norm[0].partition_broadcast(P)).then_inc(post_loaded, 16)
            wait_big_lo(sp, 5, 0)
            load_x(0)
            wait_big_lo(sp, 6, 0)
            load_x(1)
            for k in range(KD):
                wait_big_lo(sp, k, 0)
            sp.dma_start(p_nat[:], p[0, 0].rearrange("(t q) k -> q t k", q=P)).then_inc(ple_in, 16)
            sp.dma_start(wp_raw[:], w_ple[0].rearrange("(k q) d -> q k d", q=P)).then_inc(ple_in, 16)
            for lt in range(LT):
                if lt == LT - 1:
                    wait_big_lo(sp, 0, 1)
                    load_big(4, 1)
                    sp.wait_ge(x1_ready, LT - 1)
                    load_big(5, 1)
                    for k in (1, 2):
                        wait_big_lo(sp, k, 1)
                        load_big(5 + k, 1)
                sp.wait_ge(x1_ready, lt + 1)
                sp.dma_start(x1_dram[lt * P:(lt + 1) * P, :], x1[lt % 2][:]).then_inc(x1_stored[lt % 2], 16)
                if lt + 2 < LT:
                    load_x(lt + 2)
                if lt == P_AT + KP - 1:
                    sp.wait_ge(pt_ready, 2 * KP)
                    sp.wait_ge(wp_ready, 1)
                    for k in range(4):
                        load_big(k, 1)

            def load_x1(lt):
                sp.wait_ge(x1_stored[lt % 2], 16 * (lt // 2 + 1))
                if lt >= 2:
                    sp.wait_ge(out_ready, 2 * lt - 2)
                sp.dma_start(x_in[lt % 2][:], x1_dram[lt * P:(lt + 1) * P, :]).then_inc(x_in_full[lt % 2], 16)

            sp.wait_ge(x1_ready, LT)
            wait_big_lo(sp, 5, 1)
            load_x1(0)
            load_x1(1)
            wait_big_lo(sp, 4, 1)
            sp.dma_start(ple_row[:], ple_norm[0].partition_broadcast(P)).then_inc(ple_loaded, 16)
            for lt in range(LT):
                for half in range(2):
                    cols = slice(half * HALF, (half + 1) * HALF)
                    sp.wait_ge(out_ready, 2 * lt + half + 1)
                    sp.dma_start(out[0, lt * P:(lt + 1) * P, cols], x1[lt % 2][:, cols]).then_inc(out_stored[lt % 2], 16)
                if lt + 2 < LT:
                    load_x1(lt + 2)
            for i in range(2):
                sp.wait_ge(out_stored[i], 32 * (LT // 2))

        @block.gpsimd
        def _(pool):
            nc.gpsimd.memset(ident[:], 0.0).then_inc(ident_ready, 1)
            pool.wait_ge(ident_ready, 1)
            nc.gpsimd.affine_select(out=ident[:], in_=ident[:], compare_op=ALU.not_equal, fill=1.0, base=0,
                                    pattern=[[-1, P]], channel_multiplier=1).then_inc(ident_ready, 1)

            def lo(n, c, kk):
                pool.wait_ge(w_hi_ready, n + 1)
                nc.gpsimd.tensor_tensor(w_lo[c % 2][:, 0:kk, :], w_raw[c][:, 0:kk, :],
                                        w_hi[c % 2][:, 0:kk, :].bitcast(f32), ALU.subtract).then_inc(w_ready, 1)

            def quad(q, kks=(KD, KD, KD, KD)):
                for c in range(4):
                    lo(4 * q + c, c, kks[c])

            lo(0, 0, KD)
            lo(1, 1, KD)
            for c in (2, 3):
                lo(c, c, KD)
            lo(4 * Q_CONV0, 0, KD)

            steps = [0]

            def step(ins):
                steps[0] += 1
                ins.then_inc(ca_step, 1)
                pool.wait_ge(ca_step, steps[0])

            def ca_part(prs, ri):
                pw = [w[:, prs, :].unsqueeze(3).to_broadcast([P, 4, NP, GC]) for w in (pw_r, pw_i)]
                co = [c_t[:, r, prs, :].unsqueeze(2).to_broadcast([P, 4, NP, GC]) for r in range(2)]
                neg = slice(prs.start - PAIRS // 2, prs.stop - PAIRS // 2)
                co_r = co[0] if ri == 0 else c_neg[:, neg, :].unsqueeze(2).to_broadcast([P, 4, NP, GC])
                nc.gpsimd.tensor_tensor(t3[:], pw[0], co_r, ALU.mult)
                step(nc.gpsimd.tensor_tensor(t4[:], pw[1], co[1 - ri], ALU.mult))
                for par in range(2):
                    rows = slice(par * N_STATE, (par + 1) * N_STATE)
                    dst = ca[ri * N_STATE:(ri + 1) * N_STATE].rearrange(
                        "s (a b) n h -> s a b n h", b=2)[:, prs, par, :, :]
                    last = nc.gpsimd.tensor_tensor(dst, t3[rows], t4[rows], ALU.subtract)
                step(last)

            pairs_1, pairs_2 = slice(PAIRS // 2, PAIRS // 2 + 4), slice(PAIRS // 2 + 4, PAIRS)
            pool.wait_ge(powers_ready, 1)
            ca_part(pairs_1, 0)
            lo(4 * Q_CONV0 + 1, 1, KD)
            ca_part(pairs_1, 1)
            ca_part(pairs_2, 0)
            lo(4 * Q_CONV0 + 2, 2, KD)
            ca_part(pairs_2, 1)
            pool.sem_inc(ca_ready, 1)
            lo(4 * Q_CONV0 + 3, 3, KD)
            with pool.Fori(Q_CONV1, Q_GLU) as q:
                quad(q)
            quad(Q_GLU, (KS,) * 4)
            quad(Q_CONV4)
            with pool.Fori(Q_YA, Q_CONV5) as q:
                quad(q, (KD, KS, KD, KS))
            with pool.Fori(Q_CONV5, Q_END) as q:
                quad(q)

            def big_lo_part(k, index):
                pool.wait_ge(wb_hi_ready, hi_part(k, index, 0))
                b_hi, b_lo = big_block(k, index)
                nc.gpsimd.tensor_tensor(b_lo, raw_block(k, index), b_hi.bitcast(f32),
                                        ALU.subtract).then_inc(wb_ready_p, 1)

            for k in BIG_LO_P:
                big_lo_part(k, 0)
            pool.wait_ge(wp_hi_ready, 1)
            nc.gpsimd.tensor_tensor(wp_lo[:], wp_raw[:], wp_hi[:].bitcast(f32), ALU.subtract).then_inc(wp_ready, 1)
            for k in BIG_LO_P:
                big_lo_part(k, 1)

        @block.scalar
        def _(act):
            def evac_start(use):
                act.wait_ge(aux_full, use + 1)

            def hi(n, c, kk, first=False):
                act.wait_ge(raw_full[c], 4 * n + (16 - 4 * c))
                if not first:
                    act.wait_ge(tile_done, n - 1)
                nc.scalar.activation(w_hi[c % 2][:, 0:kk, :], w_raw[c][:, 0:kk, :], ACT.Copy).then_inc(w_hi_ready, 1)

            with nc.allow_non_contiguous_dma(reason="gain per partition"):
                act.dma_start(gain_pre[:], pre_norm[0].rearrange("(k p) -> p k", p=P)).then_inc(gain_loaded, 16)

            def x_squares(i):
                act.wait_ge(x_loaded[i], 16)
                if i:
                    act.wait_ge(squares_done, i)
                nc.scalar.activation(sq_junk[:], x_tile[i][:], ACT.Square,
                                     accum_out=ssq[:, i:i + 1]).then_inc(squares_done, 1)

            def h_hi(half, k):
                use = A_H + half * KD + k
                evac_start(use)
                nc.scalar.activation(big_hi[:, k, half * HALF:(half + 1) * HALF], aux[:, use % 4, :], ACT.Copy,
                                     scale=gain_pre[:, k:k + 1]).then_inc(h_hi_ready, 1)

            for i in range(6):
                x_squares(i)

            def normalise(i):
                nc.scalar.activation(x_tile[i][:], x_tile[i][:], ACT.Copy,
                                     scale=rstd[:, i:i + 1]).then_inc(xn_ready_a, 1)

            act.wait_ge(rstd_ready, 1)
            normalise(3)
            hi(0, 0, KD, first=True)
            act.wait_ge(gain_loaded, 16)
            for k in range(4):
                h_hi(0, k)
            x_squares(6)
            x_squares(7)
            for k in range(4, KD):
                h_hi(0, k)
            hi(1, 1, KD, first=True)
            act.wait_ge(rstd_ready, 2)
            normalise(6)
            normalise(7)
            for k in range(KD):
                h_hi(1, k)

            for c in range(KS):
                hi(c + 2, (c + 2) % 4, KD)
                act.wait_ge(tile_done, c + 1)
                nc.scalar.activation(u_f[:, c], flat(slot_ps(c % 2)).rearrange("p (c j) -> p j c", j=T),
                                     ACT.Copy).then_inc(u_f_ready, 1)
                act.wait_ge(u_f_ready, c + 1)
                act.sem_inc(slot_free[c % 2], 1)

            def to_s1(func, n, c, w, first=False, **kw):
                act.wait_ge(tile_done, n + 1)
                if not first:
                    act.wait_ge(s1_used, w)
                nc.scalar.activation(s1[:], flat(slot_ps(c % 2)), func, **kw).then_inc(s1_full, 1)

            def conv_quad(q, w, first=False, split_1=True, next_kk=KD):
                n = 4 * q
                if split_1:
                    hi(n + 1, 1, KD)
                act.wait_ge(tile_done, n + 1)
                if not first:
                    act.wait_ge(s1_used, w)
                nc.scalar.activation(s1[:], flat(slot_ps(0)), ACT.Copy).then_inc(s1_full, 1)
                act.wait_ge(s1_full, w + 1)
                act.sem_inc(slot_free[0], 1)
                hi(n + 2, 2, KD)
                hi(n + 3, 3, KD)
                act.wait_ge(tile_done, n + 3)
                act.wait_ge(s1_used, w + 1)
                nc.scalar.activation(s1[:], flat(slot_ps(0)), ACT.Silu).then_inc(s1_full, 1)
                act.wait_ge(s1_full, w + 2)
                act.sem_inc(slot_free[0], 1)
                hi(n + 4, 0, next_kk)

            conv_quad(Q_CONV0, 0, first=True, split_1=False)

            def copy_bank(use, dst, src):
                evac_start(use)
                nc.scalar.activation(dst, src, ACT.Copy).then_inc(aux_free[use % 4], 1)

            for b in range(0, G // 4, 2):
                copy_bank(A_W + b, flat(w_in_state[:, 4 * b:4 * b + 4, :]), aux[:, (A_W + b) % 4, :])
            for b in range(0, G // 4, 2):
                copy_bank(A_K + b, flat(kern[:, 4 * b:4 * b + 4, :]), aux[0:GC, (A_K + b) % 4, :])
            for b in range(0, G // 4, 2):
                use = A_WC + b
                evac_start(use)
                nc.scalar.activation(flat(w_c[0:N_STATE, b // 2, 0]), aux[0:N_STATE, use % 4, :], ACT.Copy)
                nc.scalar.activation(flat(w_c[0:N_STATE, b // 2, 1]), aux[N_STATE:P, use % 4, :],
                                     ACT.Copy).then_inc(aux_free[use % 4], 1)

            with act.Fori(Q_CONV1, Q_GSSM) as q:
                conv_quad(q, 2 * q + (2 - 2 * Q_CONV1))

            act.wait_ge(state_ready, 4)
            for b in range(G // 4):
                use = A_Y + b
                evac_start(use)
                nc.scalar.activation(
                    y_nat[:, :, 4 * b * GC:4 * (b + 1) * GC].rearrange("c j (g h) -> c g j h", h=GC),
                    aux[:, use % 4, :].rearrange("c (g j h) -> c g j h", g=4, h=GC),
                    ACT.Copy).then_inc(aux_free[use % 4], 1)
            for ct in range(KS):
                for jb in range(2):
                    use = A_YT + 2 * ct + jb
                    evac_start(use)
                    ins = nc.scalar.activation(
                        y_f[:, ct, :].rearrange("p (c j) -> p j c", j=T)[:, 4 * jb:4 * jb + 4, :],
                        aux[:, use % 4, :].rearrange("p (j c) -> p j c", c=C), ACT.Gelu_apprx_tanh)
                    ins.then_inc(gelu_ready, 1)
                    act.wait_ge(gelu_ready, 2 * ct + jb + 1)
                    act.sem_inc(aux_free[use % 4], 1)
            for ct in range(KS):
                nc.scalar.activation(y_hi[:, ct, :], y_f[:, ct, :], ACT.Copy).then_inc(y_hi_ready, 1)

            for c in range(4):
                n = 4 * Q_GSSM + c
                hi(n + 1, (c + 1) % 4, KD if c < 3 else KS)
                act.wait_ge(tile_done, n + 1)
                nc.scalar.activation(y_g[:, c, :], flat(slot_ps(c % 2)), ACT.Silu).then_inc(gssm_ready, 1)
                act.wait_ge(gssm_ready, c + 1)
                act.sem_inc(slot_free[c % 2], 1)
            act.wait_ge(consts_loaded, 32)
            for c in range(4):
                n = 4 * Q_GLU + c
                hi(n + 1, (c + 1) % 4, KS if c < 3 else KD)
                to_s1(ACT.Sigmoid, n, c, 8 + c, bias=bg[:, c:c + 1])
                act.wait_ge(s1_full, 9 + c)
                act.sem_inc(slot_free[c % 2], 1)
            for ct in range(KS):
                act.wait_ge(y2_ready, ct + 1)
                nc.scalar.activation(y_hi[:, ct, :], y_g[:, ct, :], ACT.Copy).then_inc(y_hi_ready, 1)
                if ct == 1:
                    hi(4 * Q_CONV4 + 1, 1, KD)

            conv_quad(Q_CONV4, 12, split_1=False)

            def ya_pair(q, c, last=False):
                n = 4 * q + c
                w = 2 * q + (14 + c // 2 - 2 * Q_YA)
                hi(n + 2, (c + 2) % 4, KD)
                to_s1(ACT.Sigmoid, n, c, w)
                act.wait_ge(s1_full, w + 1)
                act.sem_inc(slot_free[0], 1)
                if not last:
                    hi(n + 3, (c + 3) % 4, KS)

            hi(4 * Q_YA + 1, 1, KS)
            with act.Fori(Q_YA, Q_CONV5 - 1) as q:
                ya_pair(q, 0)
                ya_pair(q, 2)
            ya_pair(Q_CONV5 - 1, 0)
            ya_pair(Q_CONV5 - 1, 2, last=True)
            with act.Fori(Q_CONV5, Q_RC) as q:
                conv_quad(q, 2 * q + (22 - 2 * Q_CONV5))

            def rc_tile(q, c):
                act.wait_ge(tile_done, 4 * q + c + 1)
                nc.scalar.activation(rc_gate[:, bass.ds(4 * q + (c - 4 * Q_RC), 1), :].rearrange("p a l -> p (a l)"),
                                     flat(slot_ps(c % 2)), ACT.Sigmoid).then_inc(rc_ready, 1)
                act.wait_ge(rc_ready, 4 * q + (c + 1 - 4 * Q_RC))
                act.sem_inc(slot_free[c % 2], 1)

            with act.Fori(Q_RC, Q_YB - 1) as q:
                for c in range(4):
                    hi(4 * q + c + 1, (c + 1) % 4, KD)
                    rc_tile(q, c)
            act.wait_ge(z_done, KD)
            nc.scalar.activation(z0_hi[:], z[:, 0, :], ACT.Copy).then_inc(z_hi_ready, 1)
            for c in range(4):
                hi(4 * (Q_YB - 1) + c + 1, (c + 1) % 4, KD)
                if c < 3:
                    rc_tile(Q_YB - 1, c)

            act.wait_ge(tile_done, 4 * Q_YB)
            for k in range(1, KD):
                for cols in halves_of(k):
                    nc.scalar.activation(big_hi[:, k, cols], z[:, k, cols], ACT.Copy).then_inc(z_hi_ready, 1)
                if k == 4:
                    hi(4 * Q_YB + 1, 1, KD)

            rc_tile(Q_YB - 1, 3)

            def merge_hi(q, c, d):
                act.wait_ge(sum_ready, d + 1)
                nc.scalar.activation(mx_hi[:, bass.ds(d, 1), :].rearrange("p a l -> p (a l)"),
                                     yam[:, bass.ds(d, 1), :].rearrange("p a l -> p (a l)"),
                                     ACT.Copy).then_inc(mx_hi_ready, 1)

            act.wait_ge(z_ready, z_part(KD - 1, 0))
            with act.Fori(Q_YB, Q_END - 1) as q:
                for c in range(4):
                    hi(4 * q + c + 2, (c + 2) % 4, KD)
                    merge_hi(q, c, 4 * q + (c - 4 * Q_YB))
            for c in range(3):
                if c < 2:
                    hi(4 * (Q_END - 1) + c + 2, c + 2, KD)
                merge_hi(Q_END - 1, c, 4 + c)

            def big_part(k, index):
                act.wait_ge(wb_full[k], 16 * (index + 1))
                for cols in halves_of(k):
                    nc.scalar.activation(big_block(k, index)[0][:, cols], raw_block(k, index)[:, cols],
                                         ACT.Copy).then_inc(wb_hi_ready, 1)

            big_part(0, 0)
            act.wait_ge(w_ready, 4 * Q_END - 2)
            big_part(1, 0)
            act.wait_ge(tile_done, 4 * Q_END)
            for k in range(2, KD):
                big_part(k, 0)
                if k == 6:
                    merge_hi(Q_END - 1, 3, 7)

            def x1_hi(lt):
                for half in range(2):
                    use = pair_use("x1", lt) + half
                    evac_start(use)
                    nc.scalar.activation(mx_hi[:, 4 * half:4 * half + 4, lt * P:(lt + 1) * P],
                                         aux[:, use % 4, :].rearrange("p (k l) -> p k l", l=P),
                                         ACT.Copy).then_inc(x1_hi_ready, 1)

            def pt_hi_part(part):
                for half in range(2):
                    use = pair_use("p", part) + half
                    evac_start(use)
                    nc.scalar.activation(pt_hi[part][:, half * HALF:(half + 1) * HALF], aux[:, use % 4, :],
                                         ACT.Copy).then_inc(pt_hi_ready, 1)

            for lt in range(LT):
                if lt >= P_AT and lt - P_AT < KP:
                    pt_hi_part(lt - P_AT)
                if lt == LT - 2:
                    big_part(0, 1)
                act.wait_ge(tile_done, 4 * Q_END + lt + 1)
                if lt >= 2:
                    act.wait_ge(x1_stored[lt % 2], 16 * (lt // 2))
                    act.wait_ge(aux_full, pair_use("x1", lt - 2) + 2)
                if lt == LT - 1:
                    for k in range(1, 5):
                        big_part(k, 1)
                nc.scalar.activation(x1[lt % 2][:], flat(slot_ps(lt % 2)), ACT.Square,
                                     accum_out=ssq[:, LT + lt:LT + lt + 1]).then_inc(squares_done, 1)
                if lt == LT - 1:
                    for k in range(5, KD):
                        big_part(k, 1)
                if lt >= 1:
                    x1_hi(lt - 1)
                if lt == P_AT - 1:
                    act.wait_ge(ple_in, 32)
                    nc.scalar.activation(wp_hi[:], wp_raw[:], ACT.Copy).then_inc(wp_hi_ready, 1)

            for lt in range(LT):
                last = lt == LT - 1
                act.wait_ge(tile_done, 4 * Q_END + LT + lt + 1)
                if lt >= 1:
                    act.wait_ge(esq_done, lt)
                else:
                    act.wait_ge(x1_ready, LT)
                if not last:
                    nc.scalar.activation(sig_row[:], flat(slot_ps(lt % 2)), ACT.Sigmoid).then_inc(sig_ready, 1)
                    act.wait_ge(sig_ready, lt + 1)
                    act.sem_inc(slot_free[lt % 2], 1)
                else:
                    for half in range(2):
                        act.wait_ge(tile_done, 4 * Q_END + LT + lt + half + 1)
                        nc.scalar.activation(sig_row[:, half * HALF:(half + 1) * HALF], slot_ps(lt % 2)[:, half, :],
                                             ACT.Sigmoid).then_inc(sig_ready, 1)
                if lt == 0:
                    x1_hi(LT - 1)
                for half in range(2 if last else 1):
                    cols = slice(half * HALF, (half + 1) * HALF) if last else slice(0, D)
                    j = 2 * LT + lt + half
                    act.wait_ge(e_ready, lt + half + 1)
                    nc.scalar.activation(sig_row[:, cols], x1[lt % 2][:, cols], ACT.Square,
                                         accum_out=ssq[:, j:j + 1]).then_inc(esq_done, 1)

        @block.vector
        def _(dve):
            V = nc.vector
            count = [0]

            def link(ins):
                count[0] += 1
                ins.then_inc(dve_chain, 1)
                dve.wait_ge(dve_chain, count[0])

            def tt(o, a, b, op):
                link(V.tensor_tensor(o, a, b, op))

            def ts(o, a, s0, op0, s1_=None, op1=None):
                if op1 is None:
                    link(V.tensor_scalar(o, a, s0, None, op0))
                else:
                    link(V.tensor_scalar(o, a, s0, s1_, op0, op1))

            def stt(o, a, s, b, op0, op1):
                link(V.scalar_tensor_tensor(out=o, in0=a, scalar=s, in1=b, op0=op0, op1=op1))

            def inverse_rms(j0, j1):
                s = slice(j0, j1)
                ts(va[:, s], ssq[:, s], 1.0 / D, ALU.mult, EPS, ALU.add)
                newton(j0, j1)

            def newton(j0, j1):
                s = slice(j0, j1)
                link(V.tensor_single_scalar(vb[:, s].bitcast(i32), va[:, s].bitcast(i32), 1,
                                            ALU.arith_shift_right))
                ts(rstd[:, s].bitcast(i32), vb[:, s].bitcast(i32), -1.0, ALU.mult, 1597463007.0, ALU.add)
                ts(va[:, s], va[:, s], -0.5, ALU.mult)
                for _ in range(3):
                    if j1 - j0 == 1:
                        stt(vb[:, s], rstd[:, s], rstd[:, s], va[:, s], ALU.mult, ALU.mult)
                    else:
                        tt(vb[:, s], rstd[:, s], rstd[:, s], ALU.mult)
                        tt(vb[:, s], vb[:, s], va[:, s], ALU.mult)
                    stt(rstd[:, s], vb[:, s], 1.5, rstd[:, s], ALU.add, ALU.mult)

            def normalise(i):
                V.tensor_scalar(x_tile[i][:], x_tile[i][:], rstd[:, i:i + 1], None, ALU.mult).then_inc(xn_ready, 1)

            def h_lo(half, k):
                use = A_H + half * KD + k
                dve.wait_ge(h_hi_ready, half * KD + k + 1)
                cols = slice(half * HALF, (half + 1) * HALF)
                V.scalar_tensor_tensor(out=big_lo[:, k, cols], in0=aux[:, use % 4, :],
                                       scalar=gain_pre[:, k:k + 1], in1=big_hi[:, k, cols].bitcast(f32),
                                       op0=ALU.mult, op1=ALU.subtract).then_inc(aux_free[use % 4], 1)

            dve.wait_ge(squares_done, 4)
            inverse_rms(0, 4)
            dve.sem_inc(rstd_ready, 1)
            for i in range(3):
                normalise(i)
            dve.wait_ge(gain_loaded, 16)
            for k in range(KD):
                h_lo(0, k)
            dve.wait_ge(squares_done, LT)
            inverse_rms(4, LT)
            dve.sem_inc(rstd_ready, 1)
            normalise(4)
            normalise(5)

            for k in range(KD):
                h_lo(1, k)
            for ri in range(2):
                dve.wait_ge(aux_full, A_C + ri + 1)
                for par in range(2):
                    rows = slice(par * N_STATE, (par + 1) * N_STATE)
                    last = V.tensor_copy(c_t[rows, ri], aux[rows, (A_C + ri) % 4, :].rearrange(
                        "s (a b h) -> s a b h", b=2, h=GC)[:, :, par, :])
                last.then_inc(aux_free[(A_C + ri) % 4], 1)

            names = {}

            def t(name):
                if name not in names:
                    names[name] = len(names)
                return small[:, names[name], :]

            for n in ("are", "aim", "ls"):
                t(n)

            def exp_to(o, a):
                LN2_HI, LN2_LO = 0.693359375, -2.12194440e-4
                ROUND = 12582912.0
                ts(t("ea"), a, -170.0, ALU.max, 170.0, ALU.min)
                ts(t("en"), t("ea"), 1.0 / math.log(2.0), ALU.mult, ROUND, ALU.add)
                ts(t("en"), t("en"), ROUND, ALU.subtract)
                stt(t("er"), t("en"), -LN2_HI, t("ea"), ALU.mult, ALU.add)
                stt(t("er"), t("en"), -LN2_LO, t("er"), ALU.mult, ALU.add)
                ts(t("ep"), t("er"), 1.0 / math.factorial(7), ALU.mult)
                for i in range(6, 0, -1):
                    stt(t("ep"), t("ep"), 1.0 / math.factorial(i), t("er"), ALU.add, ALU.mult)
                ts(t("ep"), t("ep"), 1.0, ALU.add)
                ts(t("e1"), t("en"), -126.0, ALU.max, 127.0, ALU.min)
                tt(t("e2"), t("en"), t("e1"), ALU.subtract)
                ts(t("e2"), t("e2"), -126.0, ALU.max, 127.0, ALU.min)
                for e in ("e1", "e2"):
                    ts(t(e + "i").bitcast(i32), t(e), 127.0, ALU.add, 8388608.0, ALU.mult)
                    tt(t("ep"), t("ep"), t(e + "i"), ALU.mult)
                link(V.tensor_copy(o, t("ep")))

            def cmul(o_r, o_i, a_r, a_i, b_r_, b_i_, u, v):
                tt(u, a_r, b_r_, ALU.mult)
                tt(v, a_i, b_i_, ALU.mult)
                tt(o_r, u, v, ALU.subtract)
                tt(u, a_r, b_i_, ALU.mult)
                tt(v, a_i, b_r_, ALU.mult)
                tt(o_i, u, v, ALU.add)

            def discretise():
                dve.wait_ge(params_loaded, 16 * 15)
                exp_to(t("dt"), t("ls"))
                tt(t("arg"), t("are"), t("dt"), ALU.mult)
                exp_to(t("mag"), t("arg"))
                tt(t("th"), t("aim"), t("dt"), ALU.mult)
                ts(t("en"), t("th"), 1.0 / (2 * math.pi), ALU.mult, 12582912.0, ALU.add)
                ts(t("en"), t("en"), 12582912.0, ALU.subtract)
                C1 = 6.28125
                C2 = float(round((2 * math.pi - C1) * 2 ** 22)) / 2 ** 22
                C3 = 2 * math.pi - C1 - C2
                for cst in (C1, C2, C3):
                    stt(t("th"), t("en"), -cst, t("th"), ALU.mult, ALU.add)
                ts(t("q"), t("th"), 0.25, ALU.mult, 0.8, ALU.min)
                ts(t("q"), t("q"), -0.8, ALU.max)
                tt(t("qq"), t("q"), t("q"), ALU.mult)
                ts(t("s"), t("qq"), 1.0 / math.factorial(9), ALU.mult)
                for i in (7, 5, 3):
                    sign = 1.0 if i == 5 else -1.0
                    stt(t("s"), t("s"), sign / math.factorial(i), t("qq"), ALU.add, ALU.mult)
                stt(t("s"), t("s"), 1.0, t("q"), ALU.add, ALU.mult)
                ts(t("c"), t("qq"), -1.0 / math.factorial(10), ALU.mult)
                for i in (8, 6, 4, 2):
                    sign = 1.0 if i % 4 == 0 else -1.0
                    stt(t("c"), t("c"), sign / math.factorial(i), t("qq"), ALU.add, ALU.mult)
                ts(t("c"), t("c"), 1.0, ALU.add)
                for _ in range(2):
                    stt(t("c2"), t("s"), -2.0, t("s"), ALU.mult, ALU.mult)
                    stt(t("s"), t("s"), 2.0, t("c"), ALU.mult, ALU.mult)
                    ts(t("c"), t("c2"), 1.0, ALU.add)
                tt(t("ar"), t("mag"), t("c"), ALU.mult)
                tt(t("ai"), t("mag"), t("s"), ALU.mult)
                ts(t("nr"), t("ar"), 1.0, ALU.subtract)
                tt(t("u"), t("are"), t("are"), ALU.mult)
                tt(t("v"), t("aim"), t("aim"), ALU.mult)
                tt(t("u"), t("u"), t("v"), ALU.add)
                link(V.reciprocal(t("rd"), t("u")))
                tt(t("u"), t("nr"), t("are"), ALU.mult)
                tt(t("v"), t("ai"), t("aim"), ALU.mult)
                tt(t("u"), t("u"), t("v"), ALU.add)
                tt(t("fr"), t("u"), t("rd"), ALU.mult)
                tt(t("u"), t("ai"), t("are"), ALU.mult)
                tt(t("v"), t("nr"), t("aim"), ALU.mult)
                tt(t("u"), t("u"), t("v"), ALU.subtract)
                tt(t("fi"), t("u"), t("rd"), ALU.mult)

            def chunk_turn():
                tt(t("u"), t("mag"), t("mag"), ALU.mult)
                tt(t("u"), t("u"), t("u"), ALU.mult)
                tt(mag8[:], t("u"), t("u"), ALU.mult)
                cmul(t("x2"), t("y2"), t("c"), t("s"), t("c"), t("s"), t("u"), t("v"))
                cmul(t("x4"), t("y4"), t("x2"), t("y2"), t("x2"), t("y2"), t("u"), t("v"))
                cmul(turn1_r[:], turn1_i[:], t("x4"), t("y4"), t("x4"), t("y4"), t("u"), t("v"))

            def powers():
                V.memset(pw_r[:, :, 0:1], 1.0)
                V.memset(pw_i[:, :, 0:1], 0.0)
                V.tensor_copy(pw_r[:, :, 1:2], t("ar").unsqueeze(2))
                link(V.tensor_copy(pw_i[:, :, 1:2], t("ai").unsqueeze(2)))
                m = 1
                while m < T:
                    uu = t1[:].rearrange("p a b -> p (a b)")[:, 0:PAIRS * m].rearrange("p (a b) -> p a b", b=m)
                    vv = t2[:].rearrange("p a b -> p (a b)")[:, 0:PAIRS * m].rearrange("p (a b) -> p a b", b=m)
                    lo_, hi_ = slice(1, m + 1), slice(m + 1, 2 * m + 1)
                    by = [w[:, :, m:m + 1].to_broadcast([P, PAIRS, m]) for w in (pw_r, pw_i)]
                    cmul(pw_r[:, :, hi_], pw_i[:, :, hi_], pw_r[:, :, lo_], pw_i[:, :, lo_], by[0], by[1], uu, vv)
                    m *= 2

            def per_row(ap):
                return ap.unsqueeze(2).to_broadcast([P, PAIRS, GC])

            def bbar():
                u = t1[:].rearrange("p a b -> p (a b)")[:, 0:PAIRS * GC].rearrange("p (a b) -> p a b", b=GC)
                v = t2[:].rearrange("p a b -> p (a b)")[:, 0:PAIRS * GC].rearrange("p (a b) -> p a b", b=GC)
                cmul(bb_r[:], bb_i[:], b_r[:], b_i[:], per_row(t("fr")), per_row(t("fi")), u, v)
                for ri, src in enumerate((bb_r, bb_i)):
                    for par in range(2):
                        link(V.tensor_copy(
                            bb_stack[ri * N_STATE:(ri + 1) * N_STATE, :, :]
                            .rearrange("s (a b) h -> s a b h", b=2)[:, :, par, :],
                            src[par * N_STATE:(par + 1) * N_STATE, :, :]))

            def table(dst, n_pow, coef_r, coef_i, half, im_sign):
                prs = slice(8 * half, 8 * half + 8)
                cols = n_pow * GC
                u = t1[:].rearrange("p a b -> p (a b)")[:, 0:8 * cols]
                v = t2[:].rearrange("p a b -> p (a b)")[:, 0:8 * cols]
                view = lambda w: w.rearrange("p (a n h) -> p a n h", a=8, h=GC)
                pw = [w[:, prs, 0:n_pow].unsqueeze(3).to_broadcast([P, 8, n_pow, GC]) for w in (pw_r, pw_i)]
                co = [w[:, prs, :].unsqueeze(2).to_broadcast([P, 8, n_pow, GC]) for w in (coef_r, coef_i)]
                for ri in range(2):
                    V.tensor_tensor(view(u), pw[0], co[ri], ALU.mult)
                    tt(view(v), pw[1], co[1 - ri], ALU.mult)
                    for par in range(2):
                        rows = slice(par * N_STATE, (par + 1) * N_STATE)
                        o = dst[ri * N_STATE:(ri + 1) * N_STATE].rearrange("s (a b) c -> s a b c", b=2)[:, prs, par, :]
                        uu = u[rows].rearrange("s (a c) -> s a c", a=8)
                        vv = v[rows].rearrange("s (a c) -> s a c", a=8)
                        if ri == 0:
                            last = V.tensor_tensor(o, uu, vv, ALU.subtract)
                        elif im_sign > 0:
                            last = V.tensor_tensor(o, uu, vv, ALU.add)
                        else:
                            last = V.scalar_tensor_tensor(out=o, in0=uu, scalar=-1.0, in1=vv, op0=ALU.mult,
                                                          op1=ALU.subtract)
                    link(last)

            ca_flat = ca[:].rearrange("p g n h -> p g (n h)")

            discretise()
            powers()
            link(V.tensor_scalar(c_neg[:], c_t[:, 1, PAIRS // 2:PAIRS, :], -1.0, None, ALU.mult))
            dve.sem_inc(powers_ready, 1)
            chunk_turn()
            bbar()
            table(ca_flat, NP, c_t[:, 0], c_t[:, 1], 0, -1)

            link(V.memset(v_pad[:, 0:2], 0.0))
            dve.wait_ge(consts_loaded, 32)

            def tap(n_tap, ct):
                return cw[:, n_tap, bass.ds(ct, 1)]

            def conv_cc(q, ct, w, chain):
                n = 4 * q
                dve.wait_ge(tile_done, n + 2)
                dve.wait_ge(s1_full, w + 1)
                V.tensor_tensor(v_pad[:, 2:L + 2], flat(slot_ps(1)), s1[:], ALU.mult).then_inc(s1_used, 1)
                dve.wait_ge(s1_used, w + 1)
                dve.sem_inc(slot_free[1], 1)
                V.tensor_scalar(cv[:], v_pad[:, 2:L + 2], tap(2, ct), None, ALU.mult).then_inc(conv_step, 1)
                dve.wait_ge(conv_step, chain + 1)
                V.scalar_tensor_tensor(out=cv[:], in0=v_pad[:, 1:L + 1], scalar=tap(1, ct), in1=cv[:],
                                       op0=ALU.mult, op1=ALU.add).then_inc(conv_step, 1)
                dve.wait_ge(conv_step, chain + 2)
                V.scalar_tensor_tensor(out=cv[:], in0=v_pad[:, 0:L], scalar=tap(0, ct), in1=cv[:],
                                       op0=ALU.mult, op1=ALU.add).then_inc(conv_step, 1)

            def conv_bc(q, ct, w, chain, dst=None):
                n = 4 * q
                dve.wait_ge(tile_done, n + 4)
                dve.wait_ge(conv_step, chain + 3)
                V.tensor_tensor(cv[:], flat(slot_ps(1)), cv[:], ALU.mult).then_inc(conv_step, 1)
                dve.wait_ge(conv_step, chain + 4)
                dve.sem_inc(slot_free[1], 1)
                dve.wait_ge(s1_full, w + 2)
                if dst is None:
                    dst = z[:, bass.ds(ct, 1), :].rearrange("p a l -> p (a l)")
                V.tensor_tensor(dst, cv[:], s1[:], ALU.mult).then_inc(z_done, 1)
                dve.wait_ge(z_done, ct + 1)
                dve.sem_inc(s1_used, 1)

            def pv_half(half):
                table(pv[:], T, bb_r[:], bb_i[:], half, 1)

            pv_half(0)
            conv_cc(Q_CONV0, 0, 0, 0)
            pv_half(1)
            dve.sem_inc(pv_ready, 1)

            for b in range(1, G // 4, 2):
                use = A_W + b
                dve.wait_ge(aux_full, use + 1)
                V.tensor_copy(flat(w_in_state[:, 4 * b:4 * b + 4, :]), aux[:, use % 4, :]).then_inc(aux_free[use % 4], 1)
            conv_bc(Q_CONV0, 0, 0, 0)
            for b in range(1, G // 4, 2):
                use = A_K + b
                dve.wait_ge(aux_full, use + 1)
                V.tensor_copy(flat(kern[:, 4 * b:4 * b + 4, :]), aux[0:GC, use % 4, :]).then_inc(aux_free[use % 4], 1)
            for i in range(4):
                uses = [u for u in range(A_K, A_K + G // 4) if u % 4 == i]
                dve.wait_ge(aux_free[i], uses[-1] // 4 + 1)
            diag = ident[0:GC, 0:GC].unsqueeze(1).to_broadcast([GC, G, GC])
            dk = d_diag[:]
            tt(dk, diag, d_hg[:].unsqueeze(2).to_broadcast([GC, G, GC]), ALU.mult)
            link(V.tensor_tensor(kern[:, :, 0:GC], kern[:, :, 0:GC], dk, ALU.add))
            dve.sem_inc(kern_ready, 1)
            for b in range(1, G // 4, 2):
                use = A_WC + b
                dve.wait_ge(aux_full, use + 1)
                V.tensor_copy(flat(w_c[N_STATE:P, b // 2, 0]), aux[0:N_STATE, use % 4, :])
                V.tensor_copy(flat(w_c[N_STATE:P, b // 2, 1]), aux[N_STATE:P, use % 4, :]).then_inc(aux_free[use % 4], 1)
            dve.wait_ge(aux_full, A_WC + G // 4)
            V.memset(toep[:], 0.0).then_inc(toep_zero, 1)
            for i in range(4):
                uses = [u for u in range(A_WC, A_WC + G // 4) if u % 4 == i]
                dve.wait_ge(aux_free[i], uses[-1] // 4 + 1)
            dve.wait_ge(toep_ready, 16 * T)

            local = [0]

            def turns_start(q, half):
                prs = bass.ds(8 * half, 8)
                V.memset(turn_r[:, :, 0:1], 1.0)
                V.memset(turn_i[:, :, 0:1], 0.0)
                V.tensor_copy(turn_r[:, :, 1:2], turn1_r[:, prs].unsqueeze(2))
                slink(q, V.tensor_copy(turn_i[:, :, 1:2], turn1_i[:, prs].unsqueeze(2)))

            def turns_to(q, m, end):
                while m < end:
                    uu = q1q2[:, 0:8 * m].rearrange("p (a b) -> p a b", b=m)
                    vv = q3q4[:, 0:8 * m].rearrange("p (a b) -> p a b", b=m)
                    lo_, hi_ = slice(1, m + 1), slice(m + 1, 2 * m + 1)
                    b0, b1 = (w[:, :, m:m + 1].to_broadcast([P, 8, m]) for w in (turn_r, turn_i))
                    V.tensor_tensor(uu, turn_r[:, :, lo_], b0, ALU.mult)
                    slink(q, V.tensor_tensor(vv, turn_i[:, :, lo_], b1, ALU.mult))
                    slink(q, V.tensor_tensor(turn_r[:, :, hi_], uu, vv, ALU.subtract))
                    V.tensor_tensor(uu, turn_r[:, :, lo_], b1, ALU.mult)
                    slink(q, V.tensor_tensor(vv, turn_i[:, :, lo_], b0, ALU.mult))
                    slink(q, V.tensor_tensor(turn_i[:, :, hi_], uu, vv, ALU.add))
                    m *= 2

            def slink(q, ins):
                local[0] += 1
                ins.then_inc(scan_step, 1)
                dve.wait_ge(scan_step, (q - Q_CONV1) * PER_TURN + local[0])

            PER_TURN = 1 + 7 * 4 + 2 * 7

            def scan_block(q, half, b):
                qd = 2 * half + b
                wr, wi = (w_c[:, bass.ds(qd, 1), r].rearrange("p q a c -> p (q a) c") for r in range(2))
                ps = slice(4 * b, 4 * b + 4)
                er, ei = turn_r[:, ps, 1:C + 1], turn_i[:, ps, 1:C + 1]
                V.tensor_tensor(q1[:], er, wr, ALU.mult)
                V.tensor_tensor(q2[:], ei, wi, ALU.mult)
                V.tensor_tensor(q3[:], er, wi, ALU.mult)
                slink(q, V.tensor_tensor(q4[:], ei, wr, ALU.mult))
                V.tensor_tensor(q1[:], q1[:], q2[:], ALU.add)
                slink(q, V.tensor_tensor(q3[:], q3[:], q4[:], ALU.subtract))
                for src, dst in ((q1, q2), (q3, q4)):
                    for a in range(4):
                        last = V.tensor_tensor_scan(dst[:, a, :],
                                                    mag8[:, bass.ds(4 * qd + a, 1)].to_broadcast([P, C]),
                                                    src[:, a, :], 0.0, ALU.mult, ALU.add)
                slink(q, last)
                er, ei = turn_r[:, ps, 1:C], turn_i[:, ps, 1:C]
                zr, zi = q2[:, :, 0:C - 1], q4[:, :, 0:C - 1]
                o1, o3 = q1[:, :, 0:C - 1], q3[:, :, 0:C - 1]
                for ri in range(2):
                    V.tensor_tensor(o1, er, zr if ri == 0 else zi, ALU.mult)
                    slink(q, V.tensor_tensor(o3, ei, zi if ri == 0 else zr, ALU.mult))
                    for par in range(2):
                        rows = slice(par * N_STATE, (par + 1) * N_STATE)
                        dst = state[ri * N_STATE:(ri + 1) * N_STATE, bass.ds(qd, 1), :, :].rearrange(
                            "s q (a b) c -> s (q a) b c", b=2)[:, :, par, :]
                        last = V.tensor_tensor(dst[:, :, 1:C], o1[rows], o3[rows],
                                               ALU.subtract if ri == 0 else ALU.add)
                        last = V.tensor_copy(dst[:, :, 0:1], v_pad[rows, 0:1].unsqueeze(1).to_broadcast([N_STATE, 4, 1]))
                    slink(q, last)
                dve.sem_inc(state_ready, 1)

            with dve.Fori(Q_CONV1, Q_CONV3) as q:
                half = q - Q_CONV1
                w, chain = 2 * q + (2 - 2 * Q_CONV1), 4 * q + (4 - 4 * Q_CONV1)
                turns_start(q, half)
                turns_to(q, 1, C // 2)
                conv_cc(q, q - Q_CONV0, w, chain)
                turns_to(q, C // 2, C)
                scan_block(q, half, 0)
                conv_bc(q, q - Q_CONV0, w, chain)
                scan_block(q, half, 1)
            assert local[0] == PER_TURN, local[0]

            conv_cc(Q_CONV3, 3, 6, 12)
            conv_bc(Q_CONV3, 3, 6, 12, dst=cv[:])
            dve.wait_ge(aux_full, A_Y + G // 4)
            link(V.tensor_copy(z[:, 3, :], cv[:]))

            def y_split(ct, src, n):
                dve.wait_ge(y_hi_ready, n)
                V.tensor_tensor(y_lo[:, ct, :], src[:, ct, :], y_hi[:, ct, :].bitcast(f32),
                                ALU.subtract).then_inc(y_ready, 1)

            for ct in range(KS):
                y_split(ct, y_f, ct + 1)
            for c in range(4):
                dve.wait_ge(s1_full, 9 + c)
                tt(s1[:], s1[:], y_f[:, c, :], ALU.mult)
                tt(y_g[:, c, :], s1[:], y_g[:, c, :], ALU.mult)
                dve.sem_inc(s1_used, 1)
            dve.wait_ge(tile_done, 4 * Q_GLU + 4)
            dve.sem_inc(y2_ready, KS)
            for ct in range(KS):
                y_split(ct, y_g, KS + ct + 1)

            conv_cc(Q_CONV4, 4, 12, 16)
            conv_bc(Q_CONV4, 4, 12, 16)

            with dve.Fori(Q_YA, Q_CONV5) as q:
                for c in (1, 3):
                    n = 4 * q + c
                    d = 2 * q + (c // 2 - 2 * Q_YA)
                    dve.wait_ge(s1_full, d + 15)
                    dve.wait_ge(tile_done, n + 1)
                    V.tensor_tensor(yam[:, bass.ds(d, 1), :].rearrange("p a l -> p (a l)"), flat(slot_ps(1)), s1[:],
                                    ALU.mult).then_inc(s1_used, 1)
                    dve.wait_ge(s1_used, d + 15)
                    dve.sem_inc(slot_free[1], 1)
            with dve.Fori(Q_CONV5, Q_RC) as q:
                ct = q - (Q_CONV5 - 5)
                conv_cc(q, ct, 2 * q + (22 - 2 * Q_CONV5), 4 * q + (20 - 4 * Q_CONV5))
                conv_bc(q, ct, 2 * q + (22 - 2 * Q_CONV5), 4 * q + (20 - 4 * Q_CONV5))

            for k in range(KD):
                z_hi, z_lo = (z0_hi[:], z0_lo[:]) if k == 0 else (big_hi[:, k, :], big_lo[:, k, :])
                for part, cols in enumerate(halves_of(k)):
                    dve.wait_ge(z_hi_ready, z_part(k, part))
                    V.tensor_tensor(z_lo[:, cols], z[:, k, cols], z_hi[:, cols].bitcast(f32),
                                    ALU.subtract).then_inc(z_ready, 1)

            def row(ap, d):
                return ap[:, bass.ds(d, 1), :].rearrange("p a l -> p (a l)")

            def merge_gate(q, c, d):
                dve.wait_ge(tile_done, 4 * q + c + 1)
                V.tensor_tensor(s1[:], flat(slot_ps(c % 2)), row(rc_gate, d), ALU.mult).then_inc(slot_free[c % 2], 1)
                dve.wait_ge(slot_free[c % 2], 2 * q + (c // 2 + 1))

            def merge_sum(d):
                V.tensor_tensor(row(yam, d), row(yam, d), s1[:], ALU.add).then_inc(sum_ready, 1)

            def merge_lo(d):
                dve.wait_ge(mx_hi_ready, d + 1)
                V.tensor_tensor(row(mx_lo, d), row(yam, d), row(mx_hi, d).bitcast(f32),
                                ALU.subtract).then_inc(mx_ready, 1)

            def merge(q, c):
                d = 4 * q + (c - 4 * Q_YB)
                merge_gate(q, c, d)
                merge_sum(d)
                merge_lo(d)
                dve.wait_ge(mx_ready, d + 1)

            def big_lo_part(k, index):
                b_hi, b_lo = big_block(k, index)
                for part, cols in enumerate(halves_of(k)):
                    dve.wait_ge(wb_hi_ready, hi_part(k, index, part))
                    V.tensor_tensor(b_lo[:, cols], raw_block(k, index)[:, cols], b_hi[:, cols].bitcast(f32),
                                    ALU.subtract).then_inc(wb_ready_v, 1)

            with dve.Fori(Q_YB, Q_END - 1) as q:
                for c in range(4):
                    merge(q, c)
            for c in range(3):
                merge(Q_END - 1, c)
            big_lo_part(0, 0)
            big_lo_part(1, 0)
            for k in BIG_LO_V[2:]:
                big_lo_part(k, 0)
                if k == 2:
                    merge_gate(Q_END - 1, 3, KD - 1)
                    merge_sum(KD - 1)
                if k == 5:
                    merge_lo(KD - 1)

            def x1_lo(lt):
                for half in range(2):
                    use = pair_use("x1", lt) + half
                    dve.wait_ge(x1_hi_ready, 2 * lt + half + 1)
                    ks = slice(4 * half, 4 * half + 4)
                    ls = slice(lt * P, (lt + 1) * P)
                    V.tensor_tensor(mx_lo[:, ks, ls], aux[:, use % 4, :].rearrange("p (k l) -> p k l", l=P),
                                    mx_hi[:, ks, ls].bitcast(f32), ALU.subtract).then_inc(x1_split, 1)
                    dve.wait_ge(x1_split, 2 * lt + half + 1)
                    dve.sem_inc(aux_free[use % 4], 1)

            def pt_lo_part(part):
                for half in range(2):
                    use = pair_use("p", part) + half
                    cols = slice(half * HALF, (half + 1) * HALF)
                    dve.wait_ge(pt_hi_ready, 2 * part + half + 1)
                    V.tensor_tensor(pt_lo[:, part, cols], aux[:, use % 4, :], pt_hi[part][:, cols].bitcast(f32),
                                    ALU.subtract).then_inc(pt_ready, 1)
                    dve.wait_ge(pt_ready, 2 * part + half + 1)
                    dve.sem_inc(aux_free[use % 4], 1)

            dve.wait_ge(post_loaded, 16)
            for lt in range(LT):
                j = LT + lt
                if lt >= P_AT and lt - P_AT < KP:
                    pt_lo_part(lt - P_AT)
                if lt == LT - 2:
                    big_lo_part(0, 1)
                if lt == LT - 1:
                    for k in (1, 2, 4):
                        big_lo_part(k, 1)
                dve.wait_ge(squares_done, LT + lt + 1)
                inverse_rms(j, j + 1)
                if lt == LT - 1:
                    big_lo_part(5, 1)
                stt(x1[lt % 2][:], flat(slot_ps(lt % 2)), rstd[:, j:j + 1], post_row[:], ALU.mult, ALU.mult)
                dve.sem_inc(slot_free[lt % 2], 1)
                dve.wait_ge(x_in_full[lt % 2], 16 * (lt // 2 + 1))
                V.tensor_tensor(x1[lt % 2][:], x1[lt % 2][:], x_in[lt % 2][:], ALU.add).then_inc(x1_ready, 1)
                if lt == LT - 1:
                    big_lo_part(7, 1)
                if lt >= 1:
                    x1_lo(lt - 1)

            for lt in range(LT):
                j = 2 * LT + lt
                b0 = pair_use("e", lt) % 4
                halves = 2 if lt == LT - 1 else 1
                if lt == 0:
                    x1_lo(LT - 1)
                dve.wait_ge(aux_full, pair_use("e", lt) + 2)
                if lt >= 2:
                    dve.wait_ge(out_stored[lt % 2], 32 * (lt // 2))
                else:
                    dve.wait_ge(x1_stored[lt % 2], 16 * (LT // 2))
                if lt == 0:
                    dve.wait_ge(ple_loaded, 16)
                for part in range(halves):
                    cols = slice(part * HALF, (part + 1) * HALF) if halves == 2 else slice(0, D)
                    dve.wait_ge(sig_ready, lt + part + 1)
                    V.tensor_tensor(x1[lt % 2][:, cols], flat(aux[:, b0:b0 + 2, :])[:, cols], sig_row[:, cols],
                                    ALU.mult).then_inc(e_ready, 1)
                    dve.wait_ge(e_ready, lt + part + 1)
                    link(V.tensor_tensor(e_gain[:, cols], x1[lt % 2][:, cols], ple_row[:, cols], ALU.mult))
                dve.sem_inc(aux_free[b0], 1)
                dve.sem_inc(aux_free[b0 + 1], 1)
                dve.wait_ge(esq_done, lt + 1)
                if halves == 2:
                    ts(va[:, j:j + 1], ssq[:, j:j + 1], 1.0 / D, ALU.mult, EPS, ALU.add)
                    dve.wait_ge(esq_done, lt + 2)
                    stt(va[:, j:j + 1], ssq[:, j + 1:j + 2], 1.0 / D, va[:, j:j + 1], ALU.mult, ALU.add)
                    newton(j, j + 1)
                else:
                    inverse_rms(j, j + 1)
                dve.wait_ge(x_in_full[lt % 2], 16 * ((LT + lt) // 2 + 1))
                for half in range(2):
                    cols = slice(half * HALF, (half + 1) * HALF)
                    V.scalar_tensor_tensor(out=x1[lt % 2][:, cols], in0=e_gain[:, cols], scalar=rstd[:, j:j + 1],
                                           in1=x_in[lt % 2][:, cols], op0=ALU.mult,
                                           op1=ALU.add).then_inc(out_ready, 1)
                dve.wait_ge(out_ready, 2 * lt + 2)

        @block.tensor
        def _(pe):
            M = nc.tensor

            def bank(use):
                if use >= 4:
                    pe.wait_ge(aux_free[use % 4], use // 4)
                return aux[:, use % 4, :]

            def three(o, s_hi, s_lo, m_hi, m_lo, first, last):
                M.matmul(o, s_hi, m_hi, start=first, stop=False)
                M.matmul(o, s_hi, m_lo, start=False, stop=False)
                return M.matmul(o, s_lo, m_hi, start=False, stop=last)

            def transposes_x(half, ks):
                for k in ks:
                    o = bank(A_H + half * KD + k)
                    for i in range(4):
                        last = M.transpose(o[:, i * P:(i + 1) * P],
                                           x_tile[4 * half + i][:, k * P:(k + 1) * P], ident[:])
                    last.then_inc(aux_full, 1)

            def tile_half(c, half, ks):
                cols = slice(half * HALF, (half + 1) * HALF)
                for k in ks:
                    if c == 0:
                        use = A_H + half * KD + k
                        pe.wait_ge(aux_free[use % 4], use // 4 + 1)
                    last = three(slot_ps(c)[:, half, :], w_hi[c][:, k, :], w_lo[c][:, k, :],
                                 big_hi[:, k, cols], big_lo[:, k, cols], k == 0, k == KD - 1)
                return last

            WARM_UP = 28
            FRONT, BACK = range(KD // 2), range(KD // 2, KD)
            pe.wait_ge(ident_ready, 2)
            pe.wait_ge(squares_done, 4)
            for i in range(WARM_UP):
                M.transpose(tile_ps[:, 3, 0:P], ident[:], ident[:])
            pe.wait_ge(xn_ready, 3)
            pe.wait_ge(xn_ready_a, 1)
            transposes_x(0, range(KD))
            pe.wait_ge(w_ready, 1)
            tile_half(0, 0, range(KD))
            pe.wait_ge(w_ready, 2)
            tile_half(1, 0, FRONT)
            pe.wait_ge(xn_ready, 5)
            pe.wait_ge(xn_ready_a, 3)
            transposes_x(1, FRONT)
            tile_half(1, 0, BACK)
            transposes_x(1, BACK)

            pe.wait_ge(params_loaded, 16 * 15)
            for ri in range(2):
                o = bank(A_C + ri)
                for f in range(4):
                    last = M.transpose(o[:, f * P:(f + 1) * P], c_nat[:, ri, f, :], ident[:])
                last.then_inc(aux_full, 1)

            def quad(q, moving=None, kks=(KD,) * 4, by_k=None, k0=None):
                for c in range(4):
                    m_hi, m_lo = (moving or {}).get(c, (big_hi, big_lo))
                    tile(q, c, kks[c], m_hi, m_lo, by_k, k0)

            def tile(q, c, kk, m_hi, m_lo, by_k=None, k0=None):
                pe.wait_ge(w_ready, 4 * q + c + 1)
                pe.wait_ge(slot_free[c % 2], 2 * q + c // 2)
                for k in range(kk):
                    for half in range(2):
                        if by_k is not None and c == 0 and half < len(halves_of(k)):
                            pe.wait_ge(by_k, z_part(k, half))
                        cols = slice(half * HALF, (half + 1) * HALF)
                        mov = (k0[0][:, cols], k0[1][:, cols]) if k0 and k == 0 else (m_hi[:, k, cols], m_lo[:, k, cols])
                        last = three(slot_ps(c % 2)[:, half, :], w_hi[c % 2][:, k, :], w_lo[c % 2][:, k, :],
                                     mov[0], mov[1], k == 0, k == kk - 1)
                last.then_inc(tile_done, 1)

            for c in range(2):
                tile_half(c, 1, range(KD)).then_inc(tile_done, 1)
            for c in range(2, KS):
                tile(Q_U, c, KD, big_hi, big_lo)
            quad(Q_CONV0)

            pe.wait_ge(pv_ready, 1)
            pe.wait_ge(ca_ready, 1)
            for b in range(G // 4):
                o = bank(A_W + b)
                for i in range(4):
                    last = M.transpose(o[:, i * P:(i + 1) * P], pv[:, 4 * b + i, :], ident[:])
                last.then_inc(aux_full, 1)
            for b in range(G // 4):
                o = bank(A_K + b)
                for i in range(4):
                    g = 4 * b + i
                    last = M.matmul(o[0:GC, i * P:(i + 1) * P], bb_stack[:, g, :],
                                    ca[:, g, 0:T, :].rearrange("p n h -> p (n h)"), start=True, stop=True)
                last.then_inc(aux_full, 1)
            for i in range(4):
                uses = [u for u in range(A_W, A_K) if u % 4 == i]
                pe.wait_ge(aux_free[i], uses[-1] // 4 + 1)
            pe.wait_ge(u_chunk_ready, 16 * T)
            for b in range(G // 4):
                o = bank(A_WC + b)
                for i in range(4):
                    g = 2 * (4 * (b // 2) + i) + b % 2
                    last = M.matmul(o[:, i * P:(i + 1) * P], w_in_state[:, g, :], u_chunk[:, g, :],
                                    start=True, stop=True)
                last.then_inc(aux_full, 1)

            with pe.Fori(Q_CONV1, Q_GSSM) as q:
                quad(q)

            pe.wait_ge(toep_ready, 16 * T)
            for b in range(G // 4):
                pe.wait_ge(state_ready, b // 2 + 1)
                o = bank(A_Y + b)
                for i in range(4):
                    g = 4 * b + i
                    s = slice(i * P, (i + 1) * P)
                    M.matmul(o[:, s], u_chunk[:, g, :], toep[:, g, :], start=True, stop=False)
                    last = M.matmul(o[:, s], state[:, g // 8, g % 8, :],
                                    ca[:, g, 1:NP, :].rearrange("p n h -> p (n h)"), start=False, stop=True)
                last.then_inc(aux_full, 1)
            for ct in range(KS):
                for jb in range(2):
                    o = bank(A_YT + 2 * ct + jb)
                    for i in range(4):
                        last = M.transpose(o[:, i * P:(i + 1) * P], y_nat[:, 4 * jb + i, ct * P:(ct + 1) * P],
                                           ident[:])
                    last.then_inc(aux_full, 1)

            quad(Q_GSSM)
            pe.wait_ge(y_ready, KS)
            y_mov = {c: (y_hi, y_lo) for c in range(4)}
            quad(Q_GLU, y_mov, (KS,) * 4)
            quad(Q_CONV4)
            pe.wait_ge(y_ready, 2 * KS)
            with pe.Fori(Q_YA, Q_CONV5) as q:
                quad(q, {1: (y_hi, y_lo), 3: (y_hi, y_lo)}, (KD, KS, KD, KS))
            with pe.Fori(Q_CONV5, Q_YB) as q:
                quad(q)
            with pe.Fori(Q_YB, Q_END) as q:
                quad(q, by_k=z_ready, k0=(z0_hi, z0_lo))

            def transposes_x1(lt):
                pe.wait_ge(x1_ready, lt + 1)
                for half in range(2):
                    o = bank(pair_use("x1", lt) + half)
                    for i in range(4):
                        k = 4 * half + i
                        last = M.transpose(o[:, i * P:(i + 1) * P], x1[lt % 2][:, k * P:(k + 1) * P], ident[:])
                    last.then_inc(aux_full, 1)

            def row_tile(lt, base, index):
                pe.wait_ge(slot_free[lt % 2], (4 * Q_END + base + lt) // 2)
                ls = slice(lt * P, (lt + 1) * P)

                def block(k, half):
                    b_hi, b_lo = big_block(k, index)
                    cols = slice(half * HALF, (half + 1) * HALF)
                    return three(slot_ps(lt % 2)[:, half, :], mx_hi[:, k, ls], mx_lo[:, k, ls],
                                 b_hi[:, cols], b_lo[:, cols], k == 0, k == KD - 1)

                if base + lt == 2 * LT - 1:
                    for half in range(2):
                        for k in range(KD):
                            last = block(k, half)
                        last.then_inc(tile_done, 1)
                    return
                for k in range(KD):
                    if lt == 0 and index == 0:
                        pe.wait_ge(mx_ready, k + 1)
                    for half in range(2):
                        if lt == 0 and half < len(halves_of(k)):
                            wait_big_lo(pe, k, index, half)
                        last = block(k, half)
                last.then_inc(tile_done, 1)

            for lt in range(LT):
                if lt >= P_AT and lt - P_AT < KP:
                    k = lt - P_AT
                    pe.wait_ge(ple_in, 32)
                    for half in range(2):
                        o = bank(pair_use("p", k) + half)
                        for i in range(4):
                            last = M.transpose(o[:, i * P:(i + 1) * P],
                                               p_nat[:, 4 * half + i, k * P:(k + 1) * P], ident[:])
                        last.then_inc(aux_full, 1)
                row_tile(lt, 0, 0)
                if lt >= 1:
                    transposes_x1(lt - 1)

            def e_tile(lt):
                ls = slice(lt * P, (lt + 1) * P)
                for half in range(2):
                    o = bank(pair_use("e", lt) + half)
                    cols = slice(half * HALF, (half + 1) * HALF)
                    for k in range(KP):
                        last = three(o, pt_hi[k][:, ls], pt_lo[:, k, ls], wp_hi[:, k, cols], wp_lo[:, k, cols],
                                     k == 0, k == KP - 1)
                    last.then_inc(aux_full, 1)

            pe.wait_ge(pt_ready, 2 * KP)
            pe.wait_ge(wp_ready, 1)
            e_tile(0)
            for lt in range(LT):
                if lt == 1:
                    transposes_x1(LT - 1)
                if lt == LT - 1:
                    e_tile(lt)
                pe.wait_ge(x1_split, 2 * lt + 2)
                row_tile(lt, LT, 1)
                if 1 <= lt < LT - 1:
                    e_tile(lt)


def kernel(**inputs):
    import numpy as np
    import concourse.bacc as bacc
    from concourse import mybir
    from concourse.bass_utils import run_bass_kernel_spmd as run

    nc = bacc.Bacc("TRN2", target_bir_lowering=False, num_devices=1)
    names = ["x", "p", "pre_norm", "w_in", "a_re", "a_im", "log_step", "b_re", "b_im", "c_re", "c_im", "d_skip",
             "w_glu", "b_glu", "w_ssm_out", "conv_w", "w_conv_out", "w_o", "post_norm", "w_ple", "w_ple_gate",
             "ple_norm"]
    arrays, args = {}, []
    for name in names:
        a = np.ascontiguousarray(inputs[name])
        arrays[f"in_{name}"] = a
        args.append(nc.dram_tensor(f"in_{name}", a.shape, mybir.dt.from_np(a.dtype), kind="ExternalInput").ap())
    shape = inputs["x"].shape
    args.append(nc.dram_tensor("out_x", shape, mybir.dt.float32, kind="ExternalOutput").ap())
    build_block(nc, *args)
    return run(nc, [arrays], core_ids=[0]).results[0]["out_x"]
```
